# Optimizing a Trainium2 kernel written in Bass

```python
import jax, jax.numpy as jnp
from jax import lax
import numpy as np

D_MODEL = 2048
BATCH = 1
SEQ = 512
DEPTH = 1
DEC_BATCH = 1
DEC_SEQ = 32
PAST_LEN = 512

CHUNK = 64
Q_BLOCK = 128
SB_HEAD_DIM = 128
SB_WIDTH = D_MODEL // 2
SB_HEADS = SB_WIDTH // SB_HEAD_DIM
RW_HEAD_DIM = 64
RW_WIDTH = D_MODEL // 2
RW_HEADS = RW_WIDTH // RW_HEAD_DIM
RW_DECAY_RANK = 64
RW_A_RANK = 64
RW_GATE_RANK = 128
RW_PROJ = 3 * RW_WIDTH + RW_DECAY_RANK + RW_A_RANK + RW_GATE_RANK
RW_SPLITS = [RW_WIDTH, 2 * RW_WIDTH, 3 * RW_WIDTH, 3 * RW_WIDTH + RW_DECAY_RANK,
             3 * RW_WIDTH + RW_DECAY_RANK + RW_A_RANK]
N_BRANCH = 2
IN_PROJ = 3 * SB_WIDTH + RW_PROJ + N_BRANCH * D_MODEL
IN_SPLITS = [SB_WIDTH, 2 * SB_WIDTH, 3 * SB_WIDTH, 3 * SB_WIDTH + RW_PROJ,
             3 * SB_WIDTH + RW_PROJ + D_MODEL]
PEER_HEADS = 8
PEER_NKEYS = 128
PEER_EXPERTS = PEER_NKEYS * PEER_NKEYS
PEER_QDIM = 256
PEER_HALF = PEER_QDIM // 2
PEER_TOPK = 16
PEER_TOKEN_BLOCK = 128
RMS_EPS = 1e-6
GN_EPS = 64e-5

kernel_name = 'hybrid_stickbreak_rwkv7_peer_stream_step'

def rms_norm(x, g):
    xf = x.astype(jnp.float32)
    y = xf * lax.rsqrt(jnp.mean(xf * xf, axis=-1, keepdims=True) + RMS_EPS)
    return (y * g.astype(jnp.float32)).astype(x.dtype)

def sb_block(q, k, v, q_pos, k_pos):
    z = jnp.einsum('bqhd,bkhd->bhqk', q, k, preferred_element_type=jnp.float32) * (SB_HEAD_DIM ** -0.5)
    mask = (k_pos[None, :] < q_pos[:, None])[None, None]
    log_keep = jnp.where(mask, jax.nn.log_sigmoid(-z), 0.0)
    log_after = lax.cumsum(log_keep, axis=3, reverse=True) - log_keep
    w = jnp.where(mask, jnp.exp(jax.nn.log_sigmoid(z) + log_after), 0.0)
    return jnp.einsum('bhqk,bkhd->bqhd', w.astype(v.dtype), v)

def sb_attention_prompt(q, k, v):
    B, S, H, dh = q.shape
    nb = S // Q_BLOCK
    pos = jnp.arange(S)
    qb = jnp.moveaxis(q.reshape(B, nb, Q_BLOCK, H, dh), 1, 0)
    posb = pos.reshape(nb, Q_BLOCK)
    out = lax.map(lambda a: sb_block(a[0], k, v, a[1], pos), (qb, posb))
    return jnp.moveaxis(out, 0, 1).reshape(B, S, H, dh)

def rwkv_step(S, inp):
    r_t, w_t, k_t, v_t, kk_t, a_t = inp
    sa = jnp.einsum('bhvk,bhk->bhv', S, kk_t)
    S = (S * w_t[:, :, None, :] - sa[..., None] * (kk_t * a_t)[:, :, None, :]
         + v_t[..., None] * k_t[:, :, None, :])
    y = jnp.einsum('bhvk,bhk->bhv', S, r_t)
    return S, y

def rwkv7_branch(p, shift0, wkv0, mu, w0, w2, a0, a2, g2, k_k, k_a, r_k, ln_g, ln_b):
    B, T, _ = p.shape
    prev = jnp.concatenate([shift0.astype(p.dtype), p[:, :-1]], axis=1)
    ps = p + (prev - p) * mu
    r, k, v, xw, xa, xg = jnp.split(ps, RW_SPLITS, axis=-1)
    f32 = jnp.float32
    w = -jax.nn.softplus(-(w0 + jnp.tanh(xw) @ w2).astype(f32)) - 0.5
    decay = jnp.exp(-jnp.exp(w))
    a = jax.nn.sigmoid((a0 + xa @ a2).astype(f32))
    g = jax.nn.sigmoid(xg) @ g2
    k = k.astype(f32)
    hd = lambda t: t.reshape(B, T, RW_HEADS, RW_HEAD_DIM)
    kk = hd(k * k_k.astype(f32))
    kk = kk / jnp.maximum(jnp.sqrt(jnp.sum(kk * kk, axis=-1, keepdims=True)), 1e-12)
    k = hd(k * (1.0 + (a - 1.0) * k_a.astype(f32)))
    r_h, v_h, a_h, w_h = hd(r.astype(f32)), hd(v.astype(f32)), hd(a), hd(decay)
    tm = lambda t: jnp.moveaxis(t, 1, 0)
    S_final, y = lax.scan(rwkv_step, wkv0.astype(f32), (tm(r_h), tm(w_h), tm(k), tm(v_h), tm(kk), tm(a_h)))
    y = jnp.moveaxis(y, 0, 1)
    mean = jnp.mean(y, axis=-1, keepdims=True)
    var = jnp.mean(jnp.square(y - mean), axis=-1, keepdims=True)
    y = ((y - mean) * lax.rsqrt(var + GN_EPS)).reshape(B, T, RW_WIDTH) * ln_g + ln_b
    bonus = jnp.sum(r_h * k * r_k.astype(f32), axis=-1, keepdims=True) * v_h
    out = ((y + bonus.reshape(B, T, RW_WIDTH)) * g).astype(p.dtype)
    return out, S_final, p[:, -1:]

def peer_ffn(xn, w_q, sub_k1, sub_k2, u_tab, v_tab):
    B, T, D = xn.shape
    xf = xn.reshape(-1, D)
    n = xf.shape[0]
    q = (xf @ w_q).reshape(n, PEER_HEADS, 2, PEER_HALF)
    s1 = jnp.einsum('nhd,kd->nhk', q[:, :, 0], sub_k1, preferred_element_type=jnp.float32)
    s2 = jnp.einsum('nhd,kd->nhk', q[:, :, 1], sub_k2, preferred_element_type=jnp.float32)
    t1, i1 = lax.top_k(s1, PEER_TOPK)
    t2, i2 = lax.top_k(s2, PEER_TOPK)
    cand = (t1[..., :, None] + t2[..., None, :]).reshape(n, PEER_HEADS, PEER_TOPK * PEER_TOPK)
    cidx = (i1[..., :, None] * PEER_NKEYS + i2[..., None, :]).reshape(n, PEER_HEADS, PEER_TOPK * PEER_TOPK)
    best, sel = lax.top_k(cand, PEER_TOPK)
    idx = jnp.take_along_axis(cidx, sel, axis=-1).reshape(n, PEER_HEADS * PEER_TOPK)
    gate = jax.nn.softmax(best, axis=-1).reshape(n, PEER_HEADS * PEER_TOPK).astype(xn.dtype)
    nb = -(-n // PEER_TOKEN_BLOCK)
    pad = nb * PEER_TOKEN_BLOCK - n
    blk = lambda t: jnp.pad(t, ((0, pad), (0, 0))).reshape(nb, PEER_TOKEN_BLOCK, t.shape[-1])

    def one_block(args):
        xb, ib, gb = args
        u = jnp.take(u_tab, ib, axis=0)
        h = jax.nn.gelu(jnp.einsum('nkd,nd->nk', u, xb), approximate=False)
        vv = jnp.take(v_tab, ib, axis=0)
        return jnp.einsum('nk,nkd->nd', gb * h, vv)

    out = lax.map(one_block, (blk(xf), blk(idx), blk(gate)))
    return out.reshape(nb * PEER_TOKEN_BLOCK, D)[:n].reshape(B, T, D)

def layer_forward(x, past_k, past_v, wkv0, shift0, norm1_g, w_in, rw_mu, rw_w0, rw_w2, rw_a0, rw_a2,
                  rw_g2, rw_k_k, rw_k_a, rw_r_k, rw_ln_g, rw_ln_b, w_branch_sb, w_branch_rw, w_out,
                  norm2_g, peer_wq, peer_k1, peer_k2, peer_u, peer_v):
    B, T, _ = x.shape
    xn = rms_norm(x, norm1_g)
    proj = xn @ w_in
    q, k, v, p_rw, gate_sb, gate_rw = jnp.split(proj, IN_SPLITS, axis=-1)
    hs = lambda t: t.reshape(B, T, SB_HEADS, SB_HEAD_DIM)
    q, k, v = hs(q), hs(k), hs(v)
    if past_k is None:
        o_sb = sb_attention_prompt(q, k, v)
        wkv0 = jnp.zeros((B, RW_HEADS, RW_HEAD_DIM, RW_HEAD_DIM), jnp.float32)
        shift0 = jnp.zeros((B, 1, RW_PROJ), x.dtype)
    else:
        P = past_k.shape[1]
        k_all = jnp.concatenate([past_k.astype(k.dtype), k], axis=1)
        v_all = jnp.concatenate([past_v.astype(v.dtype), v], axis=1)
        o_sb = sb_block(q, k_all, v_all, P + jnp.arange(T), jnp.arange(P + T))
    o_rw, wkv_new, shift_new = rwkv7_branch(p_rw, shift0, wkv0, rw_mu, rw_w0, rw_w2, rw_a0, rw_a2, rw_g2,
                                            rw_k_k, rw_k_a, rw_r_k, rw_ln_g, rw_ln_b)
    mixed = (jax.nn.sigmoid(gate_sb) * (o_sb.reshape(B, T, SB_WIDTH) @ w_branch_sb)
             + jax.nn.sigmoid(gate_rw) * (o_rw @ w_branch_rw))
    h = x + mixed @ w_out
    h = h + peer_ffn(rms_norm(h, norm2_g), peer_wq, peer_k1, peer_k2, peer_u, peer_v)
    return h, k, v, wkv_new.astype(x.dtype), shift_new

def setup_inputs(seed: int = 0) -> dict:
    key = jax.random.key(seed)
    ks = jax.random.split(key, 32)
    f32 = jnp.float32
    nrm = lambda k, shape, s: jax.random.normal(k, shape, f32) * s
    L = DEPTH
    return {
        'x_prompt': nrm(ks[0], (BATCH, SEQ, D_MODEL), 1.0),
        'x_sample': nrm(ks[1], (DEC_BATCH, DEC_SEQ, D_MODEL), 1.0),
        'cache_sb_k': nrm(ks[2], (L, DEC_BATCH, PAST_LEN, SB_HEADS, SB_HEAD_DIM), 1.0),
        'cache_sb_v': nrm(ks[3], (L, DEC_BATCH, PAST_LEN, SB_HEADS, SB_HEAD_DIM), 1.0),
        'state_rwkv_wkv': nrm(ks[4], (L, DEC_BATCH, RW_HEADS, RW_HEAD_DIM, RW_HEAD_DIM), 0.5),
        'state_rwkv_shift': nrm(ks[5], (L, DEC_BATCH, 1, RW_PROJ), 1.0),
        'norm1_g': 1.0 + nrm(ks[6], (L, D_MODEL), 0.02),
        'w_in': nrm(ks[7], (L, D_MODEL, IN_PROJ), D_MODEL ** -0.5),
        'rw_mu': jax.random.uniform(ks[8], (L, RW_PROJ), f32, 0.2, 0.8),
        'rw_w0': jax.random.uniform(ks[9], (L, RW_WIDTH), f32, -6.5, -1.5),
        'rw_w2': nrm(ks[10], (L, RW_DECAY_RANK, RW_WIDTH), 0.5 * RW_DECAY_RANK ** -0.5),
        'rw_a0': nrm(ks[11], (L, RW_WIDTH), 0.1),
        'rw_a2': nrm(ks[12], (L, RW_A_RANK, RW_WIDTH), RW_A_RANK ** -0.5),
        'rw_g2': nrm(ks[13], (L, RW_GATE_RANK, RW_WIDTH), RW_GATE_RANK ** -0.5),
        'rw_k_k': 0.85 + nrm(ks[14], (L, RW_WIDTH), 0.02),
        'rw_k_a': 1.0 + nrm(ks[15], (L, RW_WIDTH), 0.02),
        'rw_r_k': nrm(ks[16], (L, RW_HEADS, RW_HEAD_DIM), 0.1),
        'rw_ln_g': 1.0 + nrm(ks[17], (L, RW_WIDTH), 0.02),
        'rw_ln_b': nrm(ks[18], (L, RW_WIDTH), 0.02),
        'w_branch_sb': nrm(ks[19], (L, SB_WIDTH, D_MODEL), SB_WIDTH ** -0.5),
        'w_branch_rw': nrm(ks[20], (L, RW_WIDTH, D_MODEL), RW_WIDTH ** -0.5),
        'w_out': nrm(ks[21], (L, D_MODEL, D_MODEL), D_MODEL ** -0.5),
        'norm2_g': 1.0 + nrm(ks[22], (L, D_MODEL), 0.02),
        'peer_wq': nrm(ks[23], (L, D_MODEL, PEER_HEADS * PEER_QDIM), D_MODEL ** -0.5),
        'peer_k1': nrm(ks[24], (L, PEER_NKEYS, PEER_HALF), PEER_HALF ** -0.5),
        'peer_k2': nrm(ks[25], (L, PEER_NKEYS, PEER_HALF), PEER_HALF ** -0.5),
        'peer_u': nrm(ks[26], (L, PEER_EXPERTS, D_MODEL), D_MODEL ** -0.5),
        'peer_v': nrm(ks[27], (L, PEER_EXPERTS, D_MODEL), 0.5),
        'final_norm_g': 1.0 + nrm(ks[28], (D_MODEL,), 0.02),
    }

def reference(x_prompt, x_sample, cache_sb_k, cache_sb_v, state_rwkv_wkv, state_rwkv_shift,
              norm1_g, w_in, rw_mu, rw_w0, rw_w2, rw_a0, rw_a2, rw_g2, rw_k_k, rw_k_a, rw_r_k,
              rw_ln_g, rw_ln_b, w_branch_sb, w_branch_rw, w_out, norm2_g, peer_wq, peer_k1, peer_k2,
              peer_u, peer_v, final_norm_g):
    hp, hs_ = x_prompt, x_sample
    kp, vp, wp, sp, ks_, vs_, ws_, ss_ = [], [], [], [], [], [], [], []
    for l in range(DEPTH):
        w = (norm1_g[l], w_in[l], rw_mu[l], rw_w0[l], rw_w2[l], rw_a0[l], rw_a2[l], rw_g2[l], rw_k_k[l],
             rw_k_a[l], rw_r_k[l], rw_ln_g[l], rw_ln_b[l], w_branch_sb[l], w_branch_rw[l], w_out[l],
             norm2_g[l], peer_wq[l], peer_k1[l], peer_k2[l], peer_u[l], peer_v[l])
        hp, k1, v1, wk1, sh1 = layer_forward(hp, None, None, None, None, *w)
        hs_, k2, v2, wk2, sh2 = layer_forward(hs_, cache_sb_k[l], cache_sb_v[l], state_rwkv_wkv[l],
                                              state_rwkv_shift[l], *w)
        kp.append(k1); vp.append(v1); wp.append(wk1); sp.append(sh1)
        ks_.append(k2); vs_.append(v2); ws_.append(wk2); ss_.append(sh2)
    y_prompt = rms_norm(hp, final_norm_g)
    y_sample = rms_norm(hs_, final_norm_g)
    return (y_prompt, y_sample, jnp.stack(kp), jnp.stack(vp), jnp.stack(wp), jnp.stack(sp),
            jnp.stack(ks_), jnp.stack(vs_), jnp.stack(ws_), jnp.stack(ss_))


_drawn_inputs = setup_inputs


def setup_inputs(seed=0):
    import zlib

    import numpy as np

    out = dict(_drawn_inputs(seed))
    spreads = {}
    factors = {'rw_ln_g': 3.102, 'rw_ln_b': 3.148, 'final_norm_g': 2.731}
    for name, (base, spread) in spreads.items():
        noise = np.random.default_rng([zlib.crc32(name.encode()), seed]).standard_normal(out[name].shape)
        drawn = base * np.exp(spread * noise) if base else spread * noise
        out[name] = __import__('jax').numpy.asarray(drawn.astype(out[name].dtype))
    for name, factor in factors.items():
        out[name] = (out[name] * factor).astype(out[name].dtype)
    return out
```

```python
from contextlib import ExitStack

import numpy as np
import concourse.bass as bass
from concourse import mybir

F32 = mybir.dt.float32
F32R = mybir.dt.float32r
U32 = mybir.dt.uint32
I32 = mybir.dt.int32
ACT = mybir.ActivationFunctionType
ALU = mybir.AluOpType
AX_X = mybir.AxisListType.X

P = 128
D = 2048
KB = D // P
SEQ, DEC, PAST = 512, 32, 512
T = SEQ + DEC
H2 = T // 2
HEADS = 8
RW = 1024
PAIRS = RW // P
CH = 64
CHUNKS = SEQ // CH
E = T + 2
EH = E // 2
S0 = SEQ + 1
SM_SCALE = P ** -0.5
KAPPA = float(np.exp(-0.5))
RMS_EPS, GN_EPS = 1e-6, 64e-5
PH, NK, TOPK = 8, 128, 16
NEXP = NK * NK

PAR = ["mu_r", "mu_k", "mu_v", "w0", "a0", "k_k", "k_a", "r_k", "ln_g", "ln_b"]
NPAR = len(PAR)
C_MUWA, C_MUG = PAIRS * NPAR, PAIRS * NPAR + 1
C_N1, C_N2, C_NF = C_MUG + 1, C_MUG + 1 + KB, C_MUG + 1 + 2 * KB
C_SHIFT = C_NF + KB
NCOL = C_SHIFT + 26

ZCOL = {3: 0, 1: 128, 2: 512, 0: 928}
ZS = 768
ZN = 1440

LEVELS = [2, 4, 8, 16, 32]


def constants():
    r, c = np.arange(P)[:, None], np.arange(P)[None, :]
    same = r // CH == c // CH
    out = {
        "ident": r == c,
        "ones": np.ones((P, P)),
        "headones": same,
        "negtri": -1.0 * (r >= c),
        "negones": -np.ones((P, P)),
        "before": r < c,
        "strict_T": same & (r < c),
        "incl_T": same & (r <= c),
        "strict": same & (c < r),
        "pair": (r // 2 == c // 2) & (r % 2 == 1) & (c % 2 == 0),
        "pair_T": (r // 2 == c // 2) & (c % 2 == 1) & (r % 2 == 0),
    }
    for m in LEVELS:
        out[f"level_T{m}"] = (r // (2 * m) == c // (2 * m)) & (c // m % 2 == 1) & (r // m % 2 == 0)
    out["npair"], out["npair_T"] = -1.0 * out.pop("pair"), -1.0 * out.pop("pair_T")
    out["iota"] = np.broadcast_to(c, (P, P))
    scan = np.ones((P, E))
    scan[:, [*range(0, SEQ, CH), SEQ, S0, E - 1]] = 0.0
    out["scan"] = scan
    return {k: np.asarray(v, np.float32) for k, v in out.items()}


CST_AT = {}
_n = 0
for _k, _v in constants().items():
    CST_AT[_k] = (_n, _v.shape[1])
    _n += _v.shape[1]
NCST = _n


class Sems:

    def __init__(self, nc, ctx):
        self.nc, self.ctx, self.known = nc, ctx, {}

    def __getitem__(self, name):
        if name not in self.known:
            self.known[name] = self.ctx.enter_context(self.nc.semaphore(name))
        return self.known[name]


class Chain:

    def __init__(self, eng, sem, steps, i, credit=0):
        self.credit = credit
        self.eng, self.sem, self.steps, self.i, self.k = eng, sem, steps, i, 0

    def __call__(self, instruction, wait=True):
        self.k += 1
        assert self.k <= self.steps, "more steps than counted"
        instruction.then_inc(self.sem, 1)
        if wait:
            self.eng.wait_ge(self.sem, self.i * self.steps + self.k + self.credit)

    def end(self):
        assert self.k == self.steps, (self.k, self.steps)


class Stream:

    def __init__(self, name, S, raw, hi, lo):
        self.raw, self.hi, self.lo = raw, hi, lo
        self.loaded = [S[f"{name}_loaded0"], S[f"{name}_loaded1"]]
        self.hi_done, self.split_done, self.used = S[f"{name}_hi"], S[f"{name}_split"], S[f"{name}_used"]

    def start_pool(self, pool):
        pool.sem_inc(self.split_done, 2)

    def start_pe(self, pe):
        pe.sem_inc(self.used, 2)

    def load(self, sp, src, c, per=0, i=0):
        sp.wait_ge(self.split_done, per * i + c + 1)
        sp.dma_start(self.raw[:, c % 2, :], src).then_inc(self.loaded[c % 2], 16)

    def split_hi(self, act, c, per=0, i=0):
        act.wait_ge(self.loaded[c % 2], per * 8 * i + 16 * (c // 2 + 1))
        act.wait_ge(self.used, per * i + c + 1)
        act.activation(self.hi[:, c % 2, :], self.raw[:, c % 2, :], ACT.Copy).then_inc(self.hi_done, 1)

    def split_lo(self, pool, c, per=0, i=0):
        pool.wait_ge(self.hi_done, per * i + c + 1)
        pool.tensor_tensor(self.lo[:, c % 2, :], self.raw[:, c % 2, :], self.hi[:, c % 2, :].bitcast(F32),
                           ALU.subtract).then_inc(self.split_done, 1)

    def ready(self, pe, c, per=0, i=0):
        pe.wait_ge(self.split_done, per * i + c + 3)


def product(pe, out, w_hi, w_lo, x_hi, x_lo, blocks, first=True, last=True):
    for k in range(blocks):
        for w, x in ((w_hi, x_hi), (w_hi, x_lo), (w_lo, x_hi)):
            for half in range(2):
                a = first and k == 0 and w is w_hi and x is x_hi
                z = last and k == blocks - 1 and w is w_lo
                mm = pe.matmul(out[:, half, 0:H2], w(k), x(k, half), start=a, stop=z)
        yield mm


def build(nc, A, O):
    ctx = ExitStack()
    with ctx:
        S = Sems(nc, ctx)
        dram = lambda n, s: nc.dram_tensor(n, s, F32, kind="Internal").ap()
        gates_d = dram("gates_d", (2 * KB, P, T))
        o_d = dram("o_d", (KB, P, T))
        h_d = dram("h_d", (KB, P, T))
        g_d = dram("g_d", (GB_N, P, NK, GB_T))

        acc = [ctx.enter_context(nc.psum_tensor(f"acc{b}", [P, 2, 512], F32)) for b in range(2)]
        psS = ctx.enter_context(nc.psum_tensor("psS", [P, 2, 512], F32))
        psR = ctx.enter_context(nc.psum_tensor("psR", [P, 2, 512], F32))
        sball = lambda n, s, d=F32: ctx.enter_context(nc.sbuf_tensor(n, s, d))
        par = sball("par", [P, NCOL])
        eps = sball("eps", [P, 2])

        with ExitStack() as front:
            sbf = lambda n, s, d=F32: front.enter_context(nc.sbuf_tensor(n, s, d))
            xh = sbf("xh", [P, KB, T], F32R)
            xl = sbf("xl", [P, KB, T], F32R)
            with ExitStack() as ctx1:
                X = ctx1.enter_context(nc.sbuf_tensor("X", [P, KB, T], F32))
                norm(nc, S, "n1", A, par, eps, psS, X, C_N1, src=lambda a, b: A["xT"][:, a:b, :], hi=xh, lo=xl)
            raw = sbf("raw", [P, 2, D])
            whi = sbf("whi", [P, 2, D], F32R)
            wlo = sbf("wlo", [P, 2, D], F32R)
            attention(nc, S, A, O, acc, psS, psR, xh, xl, raw, whi, wlo, gates_d, o_d)
            rwkv(nc, S, A, O, acc, psS, psR, xh, xl, raw, whi, wlo, par, eps, gates_d, o_d)

        with ExitStack() as middle:
            mh = middle.enter_context(nc.sbuf_tensor("mh", [P, KB, T], F32R))
            ml = middle.enter_context(nc.sbuf_tensor("ml", [P, KB, T], F32R))
            mix(nc, S, A, acc, psS, psR, mh, ml, gates_d, o_d)
            out_projection(nc, S, A, acc, mh, ml, h_d)

        with ExitStack() as back:
            sbk = lambda n, s, d=F32: back.enter_context(nc.sbuf_tensor(n, s, d))
            H, hh, hl = sbk("H", [P, KB, T]), sbk("hh", [P, KB, T], F32R), sbk("hl", [P, KB, T], F32R)
            norm(nc, S, "n2", A, par, eps, psS, H, C_N2, src=lambda a, b: h_d[a:b].rearrange("k p t -> p k t"), hi=hh, lo=hl)
            with ExitStack() as picks:
                IT = picks.enter_context(nc.sbuf_tensor("IT", [P, 3, T], F32))
                retrieval(nc, S, A, acc, psS, psR, hh, hl, IT)
                banks = [t[:, b, :] for t in (*acc, psS, psR) for b in range(2)]
                gate_matrix(nc, S, A, banks, IT, g_d)
            experts(nc, S, A, acc, psS, psR, H, hh, hl, g_d)
            norm(nc, S, "nf", A, par, eps, psS, H, C_NF, out=O["yT"])


def norm(nc, S, tag, A, par, eps, ps, X, gain, src=None, hi=None, lo=None, out=None):
    with ExitStack() as ctx:
        sb = lambda n, s, d=F32: ctx.enter_context(nc.sbuf_tensor(tag + n, s, d))
        SQ, RS, XT, ones = sb("SQ", [P, 2, T]), sb("RS", [P, T]), sb("XT", [P, 2, T]), sb("ones", [P, P])
        sem = lambda n: S[tag + n]
        block = ctx.enter_context(nc.Block())

        @block.sync
        def _(sp):
            if src is not None:
                for q in range(4):
                    sp.dma_start(X[:, 4 * q:4 * q + 4, :], src(4 * q, 4 * q + 4)).then_inc(sem(f"loaded{q}"), 16)
            if tag == "n1":
                sp.dma_start(par[:, :], A["par"]).then_inc(sem("par"), 16)
            if out is not None:
                for k in range(KB):
                    sp.wait_ge(sem("scaled"), k + 2)
                    sp.dma_start(out[:, k, :], XT[:, k % 2, :]).then_inc(sem(f"stored{k % 2}"), 16)
                for b in range(2):
                    sp.wait_ge(sem(f"stored{b}"), 16 * KB // 2)

        @block.scalar
        def _(act):
            for k in range(KB):
                if src is not None and k % 4 == 0:
                    act.wait_ge(sem(f"loaded{k // 4}"), 16)
                if k >= 2:
                    act.wait_ge(sem("summed"), k - 1)
                act.activation(SQ[:, k % 2, :], X[:, k, :], ACT.Square).then_inc(sem("square"), 1)
            act.wait_ge(sem("summed"), KB)
            act.wait_ge(sem("set"), 3 if tag == "n1" else 1)
            act.activation(RS[:, :].rearrange("p (h t) -> p h t", h=2), ps[:, :, 0:H2], ACT.Sqrt,
                           bias=eps[:, 0:1], scale=1.0 / D).then_inc(sem("rms"), 1)
            if hi is not None:
                for k in range(KB):
                    act.wait_ge(sem("scaled"), k + 2)
                    act.activation(hi[:, k, :], XT[:, k % 2, :], ACT.Copy).then_inc(sem("hi"), 1)

        @block.tensor
        def _(pe):
            pe.wait_ge(sem("set"), 3 if tag == "n1" else 1)
            for k in range(KB):
                pe.wait_ge(sem("square"), k + 1)
                for half in range(2):
                    mm = pe.matmul(ps[:, half, 0:H2], ones[:, :], SQ[:, k % 2, half * H2:(half + 1) * H2],
                                   start=k == 0, stop=k == KB - 1)
                mm.then_inc(sem("summed"), 1)

        @block.vector
        def _(dve):
            if tag == "n1":
                dve.memset(eps[:, 0:1], RMS_EPS).then_inc(sem("set"), 1)
                dve.memset(eps[:, 1:2], GN_EPS).then_inc(sem("set"), 1)
            dve.memset(ones[:, :], 1.0).then_inc(sem("set"), 1)
            if tag == "n1":
                dve.wait_ge(sem("par"), 16)
            dve.wait_ge(sem("rms"), 1)
            dve.reciprocal(RS[:, :], RS[:, :]).then_inc(sem("scaled"), 1)
            dve.wait_ge(sem("scaled"), 1)
            for k in range(KB + 1):
                if k < KB:
                    if k >= 2 and hi is not None:
                        dve.wait_ge(sem("hi"), k - 1)
                        dve.wait_ge(sem("lo"), k - 1)
                    if k >= 2 and out is not None:
                        dve.wait_ge(sem(f"stored{k % 2}"), 16 * (k // 2))
                    dve.scalar_tensor_tensor(XT[:, k % 2, :], X[:, k, :], par[:, gain + k:gain + k + 1], RS[:, :],
                                             ALU.mult, ALU.mult).then_inc(sem("scaled"), 1)
                if k >= 1 and hi is not None:
                    dve.wait_ge(sem("hi"), k)
                    dve.wait_ge(sem("scaled"), k + 1)
                    dve.tensor_tensor(lo[:, k - 1, :], XT[:, (k - 1) % 2, :], hi[:, k - 1, :].bitcast(F32),
                                      ALU.subtract).then_inc(sem("lo"), 1)


def row(t, k):
    return t[k] if isinstance(k, int) else t[bass.ds(k, 1)].rearrange("a p n -> (a p) n")


def unit_product(pe, W, c, acc, xh, xl, per=0, i=0):
    W.ready(pe, c, per, i)
    s = c % 2
    return product(pe, acc, lambda k: W.hi[:, s, k * P:(k + 1) * P], lambda k: W.lo[:, s, k * P:(k + 1) * P],
                   lambda k, h: xh[:, k, h * H2:(h + 1) * H2], lambda k, h: xl[:, k, h * H2:(h + 1) * H2], KB)


def attention(nc, S, A, O, acc, psS, psR, xh, xl, raw, whi, wlo, gates_d, o_d):
    with ExitStack() as ctx:
        sb = lambda n, s, d=F32: ctx.enter_context(nc.sbuf_tensor(n, s, d))
        cst = {n: sb("at_" + n, [P, P]) for n in ("ident", "negtri", "negones", "before")}
        QT, KT, VT = sb("QT", [P, T]), sb("KT", [P, SEQ + P]), sb("VT", [P, T])
        CK, CV = sb("CK", [P, PAST]), sb("CV", [P, 4, P])
        VTM = sb("VTM", [P, 5, P])
        NA, SPL, WT = sb("NA", [P, ZN]), sb("SPL", [P, ZN]), sb("WT", [P, ZN])
        GB, OT = sb("GB", [P, T]), sb("OT", [P, T])
        zbank = {"A": psS[:, 0, :], "B": psS[:, 1, 0:416], "C": psR[:, 0, :]}
        zcols = {"A": slice(0, 512), "B": slice(512, 928), "C": slice(928, 1440)}
        bank_of = {3: "A", 1: "A", 2: "B", 0: "C"}

        def z_at(kb, q0=None):
            b = bank_of[kb]
            lo = ZCOL[kb] - zcols[b].start
            return zbank[b][:, lo + ((q0 or kb * P) - kb * P):lo + SEQ - kb * P]

        def cols(kb, q0=None):
            return slice(ZCOL[kb] + ((q0 or kb * P) - kb * P), ZCOL[kb] + SEQ - kb * P)

        def smp(b):
            return slice(ZS + 32 * b, ZS + 32 * b + 32)

        W = Stream("at", S, raw, whi, wlo)
        UNITS = 4
        block = ctx.enter_context(nc.Block())

        @block.sync
        def _(sp):
            for n, t in cst.items():
                a, w = CST_AT[n]
                sp.dma_start(t[:, :], A["cst"][:, a:a + w]).then_inc(S["at_cst"], 16)
            with sp.Fori(0, HEADS) as i:
                for u in range(3):
                    W.load(sp, A["w_in"][bass.ds(i + 8 * u, 1)].rearrange("a p n -> (a p) n"), u, UNITS, i)
                sp.wait_ge(S["at_o_ready"], i + 1)
                sp.dma_start(CK[:, :], A["ckT"][bass.ds(i, 1)].rearrange("a p n -> (a p) n")).then_inc(S["cache_loaded"], 16)
                sp.dma_start(CV[:, :, :], A["cv"][bass.ds(i, 1)].rearrange("a p b n -> (a p) b n")).then_inc(S["cache_loaded"], 16)
                W.load(sp, A["w_in"][bass.ds(50 + i, 1)].rearrange("a p n -> (a p) n"), 3, UNITS, i)

        @block.gpsimd
        def _(pool):
            W.start_pool(pool)
            with pool.Fori(0, HEADS) as i:
                for u in range(UNITS):
                    W.split_lo(pool, u, UNITS, i)

        @block.tensor
        def _(pe):
            W.start_pe(pe)
            pe.sem_inc(S["at_o_ready"], 1)
            pe.wait_ge(S["at_cst"], 64)
            pe.wait_ge(S["pad_set"], 1)
            with pe.Fori(0, HEADS) as i:
                def project(u):
                    pe.wait_ge(S["at_acc_free"], UNITS * i + u + 1)
                    for mm in unit_product(pe, W, u, acc[u % 2], xh, xl, UNITS, i):
                        pass
                    mm.then_inc(W.used, 1)
                for u in range(3):
                    project(u)
                pe.wait_ge(S["at_acc_free"], UNITS * i + 5)
                pe.wait_ge(S["cache_loaded"], 32 * i + 32)
                pe.wait_ge(S["at_o_read"], i + 1)
                for kb in (3, 1):
                    mm = pe.matmul(z_at(kb), KT[:, kb * P:(kb + 1) * P], QT[:, kb * P:SEQ], start=kb == 3, stop=True,
                                   skip_group_check=True)
                mm.then_inc(S["z_ready"], 1)
                pe.matmul(z_at(2), KT[:, 2 * P:3 * P], QT[:, 2 * P:SEQ], start=True, stop=True)
                for b in range(5):
                    k = CK[:, b * P:(b + 1) * P] if b < 4 else KT[:, SEQ:SEQ + P]
                    mm = pe.matmul(zbank["B"][:, 256 + 32 * b:288 + 32 * b], k, QT[:, SEQ:T], start=False, stop=True,
                                   skip_group_check=True)
                mm.then_inc(S["z_ready"], 1)
                pe.matmul(z_at(0), KT[:, 0:P], QT[:, 0:SEQ], start=True, stop=True).then_inc(S["z_ready"], 1)
                for b in range(4):
                    mm = pe.transpose(psR[:, 1, b * P:(b + 1) * P], VT[:, b * P:(b + 1) * P], cst["ident"][:, :])
                mm.then_inc(S["vt_ready"], 1)
                project(3)
                pe.wait_ge(S["vtm_evac"], 2 * i + 1)
                pe.transpose(psR[0:DEC, 1, 0:P], VT[:, SEQ:T], cst["ident"][:, :]).then_inc(S["vt_ready"], 1)
                pe.wait_ge(S["sp_ready"], 8 * i + 8)

                def tri(out, blocks, at):
                    for n, b in enumerate(blocks):
                        mm = pe.matmul(out(b), cst["negtri" if n == 0 else "negones"][:, :], SPL[:, at(b)],
                                       start=False, stop=False, skip_group_check=True)
                    return mm
                tri(lambda b: z_at(3, b * P), (3,), cols)
                tri(lambda b: z_at(1, b * P), (1, 2, 3), cols).then_inc(S["tri_ready"], 1)
                tri(lambda b: z_at(2, b * P), (2, 3), cols)
                for b in range(5):
                    mm = tri(lambda _: zbank["B"][:, 256 + 32 * b:288 + 32 * b], range(b, 5), smp)
                mm.then_inc(S["tri_ready"], 1)
                tri(lambda b: z_at(0, b * P), (0, 1, 2, 3), cols).then_inc(S["tri_ready"], 1)
                pe.wait_ge(S["vtm_evac"], 2 * i + 2)
                pe.wait_ge(S["wt_ready"], 4 * i + 4)
                for kb in range(4):
                    pe.matmul(psR[:, 1, kb * P:SEQ], VTM[:, kb, :], WT[:, cols(kb)], start=kb == 0, stop=kb == 3,
                              skip_group_check=True)
                for b in range(4):
                    pe.matmul(psS[:, 0, 0:DEC], CV[:, b, :], WT[:, smp(b)], start=b == 0, stop=False)
                pe.matmul(psS[:, 0, 0:DEC], VTM[0:DEC, 4, :], WT[0:DEC, smp(4)], start=False,
                          stop=True).then_inc(S["at_o_ready"], 1)

        @block.scalar
        def _(act):
            act.sem_inc(S["at_acc_free"], 2)
            act.sem_inc(S["at_o_read"], 1)
            act.sem_inc(S["kv_stored"], 16)
            act.sem_inc(S["gate_stored"], 16)
            act.sem_inc(S["o_stored"], 16)
            W.split_hi(act, 0)

            def head(i, last):
                act.wait_ge(S["at_o_read"], i + 1)
                act.wait_ge(S["kv_stored"], 32 * i + 16)
                for u, (dst, scale) in enumerate(((QT, SM_SCALE), (KT, 1.0), (VT, 1.0))):
                    W.split_hi(act, u + 1, UNITS, i)
                    act.wait_ge(W.used, UNITS * i + u + 3)
                    act.activation(dst[:, 0:T].rearrange("p (h t) -> p h t", h=2), acc[u % 2][:, :, 0:H2], ACT.Copy,
                                   scale=scale).then_inc(S["at_acc_free"], 1)
                act.wait_ge(S["at_acc_free"], UNITS * i + 5)
                act.dma_start(O["kT"][bass.ds(i, 1)].rearrange("a p n -> (a p) n"), KT[:, 0:T]).then_inc(S["kv_stored"], 16)
                act.dma_start(O["vT"][bass.ds(i, 1)].rearrange("a p n -> (a p) n"), VT[:, :]).then_inc(S["kv_stored"], 16)
                act.wait_ge(S["vt_ready"], 2 * i + 1)
                act.activation(VTM[:, 0:4, :], psR[:, 1, :].rearrange("p (b n) -> p b n", b=4),
                               ACT.Copy).then_inc(S["vtm_evac"], 1)
                for n, b in enumerate("ABC"):
                    act.wait_ge(S["z_ready"], 3 * i + n + 1)
                    act.activation(NA[:, zcols[b]], zbank[b], ACT.Abs).then_inc(S["abs_done"], 1)
                act.wait_ge(S["abs_done"], 3 * i + 3)
                act.activation(NA[:, :], NA[:, :], ACT.Exp, scale=-1.0).then_inc(S["act_sp"], 1)
                act.wait_ge(S["act_sp"], 2 * i + 1)
                act.activation(NA[:, :], NA[:, :], ACT.Ln, bias=1.0).then_inc(S["act_sp"], 1)
                act.wait_ge(W.used, UNITS * i + 6)
                act.wait_ge(S["gate_stored"], 16 * i + 16)
                act.activation(GB[:, :].rearrange("p (h t) -> p h t", h=2), acc[1][:, :, 0:H2],
                               ACT.Sigmoid).then_inc(S["at_acc_free"], 1)
                act.wait_ge(S["at_acc_free"], UNITS * i + 6)
                act.dma_start(gates_d[bass.ds(i, 1)].rearrange("a p n -> (a p) n"), GB[:, :]).then_inc(S["gate_stored"], 16)
                if not last:
                    W.split_hi(act, 4, UNITS, i)
                act.wait_ge(S["vt_ready"], 2 * i + 2)
                act.activation(VTM[0:DEC, 4, :], psR[0:DEC, 1, 0:P], ACT.Copy).then_inc(S["vtm_evac"], 1)
                for n, b in enumerate("ABC"):
                    act.wait_ge(S["tri_ready"], 3 * i + n + 1)
                    act.activation(WT[:, zcols[b]], zbank[b], ACT.Exp).then_inc(S["wt_exp"], 1)
                act.wait_ge(S["at_o_ready"], i + 2)
                act.wait_ge(S["o_stored"], 16 * i + 16)
                act.activation(OT[:, 0:SEQ], psR[:, 1, :], ACT.Copy)
                act.activation(OT[:, SEQ:T], psS[:, 0, 0:DEC], ACT.Copy).then_inc(S["at_o_read"], 1)

                act.wait_ge(S["at_o_read"], i + 2)
                act.dma_start(o_d[bass.ds(i, 1)].rearrange("a p n -> (a p) n"), OT[:, :]).then_inc(S["o_stored"], 16)

            with act.Fori(0, HEADS - 1) as i:
                head(i, False)
            head(HEADS - 1, True)
            act.wait_ge(S["kv_stored"], 32 * HEADS + 16)
            act.wait_ge(S["gate_stored"], 16 * HEADS + 16)
            act.wait_ge(S["o_stored"], 16 * HEADS + 16)

        @block.vector
        def _(dve):
            dve.memset(KT[:, T:SEQ + P], 0.0).then_inc(S["pad_set"], 1)
            dve.wait_ge(S["at_cst"], 64)
            with dve.Fori(0, HEADS) as i:
                dve.wait_ge(S["act_sp"], 2 * i + 2)
                ch = Chain(dve, S["sp_ready"], 8, i)
                for n, b in enumerate("ABC"):
                    ch(dve.scalar_tensor_tensor(SPL[:, zcols[b]], zbank[b], 0.0, NA[:, zcols[b]], ALU.max, ALU.add), wait=False)
                dve.wait_ge(S["sp_ready"], 8 * i + 3)
                before = cst["before"]
                for at, parts in ((ZCOL[3], P), (ZCOL[1], P), (ZCOL[2], P), (ZCOL[0], P), (ZS + 128, DEC)):
                    s = slice(at, at + parts)
                    ch(dve.tensor_tensor(SPL[:, s], SPL[:, s], before[:, 0:parts], ALU.mult), wait=False)
                ch.end()
                dve.wait_ge(S["wt_exp"], 3 * i + 3)
                n = 0
                for at, parts in ((ZCOL[3], 2 * P), (ZCOL[2], P), (ZCOL[0], P), (ZS + 128, DEC)):
                    s = slice(at, at + parts)
                    if parts == 2 * P:
                        out = WT[:, s].rearrange("p (a n) -> p a n", a=2)
                        m = before[:, :].unsqueeze(1).to_broadcast([P, 2, P])
                    else:
                        out, m = WT[:, s], before[:, 0:parts]
                    dve.scalar_tensor_tensor(out, out, 1.0, m, ALU.min, ALU.mult).then_inc(S["wt_ready"], 1)


def rwkv(nc, S, A, O, acc, psS, psR, xh, xl, raw, whi, wlo, par, eps, gates_d, o_d):
    with ExitStack() as ctx:
        sb = lambda n, s, d=F32: ctx.enter_context(nc.sbuf_tensor(n, s, d))
        names = ["ident", "headones", "strict_T", "incl_T", "npair", "npair_T"] + [f"level_T{m}" for m in LEVELS]
        cst = sb("rw_cst", [P, len(names), P])
        C = {n: cst[:, k, :] for k, n in enumerate(names)}
        lr_mask = cst[:, 2:4, :].rearrange("p a n -> p (a n)")
        scan_mask = sb("scan_mask", [P, E])
        TWA, SGG = sb("TWA", [P, E]), sb("SGG", [P, E])
        LW = sb("LW", [P, 2, P])
        EX = sb("EX", [P, E + 1])
        RM, KM, VM, T1, T2 = (sb(n, [P, E]) for n in ("RM", "KM", "VM", "T1", "T2"))
        SG, AA, GG, CC, PP, BB, BV = (sb(n, [P, E]) for n in ("SG", "AA", "GG", "CC", "PP", "BB", "BV"))
        AR = sb("AR", [P, 2, E])
        YY = AA
        TM = sb("TM", [P, 5, 4, P])
        LTR, MTR = sb("LTR", [P, 5, 2 * P]), sb("MTR", [P, 5, 2 * P])
        TT = sb("TT", [P, 5, 2, P])
        BT, YB = sb("BT", [P, 5, P]), sb("YB", [P, 5, P])
        MV, NT = sb("MV", [P, 5, CH]), sb("NT", [P, 5, P])
        DI, K0, ST = sb("DI", [P, 9, CH]), sb("K0", [P, 9, CH]), sb("ST", [P, 9, CH])
        SS, SF = sb("SS", [P, CH]), sb("SF", [P, CH])
        SH = sb("SH", [P, 26, 2])
        GB, OT = sb("GBr", [P, T]), sb("OTr", [P, E])

        W = Stream("rw", S, raw, whi, wlo)
        UNITS, BASE, GATE0 = 6, 2, 8
        NS, NPV, NGV, NRS, NR = 12, 22, 5, 31, 94
        both = lambda t: t.rearrange("p (h t) -> p h t", h=2)
        tcol = lambda t: slice(t * P, (t + 1) * P) if t < 4 else slice(S0, S0 + DEC)
        rows = lambda hh: slice(CH * hh, CH * hh + CH)
        bank = lambda n: psR[:, n % 2, :]
        LEVEL0, POST = 6, 34
        y_fill = lambda hh, l, g: 42 * hh + LEVEL0 + 6 * l + g
        z_fill = lambda hh, l, g: 42 * hh + LEVEL0 + 6 * l + (2 if l == 4 else 3) + g
        groups = lambda l: 2 if l == 4 else 3
        tiles = lambda g: (2 * g, 2 * g + 1) if g < 2 else (4,)
        rs_bt = lambda hh, l: 15 * hh + 5 + l
        block = ctx.enter_context(nc.Block())

        def unit_src(u, i):
            k = 24 + 8 * u + i if u < 3 else 58 + (u - 3) + 3 * i
            return A["w_in"][bass.ds(k, 1)].rearrange("a p n -> (a p) n")

        @block.sync
        def _(sp):
            for k, n in enumerate(names):
                a, w = CST_AT[n]
                sp.dma_start(cst[:, k, :], A["cst"][:, a:a + w]).then_inc(S["rw_cst"], 16)
            a, w = CST_AT["scan"]
            sp.dma_start(scan_mask[:, :], A["cst"][:, a:a + w]).then_inc(S["rw_cst"], 16)
            W.load(sp, A["w_in"][48], 0)
            W.load(sp, A["w_in"][49], 1)
            with sp.Fori(0, PAIRS) as i:
                for u in range(UNITS):
                    W.load(sp, unit_src(u, i), BASE + u, UNITS, i)
                    if u == 0:
                        sp.wait_ge(S["rw_lora"], 3 * i + 1)
                        sp.dma_start(LW[:, :, :], A["lora"][bass.ds(i, 1)].rearrange("a p b n -> (a p) b n")).then_inc(S["lw_loaded"], 16)
                    if u == 1:
                        sp.wait_ge(S["rw_gn"], NGV * i + 1)
                        sp.dma_start(SS[:, :], A["s0T"][bass.ds(i, 1)].rearrange("a p n -> (a p) n")).then_inc(S["ss_loaded"], 16)

        @block.gpsimd
        def _(pool):
            W.start_pool(pool)
            W.split_lo(pool, 0)
            W.split_lo(pool, 1)
            with pool.Fori(0, PAIRS) as i:
                for u in range(UNITS):
                    W.split_lo(pool, BASE + u, UNITS, i)

        @block.tensor
        def _(pe):
            W.start_pe(pe)
            pe.sem_inc(S["rw_lora"], 1)
            pe.wait_ge(S["rw_cst"], 16 * (len(names) + 1))
            pe.wait_ge(S["rw_set"], 9)

            def project(c, per, i):
                pe.wait_ge(S["rw_acc_free"], per * i + c + 1)
                for n, mm in enumerate(unit_product(pe, W, c, acc[c % 2], xh, xl, per, i)):
                    if n == KB - 1:
                        mm.then_inc(W.used, 1)
                    yield

            def run(steps):
                for _ in steps:
                    pass
            run(project(0, 0, 0))
            run(project(1, 0, 0))

            with pe.Fori(0, PAIRS) as i:
                def gates():
                    for u in range(3, 6):
                        yield from project(BASE + u, UNITS, i)
                background = gates()

                def advance(n):
                    for _ in range(n):
                        next(background)

                def s_slot(n, lag=0):
                    pe.wait_ge(S["rw_s_free"], NS * i + n + 1 - lag)

                def small(n, lhsT, rhs):
                    s_slot(n)
                    for h in range(2):
                        mm = pe.matmul(psS[:, h, 0:EH], lhsT, rhs(slice(h * EH, (h + 1) * EH)), start=True, stop=True)
                    return mm

                run(project(BASE, UNITS, i))
                pe.wait_ge(S["lw_loaded"], 16 * i + 16)
                pe.wait_ge(S["rw_twa"], 3)
                small(0, LW[0:CH, 0, :], lambda s: TWA[0:CH, s]).then_inc(S["rw_lora"], 1)
                small(1, LW[CH:P, 0, :], lambda s: TWA[CH:P, s]).then_inc(S["rw_lora"], 1)
                small(2, LW[:, 1, :], lambda s: SGG[:, s]).then_inc(S["rw_lora"], 1)
                run(project(BASE + 1, UNITS, i))
                run(project(BASE + 2, UNITS, i))
                pe.wait_ge(S["rw_square"], 2 * i + 1)
                small(3, C["headones"], lambda s: T1[:, s]).then_inc(S["rw_n2"], 1)
                advance(8)
                pe.wait_ge(S["rw_prep"], NPV * i + 20)
                small(4, C["headones"], lambda s: T1[:, s]).then_inc(S["rw_bonus"], 1)
                pe.wait_ge(S["rw_prep"], NPV * i + 22)
                for t in range(5):
                    s_slot(5 + t, 1 if t else 0)
                    n = P if t < 4 else DEC
                    for a, x in enumerate((AR[:, 0, :], BB, KM, VM)):
                        mm = pe.transpose(psS[0:n, t % 2, a * P:(a + 1) * P], x[:, tcol(t)], C["ident"])
                    mm.then_inc(S["rw_tm"], 1)

                def slot(n, *needs):
                    pe.wait_ge(S["rw_r_free"], NR * i + max([n + 1, *(m + 3 for m in needs)]))

                def pass_waits():
                    pe.sem_inc(S["rw_pe_passed"], 1)

                def filled(mm):
                    mm.then_inc(S["rw_r_ready"], 1)

                def one(out, lhsT, rhs, start=True, stop=True, check=False):
                    return pe.matmul(out, lhsT, rhs, start=start, stop=stop, skip_group_check=not check)

                for hh in range(2):
                    r, h0 = rows(hh), 42 * hh
                    for n, (x, g) in enumerate(((BB, 0), (BB, 1), (KM, 0), (KM, 1))):
                        slot(h0 + n)
                        for j, t in enumerate(tiles(g)):
                            mm = one(bank(n)[:, 256 * j:256 * j + 256], x[r, tcol(t)], AR[r, :, tcol(t)])
                        filled(mm)
                    slot(h0 + 4)
                    for t in range(4):
                        mm = one(bank(4)[:, t * P:(t + 1) * P], AR[r, 0, tcol(t)], BB[r, tcol(t)])
                    filled(mm)
                    slot(h0 + 5)
                    pass_waits()
                    one(bank(5)[0:DEC, 0:64], BB[r, tcol(4)], AR[r, :, tcol(4)])
                    one(bank(5)[0:DEC, 64:128], KM[r, tcol(4)], AR[r, :, tcol(4)])
                    filled(one(bank(5)[0:DEC, 128:160], AR[r, 0, tcol(4)], BB[r, tcol(4)]))
                    for l, m in enumerate(LEVELS):
                        pe.wait_ge(S["rw_steps"], NRS * i + rs_bt(hh, l))
                        for g in range(groups(l)):
                            slot(y_fill(hh, l, g), *([z_fill(hh, l - 1, g)] if l else []))
                            if g == 2:
                                pass_waits()
                            o = bank(y_fill(hh, l, g))
                            for j, t in enumerate(tiles(g)):
                                n = P if t < 4 else DEC
                                mm = one(o[0:n, j * P:j * P + n], BT[0:n, t, 0:n], TT[0:n, t, 0, 0:n])
                            filled(mm)
                        advance(1)
                        for g in range(groups(l)):
                            slot(z_fill(hh, l, g), y_fill(hh, l, g))
                            if g == 2:
                                pass_waits()
                            o = bank(z_fill(hh, l, g))
                            for j, t in enumerate(tiles(g)):
                                n = P if t < 4 else DEC
                                if l < 4:
                                    one(o[0:n, 256 * j:256 * j + n], TT[0:n, t, 1, 0:n], YB[0:n, t, 0:n])
                                mm = one(o[0:n, 256 * j + P:256 * j + P + n], YB[0:n, t, 0:n], TT[0:n, t, 1, 0:n])
                            filled(mm)
                        advance(1)
                    p = h0 + POST
                    v = lambda t, n: TM[0:n, t, 3, r]
                    if hh == 0:
                        pe.wait_ge(S["rw_s_free"], NS * i + 11)
                    slot(p)
                    for t in range(5):
                        n = P if t < 4 else DEC
                        mm = one(bank(p)[0:n, t * CH:(t + 1) * CH], MTR[0:n, t, 0:n], v(t, n))
                    filled(mm)
                    for q, ts in ((p + 1, range(4)), (p + 2, (4,))):
                        slot(q, p, z_fill(hh, 4, 1))
                        pass_waits()
                        for j, t in enumerate(ts):
                            n = P if t < 4 else DEC
                            one(bank(q)[0:n, j * P:j * P + CH], TT[0:n, t, 1, 0:n], TM[0:n, t, 0, r])
                            mm = one(bank(q)[0:n, j * P + CH:(j + 1) * P], TT[0:n, t, 1, 0:n], MV[0:n, t, :])
                        filled(mm)
                    slot(p + 3, p + 1)
                    for t in range(4):
                        mm = one(bank(p + 3)[r, t * P:(t + 1) * P], NT[:, t, 0:CH], LTR[:, t, P:2 * P])
                    filled(mm)
                    slot(p + 4)
                    for t in range(4):
                        o = bank(p + 4)[r, t * P:(t + 1) * P]
                        one(o, NT[:, t, CH:P], LTR[:, t, P:2 * P], stop=False)
                        mm = one(o, v(t, P), MTR[:, t, P:2 * P], start=False)
                    filled(mm)
                    for odd in range(2):
                        slot(p + 5 + odd)
                        pass_waits()
                        s = slice(CH * odd, CH * odd + CH)
                        for n in range(CHUNKS // 2):
                            o = bank(p + 5 + odd)[r, n * CH:(n + 1) * CH]
                            one(o, NT[s, n, 0:CH], TM[s, n, 1, r])
                            o = bank(p + 5 + odd)[r, 256 + n * CH:256 + (n + 1) * CH]
                            one(o, TM[s, n, 2, r], TM[s, n, 3, r], stop=False)
                            mm = one(o, TM[s, n, 1, r], NT[s, n, CH:P], start=False)
                        filled(mm)
                    slot(p + 7, p + 2)
                    o, d = bank(p + 7)[r, :], slice(0, DEC)
                    one(o[:, 0:32], NT[d, 4, 0:CH], LTR[d, 4, P:P + DEC])
                    one(o[:, 32:64], NT[d, 4, CH:P], LTR[d, 4, P:P + DEC], stop=False)
                    one(o[:, 32:64], v(4, DEC), MTR[d, 4, P:P + DEC], start=False)
                    one(o[:, 64:128], NT[d, 4, 0:CH], TM[d, 4, 1, r])
                    one(o[:, 128:192], TM[d, 4, 2, r], TM[d, 4, 3, r], stop=False)
                    filled(one(o[:, 128:192], TM[d, 4, 1, r], NT[d, 4, CH:P], start=False))
                pe.wait_ge(S["ss_loaded"], 16 * i + 16)
                for c in range(CHUNKS):
                    slot(84 + c, 83 + c)
                    pass_waits()
                    for hh in range(2):
                        r = rows(hh)
                        mm = one(bank(84 + c)[r, 0:CH], DI[r, c, :], ST[r, c, :])
                        if c == 0:
                            mm = one(bank(84)[r, CH:2 * CH], DI[r, 8, :], SS[r, :])
                    filled(mm)
                    advance(1)
                slot(92, 91)
                pass_waits()
                for c in range(CHUNKS):
                    for hh in range(2):
                        r = rows(hh)
                        mm = one(bank(92)[r, c * CH:(c + 1) * CH], ST[r, c, :], AR[r, 1, c * CH:(c + 1) * CH])
                filled(mm)
                slot(93)
                pass_waits()
                for hh in range(2):
                    r = rows(hh)
                    mm = one(bank(93)[r, 0:DEC], SS[r, :], AR[r, 1, S0:S0 + DEC])
                filled(mm)
                slot(93, 93)
                small(10, C["headones"], lambda s: YY[:, s]).then_inc(S["rw_mean"], 1)
                advance(6)
                pe.wait_ge(S["rw_square"], 2 * i + 2)
                small(11, C["headones"], lambda s: T2[:, s]).then_inc(S["rw_var"], 1)
                run(background)

        @block.scalar
        def _(act):
            act.sem_inc(S["rw_acc_free"], 2)
            act.sem_inc(S["rw_s_free"], 1)
            act.sem_inc(S["rw_gate_stored"], 16)
            act.sem_inc(S["rw_stored"], 16)
            act.wait_ge(S["rw_set"], 9)

            def evacuate(c, per, i, ready):
                act.wait_ge(W.used, per * i + c + 3)
                act.activation(EX[:, 1:H2 + 1], acc[c % 2][:, 0, 0:H2], ACT.Copy)
                act.activation(EX[:, H2 + 1:SEQ + 1], acc[c % 2][:, 1, 0:SEQ - H2], ACT.Copy)
                act.activation(EX[:, S0 + 1:S0 + 1 + DEC], acc[c % 2][:, 1, SEQ - H2:H2], ACT.Copy).then_inc(S["rw_acc_free"], 1)
                act.activation(EX[:, S0:S0 + 1], ready, ACT.Copy).then_inc(S["rw_p_ready"], 1)

            W.split_hi(act, 0)
            W.split_hi(act, 1)
            evacuate(0, 0, 0, par[:, C_SHIFT + 24:C_SHIFT + 25])
            act.wait_ge(S["rw_first"], 3)
            act.activation(TWA[0:CH, :], RM[0:CH, :], ACT.Tanh).then_inc(S["rw_twa"], 1)
            act.activation(TWA[CH:P, :], RM[CH:P, :], ACT.Copy).then_inc(S["rw_twa"], 1)
            evacuate(1, 0, 0, par[:, C_SHIFT + 25:C_SHIFT + 26])
            act.wait_ge(S["rw_first"], 6)
            act.activation(SGG[:, :], KM[:, :], ACT.Sigmoid).then_inc(S["rw_twa"], 1)
            W.split_hi(act, 2)

            def pair(i, last):
                col = lambda n: par[:, bass.ds(NPAR * i + PAR.index(n), 1)]
                shift = lambda a: par[:, bass.ds(C_SHIFT + 8 * a + i, 1)]
                W.split_hi(act, 3, UNITS, i)
                evacuate(2, UNITS, i, shift(0))
                act.wait_ge(S["rw_gn"], NGV * i + 1)
                act.wait_ge(S["rw_lora"], 3 * i + 2)
                act.activation(both(SG[:, :]), psS[:, :, 0:EH], ACT.Sigmoid, bias=col("w0")).then_inc(S["rw_s_free"], 1)
                act.wait_ge(S["rw_lora"], 3 * i + 3)
                act.activation(both(AA[:, :]), psS[:, :, 0:EH], ACT.Sigmoid, bias=col("a0")).then_inc(S["rw_s_free"], 1)
                act.wait_ge(S["rw_lora"], 3 * i + 4)
                act.activation(both(GG[:, :]), psS[:, :, 0:EH], ACT.Copy).then_inc(S["rw_s_free"], 1)
                W.split_hi(act, 4, UNITS, i)
                act.wait_ge(S["rw_prep"], NPV * i + 5)
                act.activation(PP[:, :], CC[:, :], ACT.Exp, scale=-KAPPA).then_inc(S["rw_decay"], 1)
                act.activation(SG[:, :], SG[:, :], ACT.Exp, scale=-KAPPA).then_inc(S["rw_decay"], 1)
                act.wait_ge(S["rw_decay"], 4 * i + 1)
                act.activation(CC[:, :], CC[:, :], ACT.Exp, scale=KAPPA).then_inc(S["rw_decay"], 1)
                evacuate(3, UNITS, i, shift(1))
                W.split_hi(act, 5, UNITS, i)
                act.wait_ge(S["rw_prep"], NPV * i + 8)
                act.activation(T1[:, :], KM[:, :], ACT.Square, scale=col("k_k")).then_inc(S["rw_square"], 1)
                evacuate(4, UNITS, i, shift(2))
                W.split_hi(act, 6, UNITS, i)
                act.wait_ge(S["rw_s_free"], NS * i + 5)
                act.activation(T1[:, :], T1[:, :], ACT.Sqrt).then_inc(S["rw_decay"], 1)
                for t in range(5):
                    n = P if t < 4 else DEC
                    act.wait_ge(S["rw_tm"], 5 * i + t + 1)
                    act.activation(TM[0:n, t, :, :].rearrange("p a n -> p (a n)"), psS[0:n, t % 2, :],
                                   ACT.Copy).then_inc(S["rw_s_free"], 1)
                for u in range(2):
                    gate(i, u)
                    if u == 0 or not last:
                        W.split_hi(act, 7 + u, UNITS, i)
                act.wait_ge(S["rw_s_free"], NS * i + 12)
                act.activation(T2[:, :], T1[:, :], ACT.Square).then_inc(S["rw_square"], 1)
                act.wait_ge(S["rw_var"], i + 1)
                act.activation(both(SG[:, :]), psS[:, :, 0:EH], ACT.Sqrt, bias=eps[:, 1:2],
                               scale=1.0 / CH).then_inc(S["rw_s_free"], 1)
                act.wait_ge(S["rw_gn"], NGV * i + NGV + 1)
                act.dma_start(o_d[bass.ds(HEADS + i, 1), :, 0:SEQ].rearrange("a p n -> (a p) n"), OT[:, 0:SEQ]).then_inc(S["rw_stored"], 16)
                act.dma_start(o_d[bass.ds(HEADS + i, 1), :, SEQ:T].rearrange("a p n -> (a p) n"), OT[:, S0:S0 + DEC]).then_inc(S["rw_stored"], 16)
                act.dma_start(O["wkvp"][bass.ds(i, 1)].rearrange("a p n -> (a p) n"), ST[:, 8, :]).then_inc(S["rw_stored"], 16)
                act.dma_start(O["wkvs"][bass.ds(i, 1)].rearrange("a p n -> (a p) n"), SF[:, :]).then_inc(S["rw_stored"], 16)
                gate(i, 2)

            def gate(i, u):
                c = BASE + 3 + u
                act.wait_ge(W.used, UNITS * i + c + 3)
                act.wait_ge(S["rw_gate_stored"], 48 * i + 16 * u + 16)
                act.activation(both(GB[:, :]), acc[c % 2][:, :, 0:H2], ACT.Sigmoid).then_inc(S["rw_acc_free"], 1)
                act.wait_ge(S["rw_acc_free"], UNITS * i + c + 3)
                act.dma_start(gates_d[bass.ds(3 * i + GATE0 + u, 1)].rearrange("a p n -> (a p) n"), GB[:, :]).then_inc(S["rw_gate_stored"], 16)

            with act.Fori(0, PAIRS - 1) as i:
                pair(i, False)
            pair(PAIRS - 1, True)
            act.wait_ge(S["rw_first"], 6)
            act.dma_start(O["shift"], SH[:, :, :]).then_inc(S["rw_stored"], 16)
            act.wait_ge(S["rw_gate_stored"], 48 * PAIRS + 16)
            act.wait_ge(S["rw_stored"], 64 * PAIRS + 32)

        @block.vector
        def _(dve):
            for t in (LTR, MTR, TT, BT, YB):
                dve.memset(t[:, 4], 0.0).then_inc(S["rw_set"], 1)
            dve.memset(ST[:, 0, :], 0.0).then_inc(S["rw_set"], 1)
            dve.memset(EX[:, 0:1], 0.0).then_inc(S["rw_set"], 1)
            dve.memset(EX[:, E:E + 1], 0.0).then_inc(S["rw_set"], 1)
            dve.memset(SH[:, :, :], 0.0).then_inc(S["rw_set"], 1)
            dve.sem_inc(S["rw_gn"], 1)
            dve.sem_inc(S["rw_r_free"], 2)
            dve.wait_ge(S["rw_set"], 9)
            dve.wait_ge(S["rw_cst"], 16 * (len(names) + 1))

            def mix(ch, dst, mu, at, ready):
                dve.wait_ge(S["rw_p_ready"], ready)
                ch(dve.tensor_tensor(T1[:, :], EX[:, 0:E], EX[:, 1:E + 1], ALU.subtract))
                ch(dve.scalar_tensor_tensor(dst[:, :], T1[:, :], mu, EX[:, 1:E + 1], ALU.mult, ALU.add))
                ch(dve.tensor_copy(SH[:, at, :], EX[:, SEQ:E:DEC + 1]))

            first = Chain(dve, S["rw_first"], 6, 0)
            mix(first, RM, par[:, C_MUWA:C_MUWA + 1], slice(24, 25), 1)
            mix(first, KM, par[:, C_MUG:C_MUG + 1], slice(25, 26), 2)

            dve.wait_ge(S["rw_twa"], 3)
            with dve.Fori(0, PAIRS) as i:
                col = lambda n: par[:, bass.ds(NPAR * i + PAR.index(n), 1)]
                ch = Chain(dve, S["rw_prep"], NPV, i)
                tt = lambda o, a, b, op: ch(dve.tensor_tensor(o[:, :], a[:, :], b[:, :], op))
                mix(ch, RM, col("mu_r"), bass.ds(i, 1), 3 * i + 3)
                dve.wait_ge(S["rw_s_free"], NS * i + 2)
                ch(dve.tensor_tensor_scan(CC[:, :], scan_mask[:, :], SG[:, :], 0.0, ALU.mult, ALU.add))
                tt(SG, CC, SG, ALU.subtract)
                mix(ch, KM, col("mu_k"), bass.ds(8 + i, 1), 3 * i + 4)
                dve.wait_ge(S["rw_p_ready"], 3 * i + 5)
                ch(dve.tensor_tensor(T2[:, :], EX[:, 0:E], EX[:, 1:E + 1], ALU.subtract))
                ch(dve.scalar_tensor_tensor(VM[:, :], T2[:, :], col("mu_v"), EX[:, 1:E + 1], ALU.mult, ALU.add))
                ch(dve.tensor_copy(SH[:, bass.ds(16 + i, 1), :], EX[:, SEQ:E:DEC + 1]))
                ch(dve.tensor_scalar(T2[:, :], KM[:, :], col("k_k"), None, ALU.mult))
                dve.wait_ge(S["rw_n2"], i + 1)
                dve.tensor_scalar(both(T1[:, :]), psS[:, :, 0:EH], 1e-24, None, ALU.max).then_inc(S["rw_s_free"], 1)
                dve.wait_ge(S["rw_decay"], 4 * i + 4)
                ch(dve.reciprocal(T1[:, :], T1[:, :]))
                tt(T2, T2, T1, ALU.mult)
                ch(dve.tensor_tensor(BB[:, :], T2[:, :], AA[:, :], ALU.mult))
                ch(dve.tensor_tensor(AR[:, 0, :], T2[:, :], SG[:, :], ALU.mult), wait=False)
                tt(BB, BB, CC, ALU.mult)
                ch(dve.tensor_scalar(AA[:, :], AA[:, :], 1.0, col("k_a"), ALU.subtract, ALU.mult))
                ch(dve.scalar_tensor_tensor(KM[:, :], AA[:, :], 1.0, KM[:, :], ALU.add, ALU.mult))
                ch(dve.scalar_tensor_tensor(T1[:, :], RM[:, :], col("r_k"), KM[:, :], ALU.mult, ALU.mult))
                tt(KM, KM, CC, ALU.mult)
                ch(dve.tensor_tensor(AR[:, 1, :], RM[:, :], PP[:, :], ALU.mult))
                ch.end()
                dve.wait_ge(S["rw_bonus"], i + 1)
                dve.tensor_tensor(both(BV[:, :]), psS[:, :, 0:EH], both(VM[:, :]), ALU.mult).then_inc(S["rw_s_free"], 1)

                rs = Chain(dve, S["rw_steps"], NRS, i)
                counted = [0]

                def ready(n):
                    assert n == counted[0], (n, counted[0])
                    dve.wait_ge(S["rw_r_ready"], NR * i + n + 1)
                    return bank(n)

                def read(instruction):
                    counted[0] += 1
                    instruction.then_inc(S["rw_r_free"], 1)

                def after_read():
                    dve.wait_ge(S["rw_r_free"], NR * i + counted[0] + 2)

                over = lambda m, *shape: m.unsqueeze(1).to_broadcast(list(shape))
                split2 = lambda t: t.rearrange("p (a n) -> p a n", a=2)
                split4 = lambda t: t.rearrange("p (a n) -> p a n", a=4)
                for hh in range(2):
                    r, h0, d = rows(hh), 42 * hh, slice(0, DEC)
                    for n, (x, g) in enumerate(((LTR, 0), (LTR, 1), (MTR, 0), (MTR, 1))):
                        ps = ready(h0 + n)
                        read(dve.tensor_tensor(x[:, 2 * g:2 * g + 2, :], split2(ps), over(lr_mask, P, 2, 2 * P), ALU.mult))
                    ps = ready(h0 + 4)
                    read(dve.tensor_tensor(TT[:, 0:4, 0, :], split4(ps), over(C["npair"], P, 4, P), ALU.mult))
                    ps = ready(h0 + 5)
                    lrs = cst[d, 2:4, 0:DEC]
                    for x, o in ((LTR, 0), (MTR, 64)):
                        rs(dve.tensor_tensor(split2(x[d, 4, :])[:, :, 0:DEC], split2(ps[d, o:o + 64]), lrs, ALU.mult), wait=False)
                    read(dve.tensor_tensor(TT[d, 4, 0, 0:DEC], ps[d, 128:160], C["npair"][d, 0:DEC], ALU.mult))
                    after_read()
                    rs(dve.tensor_tensor(TT[:, :, 1, :], LTR[:, :, 0:P], over(C["npair_T"], P, 5, P), ALU.mult))
                    rs(dve.tensor_tensor(TT.rearrange("p a b n -> p (a b) n"), TT.rearrange("p a b n -> p (a b) n"), over(C["ident"], P, 10, P), ALU.add), wait=False)

                    def level_mask(l):
                        rs(dve.tensor_tensor(BT[:, :, :], LTR[:, :, 0:P], over(C[f"level_T{LEVELS[l]}"], P, 5, P), ALU.mult), wait=False)
                        assert rs.k == rs_bt(hh, l)
                    level_mask(0)
                    for l, m in enumerate(LEVELS):
                        for g in range(groups(l)):
                            ps = ready(y_fill(hh, l, g))
                            if g < 2:
                                read(dve.tensor_copy(YB[:, 2 * g:2 * g + 2, :], split2(ps[:, 0:2 * P])))
                            else:
                                read(dve.tensor_copy(YB[d, 4, 0:DEC], ps[d, 0:DEC]))
                        if l < 4:
                            level_mask(l + 1)
                        for g in range(groups(l)):
                            ps = ready(z_fill(hh, l, g))
                            if l == 4:
                                o = TT[:, 2 * g:2 * g + 2, 1, :]
                                read(dve.tensor_tensor(o, o, split2(ps)[:, :, P:2 * P], ALU.subtract))
                            elif g < 2:
                                o = TT[:, 2 * g:2 * g + 2, :, :].rearrange("p a b n -> p (a b n)")
                                read(dve.tensor_tensor(o, o, ps, ALU.subtract))
                            else:
                                o = TT[d, 4, :, 0:DEC]
                                read(dve.tensor_tensor(o, o, split2(ps[d, 0:2 * P])[:, :, 0:DEC], ALU.subtract))
                    p = h0 + POST
                    ps = ready(p)
                    rs(dve.tensor_copy(MV[:, 0:4, :], split4(ps[:, 0:4 * CH])), wait=False)
                    read(dve.tensor_copy(MV[d, 4, :], ps[d, 4 * CH:5 * CH]))
                    ps = ready(p + 1)
                    read(dve.tensor_scalar(NT[:, 0:4, :], split4(ps), -1.0, None, ALU.mult))
                    ps = ready(p + 2)
                    read(dve.tensor_scalar(NT[d, 4, :], ps[d, 0:P], -1.0, None, ALU.mult))
                    ps = ready(p + 3)
                    read(dve.tensor_tensor(AR[r, 1, 0:SEQ], AR[r, 1, 0:SEQ], ps[r, :], ALU.add))
                    ps = ready(p + 4)
                    read(dve.tensor_copy(AR[r, 0, 0:SEQ], ps[r, :]))
                    eye = C["ident"][r, r]
                    for odd in range(2):
                        ps = ready(p + 5 + odd)
                        rs(dve.tensor_tensor(DI[r, odd:8:2, :], split4(ps[r, 0:256]),
                                             eye.unsqueeze(1).to_broadcast([CH, 4, CH]), ALU.add), wait=False)
                        end = PP[r, (odd + 1) * CH - 1:SEQ:2 * CH]
                        read(dve.tensor_tensor(K0[r, odd:8:2, :], split4(ps[r, 256:512]),
                                               end.unsqueeze(2).to_broadcast([CH, 4, CH]), ALU.mult))
                    ps = ready(p + 7)
                    s = slice(S0, S0 + DEC)
                    rs(dve.tensor_tensor(AR[r, 1, s], AR[r, 1, s], ps[r, 0:32], ALU.add), wait=False)
                    rs(dve.tensor_copy(AR[r, 0, s], ps[r, 32:64]), wait=False)
                    rs(dve.tensor_tensor(DI[r, 8, :], ps[r, 64:128], eye, ALU.add), wait=False)
                    read(dve.tensor_scalar(K0[r, 8, :], ps[r, 128:192], PP[r, S0 + DEC - 1:S0 + DEC], None, ALU.mult))
                after_read()
                dve.wait_ge(S["rw_stored"], 64 * i + 16)
                for c in range(CHUNKS):
                    ps = ready(84 + c)
                    if c == 0:
                        rs(dve.scalar_tensor_tensor(SF[:, :], ps[:, CH:2 * CH], PP[:, S0 + DEC - 1:S0 + DEC], K0[:, 8, :],
                                                    ALU.mult, ALU.add), wait=False)
                    read(dve.scalar_tensor_tensor(ST[:, c + 1, :], ps[:, 0:CH], PP[:, c * CH + CH - 1:(c + 1) * CH], K0[:, c, :],
                                                  ALU.mult, ALU.add))
                rs.end()
                ps = ready(92)
                read(dve.tensor_tensor(YY[:, 0:SEQ], ps, AR[:, 0, 0:SEQ], ALU.add))
                ps = ready(93)
                read(dve.tensor_tensor(YY[:, S0:S0 + DEC], ps[:, 0:DEC], AR[:, 0, S0:S0 + DEC], ALU.add))
                after_read()
                gn = Chain(dve, S["rw_gn"], NGV, i, credit=1)
                dve.wait_ge(S["rw_mean"], i + 1)
                dve.scalar_tensor_tensor(both(T1[:, :]), psS[:, :, 0:EH], -1.0 / CH, both(YY[:, :]), ALU.mult,
                                         ALU.add).then_inc(S["rw_s_free"], 1)
                dve.wait_ge(S["rw_s_free"], NS * i + 13)
                gn(dve.reciprocal(SG[:, :], SG[:, :]))
                gn(dve.tensor_tensor(T1[:, :], T1[:, :], SG[:, :], ALU.mult))
                gn(dve.tensor_scalar(T1[:, :], T1[:, :], col("ln_g"), col("ln_b"), ALU.mult, ALU.add))
                gn(dve.tensor_tensor(T1[:, :], T1[:, :], BV[:, :], ALU.add))
                gn(dve.tensor_tensor(OT[:, :], T1[:, :], GG[:, :], ALU.mult))
                gn.end()


def mix(nc, S, A, acc, psS, psR, mh, ml, gates_d, o_d):
    with ExitStack() as ctx:
        sb = lambda n, s, d=F32: ctx.enter_context(nc.sbuf_tensor(n, s, d))
        oh, ol = sb("oh", [P, KB, T], F32R), sb("ol", [P, KB, T], F32R)
        raw, whi, wlo = sb("raw_m", [P, 2, D]), sb("whi_m", [P, 2, D], F32R), sb("wlo_m", [P, 2, D], F32R)
        OF, G, MX = sb("OF", [P, 2, T]), sb("G", [P, 2, 2, T]), sb("MX", [P, 2, T])
        W = Stream("mx", S, raw, whi, wlo)
        N = 2
        ps = [(acc[0], acc[1]), (psS, psR)]
        halves = lambda t: t.rearrange("p (h t) -> p h t", h=2)
        block = ctx.enter_context(nc.Block())

        @block.sync
        def _(sp):
            for k in range(KB):
                if k >= 2:
                    sp.wait_ge(S["mx_o_lo"], k - 1)
                sp.dma_start(OF[:, k % 2, :], o_d[k]).then_inc(S[f"mx_o_loaded{k % 2}"], 16)
                if k < 2:
                    W.load(sp, A["w_br"][k], k)

            def block_pair(i, last):
                for u in range(N):
                    sp.wait_ge(S["mx_sum"], N * i + u + 1)
                    for g in range(2):
                        sp.dma_start(G[:, u, g, :], row(gates_d, N * i + u + KB * g)).then_inc(S[f"mx_gates{u}"], 16)
                    if not last:
                        W.load(sp, row(A["w_br"], N * i + u + 2), u + 2, N, i)
            with sp.Fori(0, KB // N - 1) as i:
                block_pair(i, False)
            block_pair(KB // N - 1, True)

        @block.gpsimd
        def _(pool):
            W.start_pool(pool)
            W.split_lo(pool, 0)
            W.split_lo(pool, 1)
            with pool.Fori(0, KB // N - 1) as i:
                for u in range(N):
                    W.split_lo(pool, u + 2, N, i)

        @block.tensor
        def _(pe):
            W.start_pe(pe)
            pe.wait_ge(S["mx_o_lo"], KB)
            with pe.Fori(0, KB // N) as i:
                for u in range(N):
                    W.ready(pe, u, N, i)
                    pe.wait_ge(S["mx_mixed"], 2 * (N * i + u) + 2)
                    for g in range(2):
                        for mm in product(pe, ps[u][g], lambda k: whi[:, u, (8 * g + k) * P:(8 * g + k + 1) * P],
                                          lambda k: wlo[:, u, (8 * g + k) * P:(8 * g + k + 1) * P],
                                          lambda k, h: oh[:, 8 * g + k, h * H2:(h + 1) * H2],
                                          lambda k, h: ol[:, 8 * g + k, h * H2:(h + 1) * H2], 8):
                            pass
                    mm.then_inc(W.used, 1)

        @block.scalar
        def _(act):
            W.split_hi(act, 0)
            W.split_hi(act, 1)
            for k in range(KB):
                act.wait_ge(S[f"mx_o_loaded{k % 2}"], 16 * (k // 2 + 1))
                act.activation(oh[:, k, :], OF[:, k % 2, :], ACT.Copy).then_inc(S["mx_o_hi"], 1)

            def block_pair(i, last):
                for u in range(N):
                    act.wait_ge(S["mx_sum"], N * i + u + 3)
                    act.activation(mh[:, bass.ds(N * i + u, 1), :].rearrange("p a t -> p (a t)") if not last else mh[:, N * i + u, :],
                                   MX[:, u, :], ACT.Copy).then_inc(S["mx_hi_part"], 1)
                    if not last:
                        W.split_hi(act, u + 2, N, i)
            with act.Fori(0, KB // N - 1) as i:
                block_pair(i, False)
            block_pair(KB // N - 1, True)

        @block.vector
        def _(dve):
            dve.sem_inc(S["mx_mixed"], 4)
            dve.sem_inc(S["mx_sum"], 2)
            for k in range(KB):
                dve.wait_ge(S["mx_o_hi"], k + 1)
                dve.tensor_tensor(ol[:, k, :], OF[:, k % 2, :], oh[:, k, :].bitcast(F32), ALU.subtract).then_inc(S["mx_o_lo"], 1)
            with dve.Fori(0, KB // N) as i:
                for u in range(N):
                    dve.wait_ge(S[f"mx_gates{u}"], 32 * i + 32)
                    dve.wait_ge(W.used, N * i + u + 3)
                    g = G[:, u, :, :]
                    for b in range(2):
                        dve.tensor_tensor(halves(g[:, b, :]), ps[u][b][:, :, 0:H2], halves(g[:, b, :]), ALU.mult).then_inc(S["mx_mixed"], 1)
                    dve.wait_ge(S["mx_mixed"], 2 * (N * i + u) + 6)
                    dve.tensor_tensor(MX[:, u, :], g[:, 0, :], g[:, 1, :], ALU.add).then_inc(S["mx_sum"], 1)
                    dve.wait_ge(S["mx_hi_part"], N * i + u + 1)
                    k = bass.ds(N * i + u, 1)
                    flat = lambda t: t[:, k, :].rearrange("p a t -> p (a t)")
                    dve.tensor_tensor(flat(ml), MX[:, u, :], flat(mh).bitcast(F32), ALU.subtract).then_inc(S["mx_lo_part"], 1)
                    dve.wait_ge(S["mx_lo_part"], N * i + u + 1)


def out_projection(nc, S, A, acc, mh, ml, h_d):
    with ExitStack() as ctx:
        sb = lambda n, s, d=F32: ctx.enter_context(nc.sbuf_tensor(n, s, d))
        raw, whi, wlo = sb("raw_o", [P, 2, D]), sb("whi_o", [P, 2, D], F32R), sb("wlo_o", [P, 2, D], F32R)
        XB = sb("XB", [P, 2, T])
        W = Stream("wo", S, raw, whi, wlo)
        N = 2
        halves = lambda t: t.rearrange("p (h t) -> p h t", h=2)
        block = ctx.enter_context(nc.Block())

        @block.sync
        def _(sp):
            W.load(sp, A["w_out"][0], 0)
            W.load(sp, A["w_out"][1], 1)

            def block_pair(i, last):
                for u in range(N):
                    k = bass.ds(N * i + u, 1)
                    sp.wait_ge(S[f"wo_stored{u}"], 16 * i + 16)
                    sp.dma_start(XB[:, u, :], A["xT"][:, k, :].rearrange("p a t -> p (a t)")).then_inc(S[f"wo_x{u}"], 16)
                    if not last:
                        W.load(sp, row(A["w_out"], N * i + u + 2), u + 2, N, i)
            with sp.Fori(0, KB // N - 1) as i:
                block_pair(i, False)
            block_pair(KB // N - 1, True)

        @block.gpsimd
        def _(pool):
            W.start_pool(pool)
            W.split_lo(pool, 0)
            W.split_lo(pool, 1)
            with pool.Fori(0, KB // N - 1) as i:
                for u in range(N):
                    W.split_lo(pool, u + 2, N, i)

        @block.tensor
        def _(pe):
            W.start_pe(pe)
            with pe.Fori(0, KB // N) as i:
                for u in range(N):
                    pe.wait_ge(S["wo_sum"], N * i + u + 1)
                    for mm in unit_product(pe, W, u, acc[u], mh, ml, N, i):
                        pass
                    mm.then_inc(W.used, 1)

        @block.scalar
        def _(act):
            act.sem_inc(S["wo_stored0"], 16)
            act.sem_inc(S["wo_stored1"], 16)
            W.split_hi(act, 0)
            W.split_hi(act, 1)

            def block_pair(i, last):
                for u in range(N):
                    act.wait_ge(S["wo_sum"], N * i + u + 3)
                    dst = h_d[N * i + u] if last else h_d[bass.ds(N * i + u, 1)].rearrange("a p n -> (a p) n")
                    act.dma_start(dst, XB[:, u, :]).then_inc(S[f"wo_stored{u}"], 16)
                    if not last:
                        W.split_hi(act, u + 2, N, i)
            with act.Fori(0, KB // N - 1) as i:
                block_pair(i, False)
            block_pair(KB // N - 1, True)
            act.wait_ge(S["wo_stored0"], 16 * (KB // N) + 16)
            act.wait_ge(S["wo_stored1"], 16 * (KB // N) + 16)

        @block.vector
        def _(dve):
            dve.sem_inc(S["wo_sum"], 2)
            with dve.Fori(0, KB // N) as i:
                for u in range(N):
                    dve.wait_ge(S[f"wo_x{u}"], 16 * i + 16)
                    dve.wait_ge(W.used, N * i + u + 3)
                    dve.tensor_tensor(halves(XB[:, u, :]), acc[u][:, :, 0:H2], halves(XB[:, u, :]), ALU.add).then_inc(S["wo_sum"], 1)


def retrieval(nc, S, A, acc, psS, psR, hh, hl, IT):
    with ExitStack() as ctx:
        sb = lambda n, s, d=F32: ctx.enter_context(nc.sbuf_tensor(n, s, d))
        raw, whi, wlo = sb("raw_q", [P, 2, D]), sb("whi_q", [P, 2, D], F32R), sb("wlo_q", [P, 2, D], F32R)
        ident, iota = sb("tk_ident", [P, P]), sb("tk_iota", [P, P])
        QT, KEYS = sb("tk_QT", [P, 2, T]), sb("KEYS", [P, 2, NK])
        SC, SC2 = sb("SC", [P, 1, 5, 2, NK]), sb("SC2", [P, 5, 2, NK])
        V, I = sb("V", [P, 5, 2, TOPK]), sb("I", [P, 5, 2, TOPK], U32)
        IF = sb("IF", [P, 5, 2, TOPK])
        CA, CA2 = sb("CA", [P, 5, TOPK * TOPK]), sb("CA2", [P, 5, TOPK * TOPK])
        TOP = sb("TOP", [P, 5, TOPK])
        POS, PH2, PHF = sb("POS", [P, 5, TOPK], U32), sb("PH2", [P, 5, 2, TOPK], U32), sb("PHF", [P, 5, 2, TOPK])
        OUT = sb("OUT", [P, 3, 5, PH, TOPK])
        SUM = sb("SUM", [P, 5, PH])
        W = Stream("wq", S, raw, whi, wlo)
        N = 2
        NCH = 8
        halves = lambda t: t.rearrange("p (h t) -> p h t", h=2)
        rows = lambda t: P if t < 4 else DEC
        LOW = -3.0e38
        block = ctx.enter_context(nc.Block())

        @block.sync
        def _(sp):
            sp.dma_start(KEYS[:, :, :], A["keys"]).then_inc(S["tk_cst"], 16)
            for t, n in ((ident, "ident"), (iota, "iota")):
                sp.dma_start(t[:, :], A["cst"][:, CST_AT[n][0]:CST_AT[n][0] + P]).then_inc(S["tk_cst"], 16)
            W.load(sp, A["w_q"][0], 0)
            W.load(sp, A["w_q"][1], 1)
            with sp.Fori(0, PH - 1) as i:
                for u in range(N):
                    W.load(sp, A["w_q"][bass.ds(N * i + u + 2, 1)].rearrange("a p n -> (a p) n"), u + 2, N, i)

        @block.gpsimd
        def _(pool):
            W.start_pool(pool)
            W.split_lo(pool, 0)
            W.split_lo(pool, 1)
            with pool.Fori(0, PH - 1) as i:
                for u in range(N):
                    W.split_lo(pool, u + 2, N, i)

        @block.tensor
        def _(pe):
            W.start_pe(pe)
            pe.wait_ge(S["tk_cst"], 48)
            with pe.Fori(0, PH) as i:
                for u in range(N):
                    pe.wait_ge(S["tk_q"], N * i + u + 1)
                    for mm in unit_product(pe, W, u, acc[u], hh, hl, N, i):
                        pass
                    mm.then_inc(W.used, 1)
                for u, ps in enumerate((psS, psR)):
                    pe.wait_ge(S["tk_q"], N * i + u + 3)
                    pe.wait_ge(S["tk_scores"], N * i + u + 1)
                    for t in range(5):
                        n = rows(t)
                        mm = pe.matmul(ps[0:n, t // 4, (t % 4) * P:(t % 4 + 1) * P], QT[:, u, t * P:t * P + n],
                                       KEYS[:, u, :], start=t % 4 == 0, stop=True, skip_group_check=True)
                    mm.then_inc(S["tk_scored"], 1)
            pe.wait_ge(S["tk_gate"], 4)
            for t in range(5):
                n = rows(t)
                if t >= 2:
                    pe.wait_ge(S["tk_out"], t - 1)
                for a in range(3):
                    mm = pe.transpose(acc[t % 2][:, 0, a * P:a * P + n], OUT[0:n, a, t].rearrange("p h k -> p (h k)"), ident[0:n, 0:n])
                mm.then_inc(S["tk_turned"], 1)

        @block.scalar
        def _(act):
            act.sem_inc(S["tk_q"], 2)
            act.sem_inc(S["tk_scores"], 2)
            W.split_hi(act, 0)
            W.split_hi(act, 1)
            act.wait_ge(S["tk_set"], 3)

            def head(i, last):
                for u in range(N):
                    act.wait_ge(W.used, N * i + u + 3)
                    act.activation(halves(QT[:, u, :]), acc[u][:, :, 0:H2], ACT.Copy).then_inc(S["tk_q"], 1)
                    if not last:
                        W.split_hi(act, u + 2, N, i)
                for u, ps in enumerate((psS, psR)):
                    act.wait_ge(S["tk_scored"], N * i + u + 1)
                    act.wait_ge(S["tk_head"], i + 1)
                    act.activation(SC[:, 0, 0:4, u, :], ps[:, 0, :].rearrange("p (t n) -> p t n", t=4), ACT.Copy)
                    act.activation(SC[0:DEC, 0, 4, u, :], ps[0:DEC, 1, 0:P], ACT.Copy).then_inc(S["tk_scores"], 1)
            with act.Fori(0, PH - 1) as i:
                head(i, False)
            head(PH - 1, True)
            act.wait_ge(S["tk_gate"], 1)
            best = OUT[:, 2].rearrange("p t h k -> p (t h k)")
            act.activation(best, best, ACT.Exp).then_inc(S["tk_exp"], 1)
            for t in range(5):
                n = rows(t)
                act.wait_ge(S["tk_turned"], t + 1)
                act.activation(IT[:, :, t * P:t * P + n], acc[t % 2][:, 0, 0:3 * P].rearrange("p (a n) -> p a n", a=3)[:, :, 0:n],
                               ACT.Copy).then_inc(S["tk_out"], 1)

        @block.vector
        def _(dve):
            dve.memset(SC[:, 0, 4], 0.0).then_inc(S["tk_set"], 1)
            dve.memset(V[:, 4], 0.0).then_inc(S["tk_set"], 1)
            dve.memset(I[:, 4], 0).then_inc(S["tk_set"], 1)
            dve.memset(POS[:, 4], 0).then_inc(S["tk_set"], 1)
            dve.memset(TOP[:, 4], 0.0).then_inc(S["tk_set"], 1)
            dve.sem_inc(S["tk_head"], 1)
            dve.wait_ge(S["tk_set"], 5)
            dve.wait_ge(S["tk_cst"], 48)

            with dve.Fori(0, PH) as i:
                dve.wait_ge(S["tk_scores"], N * i + 4)
                ch = Chain(dve, S["tk_chain"], 13, i)

                def best16(values, rest, top, index, where):
                    stage = [lambda w: dve.max(top(w, 0), values(w)),
                             lambda w: dve.match_replace(rest(w), top(w, 0), values(w), LOW),
                             lambda w: dve.max(top(w, 1), rest(w)),
                             lambda w: dve.max_index(index(w, 0), top(w, 0), values(w)),
                             lambda w: dve.max_index(index(w, 1), top(w, 1), rest(w))]
                    for n, f in enumerate(stage):
                        dve.sem_inc(S["tk_passed"], 1)
                        for w in where[:-1]:
                            f(w)
                        ch(f(where[-1]), wait=n != 3)
                where = [(t, u) for t in range(5) for u in range(2)]
                eight = lambda n: slice(8 * n, 8 * n + 8)
                best16(lambda w: SC[0:rows(w[0]), 0, w[0], w[1], :], lambda w: SC2[0:rows(w[0]), w[0], w[1], :],
                       lambda w, n: V[0:rows(w[0]), w[0], w[1], eight(n)], lambda w, n: I[0:rows(w[0]), w[0], w[1], eight(n)], where)
                dve.sem_inc(S["tk_head"], 1)
                ca = CA.rearrange("p t (a b) -> p t a b", a=TOPK)
                four = [P, 5, TOPK, TOPK]
                for t in range(5):
                    n = rows(t)
                    add = dve.tensor_tensor(ca[0:n, t], V[0:n, t, 0, :].unsqueeze(2).to_broadcast([n, TOPK, TOPK]),
                                            V[0:n, t, 1, :].unsqueeze(1).to_broadcast([n, TOPK, TOPK]), ALU.add)
                ch(add)
                best = lambda t, n: TOP[0:rows(t), t, eight(n)]
                best16(lambda t: CA[0:rows(t), t, :], lambda t: CA2[0:rows(t), t, :], best,
                       lambda t, n: POS[0:rows(t), t, eight(n)], list(range(5)))
                dve.tensor_scalar(PH2[:, :, 0, :], POS[:, :, :], 4, None, ALU.logical_shift_right)
                dve.tensor_scalar(PH2[:, :, 1, :], POS[:, :, :], 15, None, ALU.bitwise_and)
                dve.tensor_copy(OUT[:, 2, :, bass.ds(i, 1), :].rearrange("p t a k -> p t (a k)"), TOP[:, :, :])
                ch(dve.tensor_copy(IF[:, :, :, :], I[:, :, :, :]))
                ch(dve.tensor_copy(PHF[:, :, :, :], PH2[:, :, :, :]))
                row = iota[:, 0:TOPK].unsqueeze(1).to_broadcast([P, TOPK, TOPK])
                for u, o in ((0, CA), (1, CA2)):
                    for t in range(5):
                        o3 = o[:, t, :].rearrange("p (k a) -> p k a", a=TOPK)
                        eq = dve.tensor_tensor(o3, PHF[:, t, u, :].unsqueeze(2).to_broadcast([P, TOPK, TOPK]), row, ALU.is_equal)
                eq.then_inc(S["tk_eq"], 1)
                dve.wait_ge(S["tk_eq"], 3 * i + 1)
                for u, o in ((0, CA), (1, CA2)):
                    for t in range(5):
                        o3 = o[:, t, :].rearrange("p (k a) -> p k a", a=TOPK)
                        pick = dve.tensor_tensor(o3, o3, IF[:, t, u, :].unsqueeze(1).to_broadcast([P, TOPK, TOPK]), ALU.mult)
                pick.then_inc(S["tk_eq"], 1)
                dve.wait_ge(S["tk_eq"], 3 * i + 2)
                for u, o in ((0, CA), (1, CA2)):
                    got = dve.tensor_reduce(OUT[:, u, :, bass.ds(i, 1), :].rearrange("p t a k -> p t (a k)"),
                                            o.rearrange("p t (k a) -> p t k a", a=TOPK), AX_X, ALU.add)
                got.then_inc(S["tk_eq"], 1)
                dve.wait_ge(S["tk_eq"], 3 * i + 3)
                ch.end()
            g = OUT[:, 2].rearrange("p t h k -> p (t h) k")
            flat = [P, 5 * PH, TOPK]
            total = SUM.rearrange("p t h -> p (t h)")
            dve.tensor_copy(total, g[:, :, 0]).then_inc(S["tk_top"], 1)
            dve.wait_ge(S["tk_top"], 1)
            dve.tensor_tensor(g, g, total.unsqueeze(2).to_broadcast(flat), ALU.subtract).then_inc(S["tk_gate"], 1)
            dve.wait_ge(S["tk_exp"], 1)
            dve.tensor_reduce(total, g, AX_X, ALU.add).then_inc(S["tk_gate"], 1)
            dve.wait_ge(S["tk_gate"], 2)
            dve.reciprocal(total, total).then_inc(S["tk_gate"], 1)
            dve.wait_ge(S["tk_gate"], 3)
            dve.tensor_tensor(g, g, total.unsqueeze(2).to_broadcast(flat), ALU.mult).then_inc(S["tk_gate"], 1)


GB_T = 68
GB_N = T // GB_T


def gate_matrix(nc, S, A, banks, IT, g_d):
    with ExitStack() as ctx:
        sb = lambda n, s, d=F32: ctx.enter_context(nc.sbuf_tensor(n, s, d))
        iota = sb("gm_iota", [P, P])
        ONE = sb("ONE", [P, 4, 4, 2, P])
        STG = sb("STG", [P, NK, GB_T])
        QUADS = GB_T // 4
        block = ctx.enter_context(nc.Block())

        @block.sync
        def _(sp):
            sp.dma_start(iota[:, :], A["cst"][:, CST_AT["iota"][0]:CST_AT["iota"][0] + P]).then_inc(S["gm_cst"], 16)
            with sp.Fori(0, GB_N) as i:
                sp.wait_ge(S["gm_evac"], QUADS * i + QUADS + 8)
                sp.dma_start(g_d[bass.ds(i, 1)].rearrange("a p n t -> (a p) (n t)"), STG.rearrange("p n t -> p (n t)")).then_inc(S["gm_stored"], 16)
            sp.wait_ge(S["gm_stored"], 16 * GB_N + 16)

        @block.vector
        def _(dve):
            dve.wait_ge(S["gm_cst"], 16)
            with dve.Fori(0, GB_N) as i:
                for q in range(QUADS):
                    dve.wait_ge(S["gm_summed"], QUADS * i + (q + 1 if q >= 4 else q or 4))
                    for j in range(4):
                        tok = bass.ds(GB_T * i + 4 * q + j, 1)
                        dve.tensor_scalar(ONE[:, q % 4, j, 0, :], iota[:, :], IT[:, 0, tok], IT[:, 2, tok], ALU.is_equal, ALU.mult)
                        one = dve.tensor_scalar(ONE[:, q % 4, j, 1, :], iota[:, :], IT[:, 1, tok], None, ALU.is_equal)
                    one.then_inc(S["gm_onehot"], 1)

        @block.tensor
        def _(pe):
            pe.sem_inc(S["gm_summed"], 4)
            with pe.Fori(0, GB_N) as i:
                for q in range(QUADS):
                    pe.wait_ge(S["gm_onehot"], QUADS * i + q + 1)
                    pe.wait_ge(S["gm_evac"], QUADS * i + (q + 1 if q >= 8 else q or 8))
                    for j in range(4):
                        mm = pe.matmul(banks[q % 8][:, j * P:(j + 1) * P], ONE[:, q % 4, j, 1, :], ONE[:, q % 4, j, 0, :], start=True, stop=True)
                    mm.then_inc(S["gm_summed"], 1)

        @block.scalar
        def _(act):
            act.sem_inc(S["gm_stored"], 16)
            act.sem_inc(S["gm_evac"], 8)
            with act.Fori(0, GB_N) as i:
                act.wait_ge(S["gm_stored"], 16 * i + 16)
                for q in range(QUADS):
                    act.wait_ge(S["gm_summed"], QUADS * i + q + 5)
                    act.activation(STG[:, :, 4 * q:4 * q + 4], banks[q % 8].rearrange("p (t n) -> p n t", t=4), ACT.Copy).then_inc(S["gm_evac"], 1)


def experts(nc, S, A, acc, psS, psR, H, hh, hl, g_d):
    with ExitStack() as ctx:
        sb = lambda n, s, d=F32: ctx.enter_context(nc.sbuf_tensor(n, s, d))
        raw, whi, wlo = sb("raw_e", [P, 2, D]), sb("whi_e", [P, 2, D], F32R), sb("wlo_e", [P, 2, D], F32R)
        G = sb("Ge", [P, 2, GB_N, 2, GB_T])
        GE, CX = sb("GE", [P, 2, T]), sb("CX", [P, 2, T])
        chi, clo = sb("chi", [P, 2, 2, T], F32R), sb("clo", [P, 2, 2, T], F32R)
        W = Stream("ex", S, raw, whi, wlo)
        GROUPS = NK // 2
        N = 8
        U = lambda k: A["u"][k]
        v_rows = A["v"].rearrange("(g k p) (h n) -> g h p k n", k=2, p=P, h=2)
        halves = lambda t: t.rearrange("p (h t) -> p h t", h=2)
        vps = [psS, psR]
        block = ctx.enter_context(nc.Block())
        ITER = GROUPS // 2 - 1

        @block.sync
        def _(sp):
            def u_unit(c, i, k, group):
                src = A["u"][bass.ds(k, 1)].rearrange("a p n -> (a p) n") if not isinstance(k, int) else A["u"][k]
                W.load(sp, src, c, N, i)

            def v_unit(c, i, group, half):
                src = v_rows[bass.ds(group, 1), half].rearrange("g p k n -> (g p) k n") if not isinstance(group, int) else v_rows[group, half]
                sp.wait_ge(W.split_done, N * i + c + 1)
                sp.dma_start(raw[:, c % 2, :].rearrange("p (k n) -> p k n", k=2), src).then_inc(W.loaded[c % 2], 16)

            def gates(group, slot, count):
                sp.wait_ge(S["ex_coef"], count)
                src = g_d.rearrange("b p n t -> p b n t")
                if isinstance(group, int):
                    a = src[:, :, 2 * group:2 * group + 2, :]
                else:
                    a = src[:, :, bass.ds(2 * group, 2), :]
                sp.dma_start(G[:, slot].rearrange("p b n t -> p b (n t)"), a.rearrange("p b n t -> p b (n t)")).then_inc(S[f"ex_gates{slot}"], 16)

            W.load(sp, A["u"][0], 0)
            W.load(sp, A["u"][1], 1)
            gates(0, 0, 1)

            def groups(i, part=2):
                gates(2 * i + 1, 1, 4 * i + 2)
                u_unit(2, i, 4 * i + 2, 0)
                u_unit(3, i, 4 * i + 3, 0)
                v_unit(4, i, 2 * i, 0)
                v_unit(5, i, 2 * i, 1)
                if part == 2:
                    gates(2 * i + 2, 0, 4 * i + 4)
                    u_unit(6, i, 4 * i + 4, 0)
                    u_unit(7, i, 4 * i + 5, 0)
                    v_unit(8, i, 2 * i + 1, 0)
                    v_unit(9, i, 2 * i + 1, 1)
                else:
                    v_unit(6, i, 2 * i + 1, 0)
                    v_unit(7, i, 2 * i + 1, 1)
            with sp.Fori(0, ITER) as i:
                groups(i)
            groups(ITER, 1)

        @block.gpsimd
        def _(pool):
            W.start_pool(pool)
            W.split_lo(pool, 0)
            W.split_lo(pool, 1)
            with pool.Fori(0, ITER) as i:
                for c in range(2, 2 + N):
                    W.split_lo(pool, c, N, i)
            for c in range(2, 8):
                W.split_lo(pool, c, N, ITER)

        @block.tensor
        def _(pe):
            W.start_pe(pe)

            def u_products(c, i, count):
                pe.wait_ge(S["ex_gelu"], count + 1)
                for mm in unit_product(pe, W, c, acc[c % 2], hh, hl, N, i):
                    pass
                mm.then_inc(W.used, 1)

            def v_products(c, i, par, half, group):
                W.ready(pe, c, N, i)
                if half == 0:
                    pe.wait_ge(S["ex_coef"], 2 * group + 4)
                for d in range(8):
                    n = 16 * group + 8 * half + d
                    pe.wait_ge(S["ex_added"], n + 1)
                    w = lambda t: lambda k: t[:, c % 2, k * 1024 + d * P:k * 1024 + (d + 1) * P]
                    x = lambda t: lambda k, h: t[:, par, k, h * H2:(h + 1) * H2]
                    for mm in product(pe, vps[d % 2], w(whi), w(wlo), x(chi), x(clo), 2):
                        pass
                    if d < 7:
                        mm.then_inc(S["ex_v"], 1)
                mm.then_inc(W.used, 1)

            u_products(0, 0, 0)
            u_products(1, 0, 1)

            def groups(i, part=2):
                u_products(2, i, 4 * i + 2)
                u_products(3, i, 4 * i + 3)
                v_products(4, i, 0, 0, 2 * i)
                v_products(5, i, 0, 1, 2 * i)
                if part == 2:
                    u_products(6, i, 4 * i + 4)
                    u_products(7, i, 4 * i + 5)
                c = 8 if part == 2 else 6
                v_products(c, i, 1, 0, 2 * i + 1)
                v_products(c + 1, i, 1, 1, 2 * i + 1)
            with pe.Fori(0, ITER) as i:
                groups(i)
            groups(ITER, 1)

        @block.scalar
        def _(act):
            act.sem_inc(S["ex_gelu"], 2)

            def gelu(c, i, count):
                act.wait_ge(W.used, N * i + c + 3)
                act.wait_ge(S["ex_coef"], count + 1)
                act.activation(halves(GE[:, c % 2, :]), acc[c % 2][:, :, 0:H2], ACT.Gelu).then_inc(S["ex_gelu"], 1)

            W.split_hi(act, 0)
            W.split_hi(act, 1)
            gelu(0, 0, 0)
            W.split_hi(act, 2)
            gelu(1, 0, 1)

            def groups(i, part=2):
                W.split_hi(act, 3, N, i)
                gelu(2, i, 4 * i + 2)
                W.split_hi(act, 4, N, i)
                gelu(3, i, 4 * i + 3)
                W.split_hi(act, 5, N, i)
                W.split_hi(act, 6, N, i)
                W.split_hi(act, 7, N, i)
                if part == 2:
                    gelu(6, i, 4 * i + 4)
                    W.split_hi(act, 8, N, i)
                    gelu(7, i, 4 * i + 5)
                    W.split_hi(act, 9, N, i)
                    W.split_hi(act, 10, N, i)
            with act.Fori(0, ITER) as i:
                groups(i)
            groups(ITER, 1)

        @block.vector
        def _(dve):
            dve.sem_inc(S["ex_coef"], 2)
            dve.sem_inc(S["ex_added"], 2)

            def coefficients(par, k, slot, count):
                dve.wait_ge(S["ex_gelu"], count + 3)
                tok = lambda t: t.rearrange("p (b t) -> p b t", b=GB_N)
                dve.tensor_tensor(tok(CX[:, k, :]), tok(GE[:, k, :]), G[:, slot, :, k, :], ALU.mult).then_inc(S["ex_prod"], 1)
                dve.wait_ge(S["ex_prod"], 2 * count + 1)
                dve.tensor_copy(chi[:, par, k, :], CX[:, k, :]).then_inc(S["ex_prod"], 1)
                dve.wait_ge(S["ex_prod"], 2 * count + 2)
                dve.tensor_tensor(clo[:, par, k, :], CX[:, k, :], chi[:, par, k, :].bitcast(F32), ALU.subtract).then_inc(S["ex_coef"], 1)

            def add(half, c, i, group):
                for d in range(8):
                    n = 14 * group + 7 * half + d + 1
                    if d < 7:
                        dve.wait_ge(S["ex_v"], n)
                    else:
                        dve.wait_ge(W.used, N * i + c + 3)
                    h = halves(H[:, 8 * half + d, :])
                    dve.tensor_tensor(h, vps[d % 2][:, :, 0:H2], h, ALU.add).then_inc(S["ex_added"], 1)

            dve.wait_ge(S["ex_gates0"], 16)
            coefficients(0, 0, 0, 0)
            coefficients(0, 1, 0, 1)

            def groups(i, part=2):
                dve.wait_ge(S["ex_gates1"], 16 * i + 16)
                coefficients(1, 0, 1, 4 * i + 2)
                coefficients(1, 1, 1, 4 * i + 3)
                add(0, 4, i, 2 * i)
                add(1, 5, i, 2 * i)
                if part == 2:
                    dve.wait_ge(S["ex_gates0"], 16 * i + 32)
                    coefficients(0, 0, 0, 4 * i + 4)
                    coefficients(0, 1, 0, 4 * i + 5)
                c = 8 if part == 2 else 6
                add(0, c, i, 2 * i + 1)
                add(1, c + 1, i, 2 * i + 1)
            with dve.Fori(0, ITER) as i:
                groups(i)
            groups(ITER, 1)


def layout(x):
    c = np.ascontiguousarray
    f = lambda a: np.asarray(a)
    def blocks(w):
        k, n = w.shape
        return c(w.reshape(k // P, P, n // P, P).transpose(2, 1, 0, 3).reshape(n // P, P, k))
    def cols(v):
        return v.reshape(-1, P).T
    A = {}
    xall = np.concatenate([f(x["x_prompt"])[0], f(x["x_sample"])[0]], axis=0)
    A["xT"] = c(xall.T.reshape(KB, P, T).transpose(1, 0, 2))
    A["w_in"] = blocks(f(x["w_in"])[0])
    A["ckT"] = c(f(x["cache_sb_k"])[0, 0].transpose(1, 2, 0))
    A["cv"] = c(f(x["cache_sb_v"])[0, 0].reshape(4, P, HEADS, P).transpose(2, 1, 0, 3))
    w2a2 = np.concatenate([f(x["rw_w2"])[0], f(x["rw_a2"])[0]], axis=0)
    A["lora"] = c(np.stack([w2a2, f(x["rw_g2"])[0]], axis=1).reshape(P, 2, PAIRS, P).transpose(2, 0, 1, 3))
    A["s0T"] = c(f(x["state_rwkv_wkv"])[0, 0].transpose(0, 2, 1).reshape(PAIRS, P, CH))
    mu = f(x["rw_mu"])[0]
    per = {"mu_r": mu[0:RW], "mu_k": mu[RW:2 * RW], "mu_v": mu[2 * RW:3 * RW], "w0": x["rw_w0"][0],
           "a0": x["rw_a0"][0], "k_k": x["rw_k_k"][0], "k_a": x["rw_k_a"][0],
           "r_k": f(x["rw_r_k"])[0].reshape(-1), "ln_g": x["rw_ln_g"][0], "ln_b": x["rw_ln_b"][0]}
    pairs = np.stack([cols(f(per[n])) for n in PAR], axis=2).reshape(P, PAIRS * NPAR)
    A["par"] = c(np.concatenate([pairs, cols(mu[3 * RW:]), cols(f(x["norm1_g"])[0]), cols(f(x["norm2_g"])[0]),
                                 cols(f(x["final_norm_g"])), cols(f(x["state_rwkv_shift"])[0, 0, 0])], axis=1))
    sbw, rww = blocks(f(x["w_branch_sb"])[0]), blocks(f(x["w_branch_rw"])[0])
    A["w_br"] = c(np.concatenate([sbw, rww], axis=2))
    A["w_out"] = blocks(f(x["w_out"])[0])
    A["w_q"] = blocks(f(x["peer_wq"])[0])
    A["keys"] = c(np.stack([f(x["peer_k1"])[0].T, f(x["peer_k2"])[0].T], axis=1))
    A["u"] = blocks(f(x["peer_u"])[0].T)
    A["v"] = c(f(x["peer_v"])[0])
    A["cst"] = c(np.concatenate([*constants().values()], axis=1))
    return A


OUTS = {"kT": (HEADS, P, T), "vT": (HEADS, P, T), "wkvp": (PAIRS, P, CH), "wkvs": (PAIRS, P, CH), "shift": (P, 26, 2), "yT": (P, KB, T)}


def kernel(**inputs):
    import concourse.bacc as _bacc
    from concourse.bass_utils import run_bass_kernel_spmd as _run

    arrays = layout({k: np.asarray(v) for k, v in inputs.items()})
    nc = _bacc.Bacc("TRN2", target_bir_lowering=False, num_devices=1)
    A = {n: nc.dram_tensor("in_" + n, a.shape, F32, kind="ExternalInput").ap() for n, a in arrays.items()}
    O = {n: nc.dram_tensor("out_" + n, s, F32, kind="ExternalOutput").ap() for n, s in OUTS.items()}
    build(nc, A, O)
    r = _run(nc, [{"in_" + n: a for n, a in arrays.items()}], core_ids=[0]).results[0]
    y = r["out_yT"].transpose(2, 1, 0).reshape(T, D)
    k, v = (r[n].transpose(2, 0, 1) for n in ("out_kT", "out_vT"))
    wkv = [r[n].reshape(PAIRS * 2, CH, CH).transpose(0, 2, 1)[None, None] for n in ("out_wkvp", "out_wkvs")]
    shift = [r["out_shift"][:, :, n].T.reshape(1, 1, 1, -1) for n in range(2)]
    c = np.ascontiguousarray
    return (c(y[None, :SEQ]), c(y[None, SEQ:]), c(k[None, None, :SEQ]), c(v[None, None, :SEQ]), c(wkv[0]), c(shift[0]),
            c(k[None, None, SEQ:]), c(v[None, None, SEQ:]), c(wkv[1]), c(shift[1]))
```

```python
from contextlib import ExitStack

import numpy as np
import concourse.bass as bass
from concourse import mybir

F32 = mybir.dt.float32
F32R = mybir.dt.float32r
U32 = mybir.dt.uint32
I32 = mybir.dt.int32
ACT = mybir.ActivationFunctionType
ALU = mybir.AluOpType
AX_X = mybir.AxisListType.X

P = 128
D = 2048
KB = D // P
SEQ, DEC, PAST = 512, 32, 512
T = SEQ + DEC
H2 = T // 2
HEADS = 8
RW = 1024
PAIRS = RW // P
CH = 64
CHUNKS = SEQ // CH
E = T + 2
EH = E // 2
S0 = SEQ + 1
SM_SCALE = P ** -0.5
KAPPA = float(np.exp(-0.5))
RMS_EPS, GN_EPS = 1e-6, 64e-5
PH, NK, TOPK = 8, 128, 16
NEXP = NK * NK

PAR = ["mu_r", "mu_k", "mu_v", "w0", "a0", "k_k", "k_a", "r_k", "ln_g", "ln_b"]
NPAR = len(PAR)
C_MUWA, C_MUG = PAIRS * NPAR, PAIRS * NPAR + 1
C_N1, C_N2, C_NF = C_MUG + 1, C_MUG + 1 + KB, C_MUG + 1 + 2 * KB
C_SHIFT = C_NF + KB
NCOL = C_SHIFT + 26

ZCOL = {3: 0, 1: 128, 2: 512, 0: 928}
ZS = 768
ZN = 1440

LEVELS = [2, 4, 8, 16, 32]


def constants():
    r, c = np.arange(P)[:, None], np.arange(P)[None, :]
    p, q = r % CH, np.arange(CH)[None, :]
    block = lambda m: (p // (2 * m) == q // (2 * m)) & (q // m % 2 == 1) & (p // m % 2 == 0)
    out = {
        "ident": r == c,
        "ones": np.ones((P, P)),
        "headones": r // CH == c // CH,
        "negtri": -1.0 * (r >= c),
        "negones": -np.ones((P, P)),
        "before": r < c,
        "chunk": np.concatenate([p < q, p <= q, -1.0 * ((p // 2 == q // 2) & (p > q)), -1.0 * block(1), p == q,
                                 *[block(m) for m in LEVELS]], axis=1),
    }
    out["iota"] = np.broadcast_to(c, (P, P))
    scan = np.ones((P, E))
    scan[:, [*range(0, SEQ, CH), SEQ, S0, E - 1]] = 0.0
    out["scan"] = scan
    return {k: np.asarray(v, np.float32) for k, v in out.items()}


CST_AT = {}
_n = 0
for _k, _v in constants().items():
    CST_AT[_k] = (_n, _v.shape[1])
    _n += _v.shape[1]
NCST = _n


class Sems:

    def __init__(self, nc, ctx):
        self.nc, self.ctx, self.known = nc, ctx, {}

    def __getitem__(self, name):
        if name not in self.known:
            self.known[name] = self.ctx.enter_context(self.nc.semaphore(name))
        return self.known[name]


class Chain:

    def __init__(self, eng, sem, steps, i, credit=0):
        self.credit = credit
        self.eng, self.sem, self.steps, self.i, self.k = eng, sem, steps, i, 0

    def __call__(self, instruction, wait=True):
        self.k += 1
        assert self.k <= self.steps, "more steps than counted"
        instruction.then_inc(self.sem, 1)
        if wait:
            self.eng.wait_ge(self.sem, self.i * self.steps + self.k + self.credit)

    def end(self):
        assert self.k == self.steps, (self.k, self.steps)


class Stream:

    def __init__(self, S, raw, hi, lo, base=0):
        self.S, self.raw, self.hi, self.lo, self.base = S, raw, hi, lo, base
        self.loaded = [S["w_loaded0"], S["w_loaded1"]]
        self.hi_done, self.split_done, self.used = S["w_hi"], S["w_split"], S["w_used"]

    def phase(self, base):
        return Stream(self.S, self.raw, self.hi, self.lo, base)

    def start_pool(self, pool):
        pool.sem_inc(self.split_done, 2)

    def start_pe(self, pe):
        pe.sem_inc(self.used, 2)

    def load(self, sp, src, c, per=0, i=0):
        sp.wait_ge(self.split_done, per * i + self.base + c + 1)
        raw = self.raw[:, c % 2, :]
        if len(src.shape) == 3:
            raw = raw.rearrange("p (k n) -> p k n", k=src.shape[1])
        sp.dma_start(raw, src).then_inc(self.loaded[c % 2], 16)

    def split_hi(self, act, c, per=0, i=0):
        act.wait_ge(self.loaded[c % 2], per * 8 * i + 16 * ((self.base + c) // 2 + 1))
        act.wait_ge(self.used, per * i + self.base + c + 1)
        act.activation(self.hi[:, c % 2, :], self.raw[:, c % 2, :], ACT.Copy).then_inc(self.hi_done, 1)

    def split_lo(self, pool, c, per=0, i=0):
        pool.wait_ge(self.hi_done, per * i + self.base + c + 1)
        pool.tensor_tensor(self.lo[:, c % 2, :], self.raw[:, c % 2, :], self.hi[:, c % 2, :].bitcast(F32),
                           ALU.subtract).then_inc(self.split_done, 1)

    def ready(self, pe, c, per=0, i=0):
        pe.wait_ge(self.split_done, per * i + self.base + c + 3)

    def wait_used(self, eng, c, per=0, i=0):
        eng.wait_ge(self.used, per * i + self.base + c + 3)


def product(pe, out, w_hi, w_lo, x_hi, x_lo, blocks, first=True, last=True):
    for k in range(blocks):
        for w, x in ((w_hi, x_hi), (w_hi, x_lo), (w_lo, x_hi)):
            for half in range(2):
                a = first and k == 0 and w is w_hi and x is x_hi
                z = last and k == blocks - 1 and w is w_lo
                mm = pe.matmul(out[:, half, 0:H2], w(k), x(k, half), start=a, stop=z)
        yield mm


def v_rows(A):
    return A["v"].rearrange("(g k p) (h n) -> g h p k n", k=2, p=P, h=2)


def build(nc, A, O):
    ctx = ExitStack()
    with ctx:
        S = Sems(nc, ctx)
        dram = lambda n, s: nc.dram_tensor(n, s, F32, kind="Internal").ap()
        gates_d = dram("gates_d", (2 * KB, P, T))
        o_d = dram("o_d", (KB, P, T))
        h_d = dram("h_d", (KB, P, T))
        g_d = dram("g_d", (GB_N, P, NK, GB_T))
        pre_d = dram("pre_d", (PRE, P, T))

        acc = [ctx.enter_context(nc.psum_tensor(f"acc{b}", [P, 2, 512], F32)) for b in range(2)]
        psS = ctx.enter_context(nc.psum_tensor("psS", [P, 2, 512], F32))
        psR = ctx.enter_context(nc.psum_tensor("psR", [P, 2, 512], F32))
        sball = lambda n, s, d=F32: ctx.enter_context(nc.sbuf_tensor(n, s, d))
        par = sball("par", [P, NCOL])
        eps = sball("eps", [P, 2])
        W = Stream(S, sball("raw", [P, 2, D]), sball("whi", [P, 2, D], F32R), sball("wlo", [P, 2, D], F32R))
        counts = {"attention": 4 * HEADS, "rwkv": 6 * PAIRS + 2, "mix": KB, "out": KB, "retrieval": 2 * PH + TAIL, "gates": PRE - TAIL}
        base, at = {}, 0
        for name, count in counts.items():
            base[name], at = at, at + count
        base["experts"] = at

        with ExitStack() as front:
            sbf = lambda n, s, d=F32: front.enter_context(nc.sbuf_tensor(n, s, d))
            xh = sbf("xh", [P, KB, T], F32R)
            xl = sbf("xl", [P, KB, T], F32R)
            with ExitStack() as ctx1:
                X = ctx1.enter_context(nc.sbuf_tensor("X", [P, KB, T], F32))
                norm(nc, S, "n1", A, par, eps, psS, X, C_N1, src=lambda a, b: A["xT"][:, a:b, :], hi=xh, lo=xl, W=W,
                     ahead=[A["w_in"][0], A["w_in"][8]])
            attention(nc, S, A, O, W.phase(0), [A["w_in"][48], A["w_in"][49]], acc, psS, psR, xh, xl, gates_d, o_d)
            rwkv(nc, S, A, O, W.phase(base["rwkv"]), [A["w_br"][0], A["w_br"][1]], acc, psS, psR, xh, xl, par, eps, gates_d, o_d)

        with ExitStack() as back:
            sbk = lambda n, s, d=F32: back.enter_context(nc.sbuf_tensor(n, s, d))
            hh, hl = sbk("hh", [P, KB, T], F32R), sbk("hl", [P, KB, T], F32R)
            load_h = lambda a, b: h_d[a:b].rearrange("k p t -> p k t")
            mix(nc, S, A, W.phase(base["mix"]), [A["w_out"][0], A["w_out"][1]], acc, psS, psR, hh, hl, gates_d, o_d)
            with ExitStack() as ctx2:
                X = ctx2.enter_context(nc.sbuf_tensor("X2", [P, KB, T], F32))
                out_projection(nc, S, A, W.phase(base["out"]), [A["w_q"][0], A["w_q"][1]], acc, psS, hh, hl, X)
                norm(nc, S, "n2", A, par, eps, psS, X, C_N2, hi=hh, lo=hl, keep=load_h)
            with ExitStack() as picks:
                IT = picks.enter_context(nc.sbuf_tensor("IT", [P, 3, T], F32))
                retrieval(nc, S, A, W.phase(base["retrieval"]), [A["u"][TAIL], A["u"][TAIL + 1]], acc, psS, psR, hh, hl, IT, pre_d)
                gate_matrix(nc, S, A, W.phase(base["gates"]), [v_rows(A)[0, 0], v_rows(A)[0, 1]], acc, psS, psR, hh, hl, IT, g_d, pre_d)
            H = sbk("H", [P, KB, T])
            experts(nc, S, A, W.phase(base["experts"]), acc, psS, psR, H, load_h, hh, hl, g_d, pre_d)
            norm(nc, S, "nf", A, par, eps, psS, H, C_NF, out=O["yT"])


def norm(nc, S, tag, A, par, eps, ps, X, gain, src=None, hi=None, lo=None, out=None, W=None, ahead=(), keep=None):
    with ExitStack() as ctx:
        sb = lambda n, s, d=F32: ctx.enter_context(nc.sbuf_tensor(tag + n, s, d))
        SQ, RS, XT, ones = sb("SQ", [P, 2, T]), sb("RS", [P, T]), sb("XT", [P, 4, T]), sb("ones", [P, P])
        sem = lambda n: S[tag + n]
        block = ctx.enter_context(nc.Block())

        @block.sync
        def _(sp):
            if src is not None:
                for q in range(4):
                    sp.dma_start(X[:, 4 * q:4 * q + 4, :], src(4 * q, 4 * q + 4)).then_inc(sem(f"loaded{q}"), 16)
            if tag == "n1":
                sp.dma_start(par[:, :], A["par"]).then_inc(sem("par"), 16)
            for c, unit in enumerate(ahead):
                W.load(sp, unit, c)
            if keep is not None:
                for q in range(4):
                    sp.dma_start(keep(4 * q, 4 * q + 4), X[:, 4 * q:4 * q + 4, :]).then_inc(sem("kept"), 16)
                sp.wait_ge(sem("kept"), 64)
            if out is not None:
                for k in range(KB):
                    sp.wait_ge(sem("scaled"), k + 2)
                    sp.dma_start(out[:, k, :], XT[:, k % 4, :]).then_inc(sem(f"stored{k % 4}"), 16)
                for b in range(4):
                    sp.wait_ge(sem(f"stored{b}"), 16 * KB // 4)

        @block.scalar
        def _(act):
            for k in range(0 if keep is not None else KB):
                if src is not None and k % 4 == 0:
                    act.wait_ge(sem(f"loaded{k // 4}"), 16)
                if k >= 2:
                    act.wait_ge(sem("summed"), k - 1)
                act.activation(SQ[:, k % 2, :], X[:, k, :], ACT.Square).then_inc(sem("square"), 1)
            if keep is None:
                act.wait_ge(sem("summed"), KB)
            act.wait_ge(sem("set"), 3 if tag == "n1" else 1)
            act.activation(RS[:, :].rearrange("p (h t) -> p h t", h=2), ps[:, :, 0:H2], ACT.Sqrt,
                           bias=eps[:, 0:1], scale=1.0 / D).then_inc(sem("square"), 1)
            for c in range(len(ahead)):
                W.split_hi(act, c)
            if hi is not None:
                for k in range(KB):
                    act.wait_ge(sem("scaled"), k + 2)
                    act.activation(hi[:, k, :], XT[:, k % 4, :], ACT.Copy).then_inc(sem("hi"), 1)

        def split_lo(eng, k):
            eng.wait_ge(sem("hi"), k + 1)
            eng.tensor_tensor(lo[:, k, :], XT[:, k % 4, :], hi[:, k, :].bitcast(F32), ALU.subtract).then_inc(sem(f"lo{k % 2}"), 1)

        @block.gpsimd
        def _(pool):
            if ahead:
                W.start_pool(pool)
                for c in range(len(ahead)):
                    W.split_lo(pool, c)
            if hi is not None:
                for k in range(1, KB, 2):
                    pool.wait_ge(sem("scaled"), k + 2)
                    split_lo(pool, k)

        @block.tensor
        def _(pe):
            if ahead:
                W.start_pe(pe)
            pe.wait_ge(sem("set"), 3 if tag == "n1" else 1)
            for k in range(0 if keep is not None else KB):
                pe.wait_ge(sem("square"), k + 1)
                for half in range(2):
                    mm = pe.matmul(ps[:, half, 0:H2], ones[:, :], SQ[:, k % 2, half * H2:(half + 1) * H2],
                                   start=k == 0, stop=k == KB - 1)
                mm.then_inc(sem("summed"), 1)

        @block.vector
        def _(dve):
            if tag == "n1":
                dve.memset(eps[:, 0:1], RMS_EPS).then_inc(sem("set"), 1)
                dve.memset(eps[:, 1:2], GN_EPS).then_inc(sem("set"), 1)
            dve.memset(ones[:, :], 1.0).then_inc(sem("set"), 1)
            if tag == "n1":
                dve.wait_ge(sem("par"), 16)
            dve.wait_ge(sem("square"), 1 if keep is not None else KB + 1)
            dve.reciprocal(RS[:, :], RS[:, :]).then_inc(sem("scaled"), 1)
            dve.wait_ge(sem("scaled"), 1)
            for k in range(KB + 2):
                if k < KB:
                    if k >= 4 and hi is not None:
                        dve.wait_ge(sem(f"lo{k % 2}"), (k - 4) // 2 + 1)
                    if k >= 4 and out is not None:
                        dve.wait_ge(sem(f"stored{k % 4}"), 16 * (k // 4))
                    dve.scalar_tensor_tensor(XT[:, k % 4, :], X[:, k, :], par[:, gain + k:gain + k + 1], RS[:, :],
                                             ALU.mult, ALU.mult).then_inc(sem("scaled"), 1)
                if hi is not None and k >= 2 and k % 2 == 0:
                    dve.wait_ge(sem("scaled"), k)
                    split_lo(dve, k - 2)


def row(t, k):
    return t[k] if isinstance(k, int) else t[bass.ds(k, 1)].rearrange("a p n -> (a p) n")


def unit_product(pe, W, c, acc, xh, xl, per=0, i=0):
    W.ready(pe, c, per, i)
    s = c % 2
    return product(pe, acc, lambda k: W.hi[:, s, k * P:(k + 1) * P], lambda k: W.lo[:, s, k * P:(k + 1) * P],
                   lambda k, h: xh[:, k, h * H2:(h + 1) * H2], lambda k, h: xl[:, k, h * H2:(h + 1) * H2], KB)


def attention(nc, S, A, O, W, ahead, acc, psS, psR, xh, xl, gates_d, o_d):
    with ExitStack() as ctx:
        sb = lambda n, s, d=F32: ctx.enter_context(nc.sbuf_tensor(n, s, d))
        cst = {n: sb("at_" + n, [P, P]) for n in ("ident", "negtri", "negones", "before")}
        QT, KT, VT = sb("QT", [P, T]), sb("KT", [P, SEQ + P]), sb("VT", [P, T])
        CK, CV = sb("CK", [P, PAST]), sb("CV", [P, 4, P])
        VTM = sb("VTM", [P, 5, P])
        NA, SPL, WT = sb("NA", [P, ZN]), sb("SPL", [P, ZN]), sb("WT", [P, ZN])
        GB, OT = sb("GB", [P, T]), sb("OT", [P, T])
        zbank = {"A": psS[:, 0, :], "B": psS[:, 1, 0:416], "C": psR[:, 0, :]}
        zcols = {"A": slice(0, 512), "B": slice(512, 928), "C": slice(928, 1440)}
        bank_of = {3: "A", 1: "A", 2: "B", 0: "C"}

        def z_at(kb, q0=None):
            b = bank_of[kb]
            lo = ZCOL[kb] - zcols[b].start
            return zbank[b][:, lo + ((q0 or kb * P) - kb * P):lo + SEQ - kb * P]

        def cols(kb, q0=None):
            return slice(ZCOL[kb] + ((q0 or kb * P) - kb * P), ZCOL[kb] + SEQ - kb * P)

        def smp(b):
            return slice(ZS + 32 * b, ZS + 32 * b + 32)

        UNITS = 4
        block = ctx.enter_context(nc.Block())

        @block.sync
        def _(sp):
            for n, t in cst.items():
                a, w = CST_AT[n]
                sp.dma_start(t[:, :], A["cst"][:, a:a + w]).then_inc(S["at_cst"], 16)

            def head(i, last):
                W.load(sp, row(A["w_in"], i + 16), 2, UNITS, i)
                sp.wait_ge(S["at_o_ready"], i + 1)
                sp.dma_start(CK[:, :], A["ckT"][bass.ds(i, 1)].rearrange("a p n -> (a p) n")).then_inc(S["cache_loaded"], 16)
                sp.dma_start(CV[:, :, :], A["cv"][bass.ds(i, 1)].rearrange("a p b n -> (a p) b n")).then_inc(S["cache_loaded"], 16)
                W.load(sp, row(A["w_in"], i + 50), 3, UNITS, i)
                for u in range(2):
                    W.load(sp, ahead[u] if last else row(A["w_in"], i + 1 + 8 * u), 4 + u, UNITS, i)
            with sp.Fori(0, HEADS - 1) as i:
                head(i, False)
            head(HEADS - 1, True)

        @block.gpsimd
        def _(pool):
            with pool.Fori(0, HEADS) as i:
                for u in range(UNITS):
                    W.split_lo(pool, u + 2, UNITS, i)

        @block.tensor
        def _(pe):
            pe.sem_inc(S["at_o_ready"], 1)
            pe.wait_ge(S["at_cst"], 64)
            pe.wait_ge(S["pad_set"], 1)
            with pe.Fori(0, HEADS) as i:
                def project(u):
                    pe.wait_ge(S["at_acc_free"], UNITS * i + u + 1)
                    for mm in unit_product(pe, W, u, acc[u % 2], xh, xl, UNITS, i):
                        pass
                    mm.then_inc(W.used, 1)
                for u in range(3):
                    project(u)
                pe.wait_ge(S["at_acc_free"], UNITS * i + 4)
                pe.wait_ge(S["cache_loaded"], 32 * i + 32)
                pe.wait_ge(S["at_o_read"], i + 1)
                for kb in (3, 1):
                    mm = pe.matmul(z_at(kb), KT[:, kb * P:(kb + 1) * P], QT[:, kb * P:SEQ], start=kb == 3, stop=True,
                                   skip_group_check=True)
                mm.then_inc(S["z_ready"], 1)
                pe.matmul(z_at(2), KT[:, 2 * P:3 * P], QT[:, 2 * P:SEQ], start=True, stop=True)
                for b in range(5):
                    k = CK[:, b * P:(b + 1) * P] if b < 4 else KT[:, SEQ:SEQ + P]
                    mm = pe.matmul(zbank["B"][:, 256 + 32 * b:288 + 32 * b], k, QT[:, SEQ:T], start=False, stop=True,
                                   skip_group_check=True)
                mm.then_inc(S["z_ready"], 1)
                pe.matmul(z_at(0), KT[:, 0:P], QT[:, 0:SEQ], start=True, stop=True).then_inc(S["z_ready"], 1)
                pe.wait_ge(S["at_acc_free"], UNITS * i + 5)
                for b in range(4):
                    mm = pe.transpose(psR[:, 1, b * P:(b + 1) * P], VT[:, b * P:(b + 1) * P], cst["ident"][:, :])
                mm.then_inc(S["vt_ready"], 1)
                project(3)
                pe.wait_ge(S["vtm_evac"], 2 * i + 1)
                pe.transpose(psR[0:DEC, 1, 0:P], VT[:, SEQ:T], cst["ident"][:, :]).then_inc(S["vt_ready"], 1)
                pe.wait_ge(S["sp_ready"], 8 * i + 8)

                def tri(out, blocks, at):
                    for n, b in enumerate(blocks):
                        mm = pe.matmul(out(b), cst["negtri" if n == 0 else "negones"][:, :], SPL[:, at(b)],
                                       start=False, stop=False, skip_group_check=True)
                    return mm
                tri(lambda b: z_at(3, b * P), (3,), cols)
                tri(lambda b: z_at(1, b * P), (1, 2, 3), cols).then_inc(S["tri_ready"], 1)
                tri(lambda b: z_at(2, b * P), (2, 3), cols)
                for b in range(5):
                    mm = tri(lambda _: zbank["B"][:, 256 + 32 * b:288 + 32 * b], range(b, 5), smp)
                mm.then_inc(S["tri_ready"], 1)
                tri(lambda b: z_at(0, b * P), (0, 1, 2, 3), cols).then_inc(S["tri_ready"], 1)
                pe.wait_ge(S["vtm_evac"], 2 * i + 2)
                pe.wait_ge(S["wt_ready"], 4 * i + 4)
                for kb in range(4):
                    pe.matmul(psR[:, 1, kb * P:SEQ], VTM[:, kb, :], WT[:, cols(kb)], start=kb == 0, stop=kb == 3,
                              skip_group_check=True)
                for b in range(4):
                    pe.matmul(psS[:, 0, 0:DEC], CV[:, b, :], WT[:, smp(b)], start=b == 0, stop=False)
                pe.matmul(psS[:, 0, 0:DEC], VTM[0:DEC, 4, :], WT[0:DEC, smp(4)], start=False,
                          stop=True).then_inc(S["at_o_ready"], 1)

        @block.scalar
        def _(act):
            act.sem_inc(S["at_acc_free"], 2)
            act.sem_inc(S["at_o_read"], 1)
            act.sem_inc(S["kv_stored"], 16)
            act.sem_inc(S["gate_stored"], 16)
            act.sem_inc(S["o_stored"], 16)

            with act.Fori(0, HEADS) as i:
                act.wait_ge(S["at_o_read"], i + 1)
                act.wait_ge(S["kv_stored"], 32 * i + 16)
                for u, (dst, scale) in enumerate(((QT, SM_SCALE), (KT, 1.0), (VT, 1.0))):
                    W.wait_used(act, u, UNITS, i)
                    act.activation(dst[:, 0:T].rearrange("p (h t) -> p h t", h=2), acc[u % 2][:, :, 0:H2], ACT.Copy,
                                   scale=scale).then_inc(S["at_acc_free"], 1)
                    W.split_hi(act, u + 2, UNITS, i)
                act.wait_ge(S["at_acc_free"], UNITS * i + 5)
                act.dma_start(O["kT"][bass.ds(i, 1)].rearrange("a p n -> (a p) n"), KT[:, 0:T]).then_inc(S["kv_stored"], 16)
                act.dma_start(O["vT"][bass.ds(i, 1)].rearrange("a p n -> (a p) n"), VT[:, :]).then_inc(S["kv_stored"], 16)
                act.wait_ge(S["vt_ready"], 2 * i + 1)
                act.activation(VTM[:, 0:4, :], psR[:, 1, :].rearrange("p (b n) -> p b n", b=4),
                               ACT.Copy).then_inc(S["vtm_evac"], 1)
                for n, b in enumerate("ABC"):
                    act.wait_ge(S["z_ready"], 3 * i + n + 1)
                    act.activation(NA[:, zcols[b]], zbank[b], ACT.Abs).then_inc(S["abs_done"], 1)
                act.wait_ge(S["abs_done"], 3 * i + 3)
                act.activation(NA[:, :], NA[:, :], ACT.Exp, scale=-1.0).then_inc(S["act_sp"], 1)
                act.wait_ge(S["act_sp"], 2 * i + 1)
                act.activation(NA[:, :], NA[:, :], ACT.Ln, bias=1.0).then_inc(S["act_sp"], 1)
                W.wait_used(act, 3, UNITS, i)
                act.wait_ge(S["gate_stored"], 16 * i + 16)
                act.activation(GB[:, :].rearrange("p (h t) -> p h t", h=2), acc[1][:, :, 0:H2],
                               ACT.Sigmoid).then_inc(S["at_acc_free"], 1)
                act.wait_ge(S["at_acc_free"], UNITS * i + 6)
                act.dma_start(gates_d[bass.ds(i, 1)].rearrange("a p n -> (a p) n"), GB[:, :]).then_inc(S["gate_stored"], 16)
                W.split_hi(act, 5, UNITS, i)
                act.wait_ge(S["vt_ready"], 2 * i + 2)
                act.activation(VTM[0:DEC, 4, :], psR[0:DEC, 1, 0:P], ACT.Copy).then_inc(S["vtm_evac"], 1)
                for n, b in enumerate("ABC"):
                    act.wait_ge(S["tri_ready"], 3 * i + n + 1)
                    act.activation(WT[:, zcols[b]], zbank[b], ACT.Exp).then_inc(S["wt_exp"], 1)
                act.wait_ge(S["at_o_ready"], i + 2)
                act.wait_ge(S["o_stored"], 16 * i + 16)
                act.activation(OT[:, 0:SEQ], psR[:, 1, :], ACT.Copy)
                act.activation(OT[:, SEQ:T], psS[:, 0, 0:DEC], ACT.Copy).then_inc(S["at_o_read"], 1)

                act.wait_ge(S["at_o_read"], i + 2)
                act.dma_start(o_d[bass.ds(i, 1)].rearrange("a p n -> (a p) n"), OT[:, :]).then_inc(S["o_stored"], 16)

            act.wait_ge(S["kv_stored"], 32 * HEADS + 16)
            act.wait_ge(S["gate_stored"], 16 * HEADS + 16)
            act.wait_ge(S["o_stored"], 16 * HEADS + 16)

        @block.vector
        def _(dve):
            dve.memset(KT[:, T:SEQ + P], 0.0).then_inc(S["pad_set"], 1)
            dve.wait_ge(S["at_cst"], 64)
            with dve.Fori(0, HEADS) as i:
                dve.wait_ge(S["act_sp"], 2 * i + 2)
                ch = Chain(dve, S["sp_ready"], 8, i)
                for n, b in enumerate("ABC"):
                    ch(dve.scalar_tensor_tensor(SPL[:, zcols[b]], zbank[b], 0.0, NA[:, zcols[b]], ALU.max, ALU.add), wait=False)
                dve.wait_ge(S["sp_ready"], 8 * i + 3)
                before = cst["before"]
                for at, parts in ((ZCOL[3], P), (ZCOL[1], P), (ZCOL[2], P), (ZCOL[0], P), (ZS + 128, DEC)):
                    s = slice(at, at + parts)
                    ch(dve.tensor_tensor(SPL[:, s], SPL[:, s], before[:, 0:parts], ALU.mult), wait=False)
                ch.end()
                dve.wait_ge(S["wt_exp"], 3 * i + 3)
                n = 0
                for at, parts in ((ZCOL[3], 2 * P), (ZCOL[2], P), (ZCOL[0], P), (ZS + 128, DEC)):
                    s = slice(at, at + parts)
                    if parts == 2 * P:
                        out = WT[:, s].rearrange("p (a n) -> p a n", a=2)
                        m = before[:, :].unsqueeze(1).to_broadcast([P, 2, P])
                    else:
                        out, m = WT[:, s], before[:, 0:parts]
                    dve.scalar_tensor_tensor(out, out, 1.0, m, ALU.min, ALU.mult).then_inc(S["wt_ready"], 1)


def rwkv(nc, S, A, O, W, ahead, acc, psS, psR, xh, xl, par, eps, gates_d, o_d):
    with ExitStack() as ctx:
        sb = lambda n, s, d=F32: ctx.enter_context(nc.sbuf_tensor(n, s, d))
        EP = S0 + CH + 1
        ident, headones = sb("rw_ident", [P, P]), sb("rw_headones", [P, P])
        cm = sb("rw_chunk", [P, 10, CH])
        lr_mask, npair, npair_T, eye = cm[:, 0:2, :], cm[:, 2, :], cm[:, 3, :], cm[:, 4, :]
        scan_mask = sb("scan_mask", [P, E])
        TWA, SGG = sb("TWA", [P, E]), sb("SGG", [P, E])
        LW = sb("LW", [P, 2, P])
        EX = sb("EX", [P, E + 1])
        RM, T1, T2 = (sb(n, [P, E]) for n in ("RM", "T1", "T2"))
        KM, VM, BB = (sb(n, [P, EP]) for n in ("KM", "VM", "BB"))
        SG, AA, GG, CC, PP, BV = (sb(n, [P, E]) for n in ("SG", "AA", "GG", "CC", "PP", "BV"))
        AR = sb("AR", [P, 2, EP])
        YY = sb("YY", [P, E])
        TM, TS = sb("TM", [P, 4, 4, P]), sb("TS", [P, 4, CH])
        LTR, MTR = sb("LTR", [P, 9, 2, CH]), sb("MTR", [P, 9, 2, CH])
        TT = sb("TT", [P, 9, 2, CH])
        BT, YB, MV = sb("BT", [P, 9, CH]), sb("YB", [P, 9, CH]), sb("MV", [P, 9, CH])
        NT = sb("NT", [P, 9, P])
        DI, K0, ST = sb("DI", [P, 9, CH]), sb("K0", [P, 9, CH]), sb("ST", [P, 9, CH])
        SS, SF = sb("SS", [P, CH]), sb("SF", [P, CH])
        SH = sb("SH", [P, 26, 2])
        GB = sb("GBr", [P, T])

        UNITS, BASE, GATE0 = 6, 2, 8
        NS, NPV, NGV, NRS, NR = 12, 24, 5, 18, 50
        both = lambda t: t.rearrange("p (h t) -> p h t", h=2)
        rows = lambda hh: slice(CH * hh, CH * hh + CH)
        bank = lambda n: psR[:, n % 2, :]
        pad = slice(S0, S0 + CH)
        y_fill = lambda l, g: 7 + 5 * l + g
        z_fill = lambda l, g: 9 + 5 * l + g
        POST = 31
        y_slots = [range(0, 4), range(4, 9)]
        z_slots = lambda l: y_slots if l == 4 else [range(0, 4), range(4, 8), range(8, 9)]
        rs_bt = lambda l: 5 + l
        block = ctx.enter_context(nc.Block())

        def place(j, q):
            return (rows(q), pad) if j == 8 else (rows(j // 4), slice((2 * (j % 4) + q) * CH, (2 * (j % 4) + q + 1) * CH))

        def token_major(j, q, a):
            return TS[rows(q), a, :] if j == 8 else TM[rows(q), j % 4, a, rows(j // 4)]

        def unit_src(u, i):
            k = 24 + 8 * u + i if u < 3 else 58 + (u - 3) + 3 * i
            return A["w_in"][bass.ds(k, 1)].rearrange("a p n -> (a p) n")

        @block.sync
        def _(sp):
            for t, n in ((ident, "ident"), (headones, "headones"), (cm.rearrange("p a n -> p (a n)"), "chunk"), (scan_mask, "scan")):
                a, w = CST_AT[n]
                sp.dma_start(t[:, :], A["cst"][:, a:a + w]).then_inc(S["rw_cst"], 16)
            with sp.Fori(0, PAIRS) as i:
                for u in range(UNITS):
                    W.load(sp, unit_src(u, i), BASE + u, UNITS, i)
                    if u == 0:
                        sp.wait_ge(S["rw_lora"], 3 * i + 1)
                        sp.dma_start(LW[:, :, :], A["lora"][bass.ds(i, 1)].rearrange("a p b n -> (a p) b n")).then_inc(S["lw_loaded"], 16)
                    if u == 1:
                        sp.wait_ge(S["rw_gn"], NGV * i + 1)
                        sp.dma_start(SS[:, :], A["s0T"][bass.ds(i, 1)].rearrange("a p n -> (a p) n")).then_inc(S["ss_loaded"], 16)

            for u in range(2):
                W.load(sp, ahead[u], BASE + UNITS * PAIRS + u)

        @block.gpsimd
        def _(pool):
            with pool.Fori(0, PAIRS) as i:
                for u in range(UNITS):
                    W.split_lo(pool, BASE + u, UNITS, i)
            for u in range(2):
                W.split_lo(pool, BASE + UNITS * PAIRS + u)

        @block.tensor
        def _(pe):
            pe.sem_inc(S["rw_lora"], 1)
            pe.wait_ge(S["rw_cst"], 64)
            pe.wait_ge(S["rw_set"], 9)

            def project(c, per, i):
                pe.wait_ge(S["rw_acc_free"], per * i + c + 1)
                for n, mm in enumerate(unit_product(pe, W, c, acc[c % 2], xh, xl, per, i)):
                    if n == KB - 1:
                        mm.then_inc(W.used, 1)
                    yield

            def run(steps):
                for _ in steps:
                    pass
            run(project(0, 0, 0))
            run(project(1, 0, 0))

            with pe.Fori(0, PAIRS) as i:
                def gates():
                    for u in range(3, 6):
                        yield from project(BASE + u, UNITS, i)
                background = gates()

                def advance(n):
                    for _ in range(n):
                        next(background)

                def s_slot(n, lag=0):
                    pe.wait_ge(S["rw_s_free"], NS * i + n + 1 - lag)

                def small(n, lhsT, rhs):
                    s_slot(n)
                    for h in range(2):
                        mm = pe.matmul(psS[:, h, 0:EH], lhsT, rhs(slice(h * EH, (h + 1) * EH)), start=True, stop=True)
                    return mm

                r = project(BASE, UNITS, i)
                for _ in range(11):
                    next(r)
                pe.wait_ge(S["lw_loaded"], 16 * i + 16)
                pe.wait_ge(S["rw_twa"], 3)
                small(0, LW[0:CH, 0, :], lambda s: TWA[0:CH, s]).then_inc(S["rw_lora"], 1)
                for _ in range(2):
                    next(r)
                small(1, LW[CH:P, 0, :], lambda s: TWA[CH:P, s]).then_inc(S["rw_lora"], 1)
                for _ in range(2):
                    next(r)
                small(2, LW[:, 1, :], lambda s: SGG[:, s]).then_inc(S["rw_lora"], 1)
                run(r)
                run(project(BASE + 1, UNITS, i))
                v = project(BASE + 2, UNITS, i)
                for _ in range(8):
                    next(v)
                pe.wait_ge(S["rw_square"], 2 * i + 1)
                small(3, headones[:, :], lambda s: T1[:, s]).then_inc(S["rw_n2"], 1)
                run(v)
                advance(5)
                pe.wait_ge(S["rw_prep"], NPV * i + 19)
                small(4, headones[:, :], lambda s: T1[:, s]).then_inc(S["rw_bonus"], 1)
                advance(3)
                pe.wait_ge(S["rw_prep"], NPV * i + NPV)
                for t in range(4):
                    s_slot(5 + t, 1 if t else 0)
                    for a, x in enumerate((AR[:, 0, :], BB, KM, VM)):
                        mm = pe.transpose(psS[:, t % 2, a * P:(a + 1) * P], x[:, t * P:(t + 1) * P], ident[:, :])
                    mm.then_inc(S["rw_tm"], 1)
                s_slot(9, 1)
                pe.sem_inc(S["waits_passed"], 1)
                for q in range(2):
                    for a, x in enumerate((AR[:, 0, :], BB, KM, VM)):
                        mm = pe.matmul(psS[rows(q), 0, a * CH:(a + 1) * CH], x[rows(q), pad], ident[rows(q), rows(q)], start=True, stop=True,
                                       skip_group_check=True)
                mm.then_inc(S["rw_tm"], 1)

                def slot(n, *needs):
                    pe.wait_ge(S["rw_r_free"], NR * i + max([n + 1, *(m + 3 for m in needs)]))

                def pass_waits():
                    pe.sem_inc(S["waits_passed"], 1)

                def filled(mm):
                    mm.then_inc(S["rw_r_ready"], 1)

                def one(out, lhsT, rhs, start=True, stop=True, check=False):
                    return pe.matmul(out, lhsT, rhs, start=start, stop=stop, skip_group_check=not check)

                def pairs(slots):
                    return [(n, j, q) for n, j in enumerate(slots) for q in range(2)]

                for n, (x, hh) in enumerate(((BB, 0), (BB, 1), (KM, 0), (KM, 1))):
                    slot(n)
                    pass_waits()
                    for m, j, q in pairs(range(4 * hh, 4 * hh + 4)):
                        r, s = place(j, q)
                        mm = one(bank(n)[rows(q), m * P:(m + 1) * P], x[r, s], AR[r, :, s])
                    filled(mm)
                for n, slots in ((4, range(0, 4)), (5, range(4, 8)), (6, (8,))):
                    slot(n)
                    pass_waits()
                    at = 256 if n == 6 else 0
                    for m, j, q in pairs(slots):
                        r, s = place(j, q)
                        if n == 6:
                            one(bank(n)[rows(q), 0:P], BB[r, s], AR[r, :, s])
                            one(bank(n)[rows(q), P:2 * P], KM[r, s], AR[r, :, s])
                        mm = one(bank(n)[rows(q), at + m * CH:at + (m + 1) * CH], AR[r, 0, s], BB[r, s])
                    filled(mm)
                advance(5)
                for l in range(5):
                    pe.wait_ge(S["rw_steps"], NRS * i + rs_bt(l))
                    for g, slots in enumerate(y_slots):
                        slot(y_fill(l, g), *([z_fill(l - 1, 0 if g == 0 else 2)] if l else []))
                        pass_waits()
                        for m, j, q in pairs(slots):
                            mm = one(bank(y_fill(l, g))[rows(q), m * CH:(m + 1) * CH], BT[rows(q), j, :], TT[rows(q), j, 0, :])
                        filled(mm)
                    advance(1)
                    for g, slots in enumerate(z_slots(l)):
                        slot(z_fill(l, g), y_fill(l, min(g, 1)))
                        pass_waits()
                        o = bank(z_fill(l, g))
                        for m, j, q in pairs(slots):
                            r = rows(q)
                            if l < 4:
                                one(o[r, m * P:m * P + CH], TT[r, j, 1, :], YB[r, j, :])
                                mm = one(o[r, m * P + CH:(m + 1) * P], YB[r, j, :], TT[r, j, 1, :])
                            else:
                                mm = one(o[r, m * CH:(m + 1) * CH], YB[r, j, :], TT[r, j, 1, :])
                        filled(mm)
                    advance(2)
                p = POST
                pe.wait_ge(S["rw_s_free"], NS * i + 11)
                for g, slots in enumerate(y_slots):
                    slot(p + g)
                    pass_waits()
                    for m, j, q in pairs(slots):
                        mm = one(bank(p + g)[rows(q), m * CH:(m + 1) * CH], MTR[rows(q), j, 0, :], token_major(j, q, 3))
                    filled(mm)
                for g, slots in enumerate((range(0, 4), range(4, 8), (8,))):
                    slot(p + 2 + g, p + min(g, 1), z_fill(4, min(g, 1)))
                    pass_waits()
                    o = bank(p + 2 + g)
                    for m, j, q in pairs(slots):
                        r = rows(q)
                        one(o[r, m * P:m * P + CH], TT[r, j, 1, :], token_major(j, q, 0))
                        mm = one(o[r, m * P + CH:(m + 1) * P], TT[r, j, 1, :], MV[r, j, :])
                    filled(mm)
                for q in range(2):
                    slot(p + 5 + q, p + 3)
                    pass_waits()
                    o, s = bank(p + 5 + q), rows(q)
                    for hh in range(2):
                        for t in range(4):
                            j, r = 4 * hh + t, rows(hh)
                            one(o[r, t * CH:(t + 1) * CH], NT[s, j, 0:CH], LTR[s, j, 1, :])
                            one(o[r, 256 + t * CH:256 + (t + 1) * CH], NT[s, j, CH:P], LTR[s, j, 1, :], stop=False)
                            mm = one(o[r, 256 + t * CH:256 + (t + 1) * CH], token_major(j, q, 3), MTR[s, j, 1, :], start=False)
                    filled(mm)
                for q in range(2):
                    slot(p + 7 + q)
                    pass_waits()
                    o, s = bank(p + 7 + q), rows(q)
                    for hh in range(2):
                        for t in range(4):
                            j, r = 4 * hh + t, rows(hh)
                            one(o[r, t * CH:(t + 1) * CH], NT[s, j, 0:CH], token_major(j, q, 1))
                            one(o[r, 256 + t * CH:256 + (t + 1) * CH], token_major(j, q, 2), token_major(j, q, 3), stop=False)
                            mm = one(o[r, 256 + t * CH:256 + (t + 1) * CH], token_major(j, q, 1), NT[s, j, CH:P], start=False)
                    filled(mm)
                slot(p + 9, p + 4)
                pass_waits()
                for q in range(2):
                    r = rows(q)
                    o = bank(p + 9)[r, :]
                    one(o[:, 0:64], NT[r, 8, 0:CH], LTR[r, 8, 1, :])
                    one(o[:, 64:128], NT[r, 8, CH:P], LTR[r, 8, 1, :], stop=False)
                    one(o[:, 64:128], TS[r, 3, :], MTR[r, 8, 1, :], start=False)
                    one(o[:, 128:192], NT[r, 8, 0:CH], TS[r, 1, :])
                    one(o[:, 192:256], TS[r, 2, :], TS[r, 3, :], stop=False)
                    mm = one(o[:, 192:256], TS[r, 1, :], NT[r, 8, CH:P], start=False)
                filled(mm)
                pe.wait_ge(S["ss_loaded"], 16 * i + 16)
                chain = p + 10
                for c in range(CHUNKS):
                    slot(chain + c, chain + c - 1)
                    pass_waits()
                    for hh in range(2):
                        r = rows(hh)
                        mm = one(bank(chain + c)[r, 0:CH], DI[r, c, :], ST[r, c, :])
                        if c == 0:
                            one(bank(chain)[r, CH:2 * CH], DI[r, 8, :], SS[r, :])
                            mm = one(bank(chain)[r, 2 * CH:2 * CH + DEC], SS[r, :], AR[r, 1, S0:S0 + DEC])
                    filled(mm)
                    advance(1)
                last = chain + CHUNKS
                advance(1)
                slot(last, last - 1)
                pass_waits()
                for c in range(CHUNKS):
                    for hh in range(2):
                        r = rows(hh)
                        mm = one(bank(last)[r, c * CH:(c + 1) * CH], ST[r, c, :], AR[r, 1, c * CH:(c + 1) * CH])
                filled(mm)
                advance(1)
                slot(last, last)
                small(10, headones[:, :], lambda s: YY[:, s]).then_inc(S["rw_mean"], 1)
                advance(7)
                pe.wait_ge(S["rw_square"], 2 * i + 2)
                small(11, headones[:, :], lambda s: T2[:, s]).then_inc(S["rw_var"], 1)
                run(background)

        @block.scalar
        def _(act):
            act.sem_inc(S["rw_acc_free"], 2)
            act.sem_inc(S["rw_s_free"], 1)
            act.sem_inc(S["rw_gate_stored"], 16)
            act.sem_inc(S["rw_stored"], 16)
            act.wait_ge(S["rw_set"], 9)

            def evacuate(c, per, i, ready):
                W.wait_used(act, c, per, i)
                act.activation(EX[:, 1:H2 + 1], acc[c % 2][:, 0, 0:H2], ACT.Copy)
                act.activation(EX[:, H2 + 1:SEQ + 1], acc[c % 2][:, 1, 0:SEQ - H2], ACT.Copy)
                act.activation(EX[:, S0 + 1:S0 + 1 + DEC], acc[c % 2][:, 1, SEQ - H2:H2], ACT.Copy).then_inc(S["rw_acc_free"], 1)
                act.activation(EX[:, S0:S0 + 1], ready, ACT.Copy).then_inc(S["rw_p_ready"], 1)

            evacuate(0, 0, 0, par[:, C_SHIFT + 24:C_SHIFT + 25])
            act.wait_ge(S["rw_first"], 3)
            act.activation(TWA[0:CH, :], RM[0:CH, :], ACT.Tanh).then_inc(S["rw_twa"], 1)
            act.activation(TWA[CH:P, :], RM[CH:P, :], ACT.Copy).then_inc(S["rw_twa"], 1)
            evacuate(1, 0, 0, par[:, C_SHIFT + 25:C_SHIFT + 26])
            act.wait_ge(S["rw_first"], 6)
            act.activation(SGG[:, :], KM[:, 0:E], ACT.Sigmoid).then_inc(S["rw_twa"], 1)
            W.split_hi(act, 2)
            W.split_hi(act, 3)

            def gate(i, u):
                c = BASE + 3 + u
                W.wait_used(act, c, UNITS, i)
                act.wait_ge(S["rw_gate_stored"], 48 * i + 16 * u + 16)
                act.activation(both(GB[:, :]), acc[c % 2][:, :, 0:H2], ACT.Sigmoid).then_inc(S["rw_acc_free"], 1)
                act.wait_ge(S["rw_acc_free"], UNITS * i + c + 3)
                act.dma_start(gates_d[bass.ds(3 * i + GATE0 + u, 1)].rearrange("a p n -> (a p) n"), GB[:, :]).then_inc(S["rw_gate_stored"], 16)

            with act.Fori(0, PAIRS) as i:
                col = lambda n: par[:, bass.ds(NPAR * i + PAR.index(n), 1)]
                shift = lambda a: par[:, bass.ds(C_SHIFT + 8 * a + i, 1)]
                act.wait_ge(S["rw_gn"], NGV * i + 1)
                act.wait_ge(S["rw_lora"], 3 * i + 2)
                act.activation(both(SG[:, :]), psS[:, :, 0:EH], ACT.Sigmoid, bias=col("w0")).then_inc(S["rw_s_free"], 1)
                act.wait_ge(S["rw_lora"], 3 * i + 3)
                act.activation(both(AA[:, :]), psS[:, :, 0:EH], ACT.Sigmoid, bias=col("a0")).then_inc(S["rw_s_free"], 1)
                act.wait_ge(S["rw_lora"], 3 * i + 4)
                act.activation(both(GG[:, :]), psS[:, :, 0:EH], ACT.Copy).then_inc(S["rw_s_free"], 1)
                evacuate(2, UNITS, i, shift(0))
                W.split_hi(act, 4, UNITS, i)
                act.wait_ge(S["rw_prep"], NPV * i + 5)
                act.activation(PP[:, :], CC[:, :], ACT.Exp, scale=-KAPPA).then_inc(S["rw_decay"], 1)
                act.activation(SG[:, :], SG[:, :], ACT.Exp, scale=-KAPPA).then_inc(S["rw_decay"], 1)
                act.wait_ge(S["rw_decay"], 4 * i + 1)
                act.activation(CC[:, :], CC[:, :], ACT.Exp, scale=KAPPA).then_inc(S["rw_decay"], 1)
                evacuate(3, UNITS, i, shift(1))
                W.split_hi(act, 5, UNITS, i)
                act.wait_ge(S["rw_prep"], NPV * i + 9)
                act.activation(T1[:, :], KM[:, 0:E], ACT.Square, scale=col("k_k")).then_inc(S["rw_square"], 1)
                act.wait_ge(S["rw_s_free"], NS * i + 5)
                act.activation(T1[:, :], T1[:, :], ACT.Sqrt).then_inc(S["rw_decay"], 1)
                evacuate(4, UNITS, i, shift(2))
                W.split_hi(act, 6, UNITS, i)
                for t in range(5):
                    act.wait_ge(S["rw_tm"], 5 * i + t + 1)
                    if t < 4:
                        act.activation(TM[:, t, :, :].rearrange("p a n -> p (a n)"), psS[:, t % 2, :],
                                       ACT.Copy).then_inc(S["rw_s_free"], 1)
                    else:
                        act.activation(TS.rearrange("p a n -> p (a n)"), psS[:, 0, 0:4 * CH], ACT.Copy).then_inc(S["rw_s_free"], 1)
                for u in range(2):
                    gate(i, u)
                    W.split_hi(act, 7 + u, UNITS, i)
                act.wait_ge(S["rw_s_free"], NS * i + 12)
                act.activation(T2[:, :], T1[:, :], ACT.Square).then_inc(S["rw_square"], 1)
                act.wait_ge(S["rw_var"], i + 1)
                act.activation(both(SG[:, :]), psS[:, :, 0:EH], ACT.Sqrt, bias=eps[:, 1:2],
                               scale=1.0 / CH).then_inc(S["rw_s_free"], 1)
                gate(i, 2)
                W.split_hi(act, 9, UNITS, i)
                act.wait_ge(S["rw_gn"], NGV * i + NGV + 1)
                act.dma_start(o_d[bass.ds(HEADS + i, 1), :, 0:SEQ].rearrange("a p n -> (a p) n"), RM[:, 0:SEQ]).then_inc(S["rw_stored"], 16)
                act.dma_start(o_d[bass.ds(HEADS + i, 1), :, SEQ:T].rearrange("a p n -> (a p) n"), RM[:, S0:S0 + DEC]).then_inc(S["rw_stored"], 16)
                act.dma_start(O["wkvp"][bass.ds(i, 1)].rearrange("a p n -> (a p) n"), ST[:, 8, :]).then_inc(S["rw_stored"], 16)
                act.dma_start(O["wkvs"][bass.ds(i, 1)].rearrange("a p n -> (a p) n"), SF[:, :]).then_inc(S["rw_stored"], 16)
            act.wait_ge(S["rw_first"], 6)
            act.dma_start(O["shift"], SH[:, :, :]).then_inc(S["rw_stored"], 16)
            act.wait_ge(S["rw_gate_stored"], 48 * PAIRS + 16)
            act.wait_ge(S["rw_stored"], 64 * PAIRS + 32)

        @block.vector
        def _(dve):
            for t in (KM, VM, BB, AR[:, 0, :], AR[:, 1, :]):
                dve.memset(t[:, E:EP], 0.0).then_inc(S["rw_set"], 1)
            dve.memset(ST[:, 0, :], 0.0).then_inc(S["rw_set"], 1)
            dve.memset(EX[:, 0:1], 0.0).then_inc(S["rw_set"], 1)
            dve.memset(EX[:, E:E + 1], 0.0).then_inc(S["rw_set"], 1)
            dve.memset(YY[:, SEQ:E], 0.0).then_inc(S["rw_set"], 1)
            dve.sem_inc(S["rw_gn"], 1)
            dve.sem_inc(S["rw_r_free"], 2)
            dve.wait_ge(S["rw_set"], 9)
            dve.wait_ge(S["rw_cst"], 64)

            def mix(ch, dst, mu, at, ready):
                dve.wait_ge(S["rw_p_ready"], ready)
                ch(dve.tensor_tensor(T1[:, :], EX[:, 0:E], EX[:, 1:E + 1], ALU.subtract))
                ch(dve.scalar_tensor_tensor(dst[:, 0:E], T1[:, :], mu, EX[:, 1:E + 1], ALU.mult, ALU.add))
                ch(dve.tensor_copy(SH[:, at, :], EX[:, SEQ:E:DEC + 1]))

            first = Chain(dve, S["rw_first"], 6, 0)
            mix(first, RM, par[:, C_MUWA:C_MUWA + 1], slice(24, 25), 1)
            mix(first, KM, par[:, C_MUG:C_MUG + 1], slice(25, 26), 2)

            dve.wait_ge(S["rw_twa"], 3)
            with dve.Fori(0, PAIRS) as i:
                col = lambda n: par[:, bass.ds(NPAR * i + PAR.index(n), 1)]
                ch = Chain(dve, S["rw_prep"], NPV, i)
                tt = lambda o, a, b, op: ch(dve.tensor_tensor(o[:, :], a[:, :], b[:, :], op))
                dve.wait_ge(S["rw_stored"], 64 * i + 16)
                mix(ch, RM, col("mu_r"), bass.ds(i, 1), 3 * i + 3)
                dve.wait_ge(S["rw_s_free"], NS * i + 2)
                ch(dve.tensor_tensor_scan(CC[:, :], scan_mask[:, :], SG[:, :], 0.0, ALU.mult, ALU.add))
                tt(SG, CC, SG, ALU.subtract)
                mix(ch, KM, col("mu_k"), bass.ds(8 + i, 1), 3 * i + 4)
                k, b = KM[:, 0:E], BB[:, 0:E]
                ch(dve.memset(KM[:, E - 1:E], 0.0))
                ch(dve.tensor_scalar(T2[:, :], k, col("k_k"), None, ALU.mult))
                dve.wait_ge(S["rw_s_free"], NS * i + 3)
                ch(dve.tensor_tensor(b, T2[:, :], AA[:, :], ALU.mult))
                ch(dve.tensor_scalar(AA[:, :], AA[:, :], 1.0, col("k_a"), ALU.subtract, ALU.mult))
                dve.wait_ge(S["rw_n2"], i + 1)
                dve.tensor_scalar(both(T1[:, :]), psS[:, :, 0:EH], 1e-24, None, ALU.max).then_inc(S["rw_s_free"], 1)
                ch(dve.scalar_tensor_tensor(k, AA[:, :], 1.0, k, ALU.add, ALU.mult))
                dve.wait_ge(S["rw_decay"], 4 * i + 3)
                ch(dve.tensor_tensor(AR[:, 1, 0:E], RM[:, :], PP[:, :], ALU.mult))
                dve.wait_ge(S["rw_decay"], 4 * i + 4)
                ch(dve.reciprocal(T1[:, :], T1[:, :]))
                ch(dve.tensor_tensor(T2[:, :], T2[:, :], T1[:, :], ALU.mult), wait=False)
                ch(dve.tensor_tensor(b, b, T1[:, :], ALU.mult))
                ch(dve.tensor_tensor(AR[:, 0, 0:E], T2[:, :], SG[:, :], ALU.mult), wait=False)
                ch(dve.scalar_tensor_tensor(T1[:, :], RM[:, :], col("r_k"), k, ALU.mult, ALU.mult))
                ch(dve.tensor_tensor(b, b, CC[:, :], ALU.mult), wait=False)
                ch(dve.tensor_tensor(k, k, CC[:, :], ALU.mult))
                dve.wait_ge(S["rw_p_ready"], 3 * i + 5)
                ch(dve.tensor_tensor(T2[:, :], EX[:, 0:E], EX[:, 1:E + 1], ALU.subtract))
                ch(dve.scalar_tensor_tensor(VM[:, 0:E], T2[:, :], col("mu_v"), EX[:, 1:E + 1], ALU.mult, ALU.add))
                ch(dve.tensor_copy(SH[:, bass.ds(16 + i, 1), :], EX[:, SEQ:E:DEC + 1]))
                ch.end()
                dve.wait_ge(S["rw_bonus"], i + 1)
                dve.tensor_tensor(both(BV[:, :]), psS[:, :, 0:EH], both(VM[:, 0:E]), ALU.mult).then_inc(S["rw_s_free"], 1)

                rs = Chain(dve, S["rw_steps"], NRS, i)
                counted = [0]

                def ready(n):
                    assert n == counted[0], (n, counted[0])
                    dve.wait_ge(S["rw_r_ready"], NR * i + n + 1)
                    return bank(n)

                def read(instruction):
                    counted[0] += 1
                    instruction.then_inc(S["rw_r_free"], 1)

                def after_read():
                    dve.wait_ge(S["rw_r_free"], NR * i + counted[0] + 2)

                def over(m, n):
                    return m.unsqueeze(1).to_broadcast([P, n, CH])
                slots = lambda t, n: t.rearrange("p (a n) -> p a n", a=n)
                for n, (x, hh) in enumerate(((LTR, 0), (LTR, 1), (MTR, 0), (MTR, 1))):
                    ps = ready(n)
                    read(dve.tensor_tensor(x[:, 4 * hh:4 * hh + 4], ps.rearrange("p (a b n) -> p a b n", a=4, b=2),
                                           lr_mask.unsqueeze(1).to_broadcast([P, 4, 2, CH]), ALU.mult))
                for hh in range(2):
                    ps = ready(4 + hh)
                    read(dve.tensor_tensor(TT[:, 4 * hh:4 * hh + 4, 0, :], slots(ps[:, 0:256], 4), over(npair, 4), ALU.mult))
                ps = ready(6)
                rs(dve.tensor_tensor(LTR[:, 8], slots(ps[:, 0:P], 2), lr_mask, ALU.mult), wait=False)
                rs(dve.tensor_tensor(MTR[:, 8], slots(ps[:, P:2 * P], 2), lr_mask, ALU.mult), wait=False)
                read(dve.tensor_tensor(TT[:, 8, 0, :], ps[:, 256:320], npair, ALU.mult))
                after_read()
                rs(dve.tensor_tensor(TT[:, :, 1, :], LTR[:, :, 0, :], over(npair_T, 9), ALU.mult))
                tt18 = TT.rearrange("p a b n -> p (a b) n")
                rs(dve.tensor_tensor(tt18, tt18, over(eye, 18), ALU.add), wait=False)

                def level_mask(l):
                    rs(dve.tensor_tensor(BT[:, :, :], LTR[:, :, 0, :], over(cm[:, 5 + l, :], 9), ALU.mult), wait=False)
                    assert rs.k == rs_bt(l)
                level_mask(0)
                for l in range(5):
                    for g, js in enumerate(y_slots):
                        ps, n = ready(y_fill(l, g)), len(js)
                        read(dve.tensor_copy(YB[:, js[0]:js[0] + n, :], slots(ps[:, 0:n * CH], n)))
                    if l < 4:
                        level_mask(l + 1)
                    for g, js in enumerate(z_slots(l)):
                        ps, n = ready(z_fill(l, g)), len(js)
                        if l == 4:
                            o, ps = TT[:, js[0]:js[0] + n, 1, :], slots(ps[:, 0:n * CH], n)
                        else:
                            o, ps = TT[:, js[0]:js[0] + n].rearrange("p a b n -> p (a b n)"), ps[:, 0:n * P]
                        read(dve.tensor_tensor(o, o, ps, ALU.subtract))
                p = POST
                for g, js in enumerate(y_slots):
                    ps, n = ready(p + g), len(js)
                    read(dve.tensor_copy(MV[:, js[0]:js[0] + n, :], slots(ps[:, 0:n * CH], n)))
                for g, (j, n) in enumerate(((0, 4), (4, 4), (8, 1))):
                    ps = ready(p + 2 + g)
                    read(dve.tensor_scalar(NT[:, j:j + n, :], slots(ps[:, 0:n * P], n), -1.0, None, ALU.mult))
                chunks = lambda t, q: t.rearrange("p (t q n) -> p t q n", q=2, n=CH)[:, :, q, :]
                for q in range(2):
                    ps = ready(p + 5 + q)
                    o = chunks(AR[:, 1, 0:SEQ], q)
                    rs(dve.tensor_tensor(o, o, slots(ps[:, 0:256], 4), ALU.add), wait=False)
                    read(dve.tensor_copy(chunks(AR[:, 0, 0:SEQ], q), slots(ps[:, 256:512], 4)))
                for q in range(2):
                    ps = ready(p + 7 + q)
                    rs(dve.tensor_tensor(DI[:, q:8:2, :], slots(ps[:, 0:256], 4), over(eye, 4), ALU.add), wait=False)
                    end = PP[:, (q + 1) * CH - 1:SEQ:2 * CH]
                    read(dve.tensor_tensor(K0[:, q:8:2, :], slots(ps[:, 256:512], 4),
                                           end.unsqueeze(2).to_broadcast([P, 4, CH]), ALU.mult))
                ps = ready(p + 9)
                send = PP[:, S0 + DEC - 1:S0 + DEC]
                smp = slice(S0, S0 + DEC)
                rs(dve.tensor_tensor(AR[:, 1, smp], AR[:, 1, smp], ps[:, 0:DEC], ALU.add), wait=False)
                rs(dve.tensor_copy(AR[:, 0, smp], ps[:, 64:64 + DEC]), wait=False)
                rs(dve.tensor_tensor(DI[:, 8, :], ps[:, 128:192], eye, ALU.add), wait=False)
                read(dve.tensor_scalar(K0[:, 8, :], ps[:, 192:256], send, None, ALU.mult))
                after_read()
                chain = p + 10
                for c in range(CHUNKS):
                    ps = ready(chain + c)
                    if c == 0:
                        rs(dve.scalar_tensor_tensor(SF[:, :], ps[:, CH:2 * CH], send, K0[:, 8, :], ALU.mult, ALU.add), wait=False)
                        rs(dve.tensor_tensor(YY[:, S0:S0 + DEC], ps[:, 2 * CH:2 * CH + DEC], AR[:, 0, S0:S0 + DEC], ALU.add), wait=False)
                    read(dve.scalar_tensor_tensor(ST[:, c + 1, :], ps[:, 0:CH], PP[:, c * CH + CH - 1:(c + 1) * CH], K0[:, c, :],
                                                  ALU.mult, ALU.add))
                rs.end()
                ps = ready(chain + CHUNKS)
                read(dve.tensor_tensor(YY[:, 0:SEQ], ps, AR[:, 0, 0:SEQ], ALU.add))
                assert counted[0] == NR
                after_read()
                gn = Chain(dve, S["rw_gn"], NGV, i, credit=1)
                dve.wait_ge(S["rw_mean"], i + 1)
                dve.scalar_tensor_tensor(both(T1[:, :]), psS[:, :, 0:EH], -1.0 / CH, both(YY[:, :]), ALU.mult,
                                         ALU.add).then_inc(S["rw_s_free"], 1)
                dve.wait_ge(S["rw_s_free"], NS * i + 13)
                gn(dve.reciprocal(SG[:, :], SG[:, :]))
                gn(dve.tensor_tensor(T1[:, :], T1[:, :], SG[:, :], ALU.mult))
                gn(dve.tensor_scalar(T1[:, :], T1[:, :], col("ln_g"), col("ln_b"), ALU.mult, ALU.add))
                gn(dve.tensor_tensor(T1[:, :], T1[:, :], BV[:, :], ALU.add))
                gn(dve.tensor_tensor(RM[:, :], T1[:, :], GG[:, :], ALU.mult))
                gn.end()


def mix(nc, S, A, W, ahead, acc, psS, psR, mh, ml, gates_d, o_d):
    with ExitStack() as ctx:
        sb = lambda n, s, d=F32: ctx.enter_context(nc.sbuf_tensor(n, s, d))
        oh, ol = sb("oh", [P, KB, T], F32R), sb("ol", [P, KB, T], F32R)
        OF, G, MX = sb("OF", [P, 4, T]), sb("G", [P, 2, 2, T]), sb("MX", [P, 2, T])
        N = 2
        ps = [(acc[0], acc[1]), (psS, psR)]
        halves = lambda t: t.rearrange("p (h t) -> p h t", h=2)
        block = ctx.enter_context(nc.Block())

        @block.sync
        def _(sp):
            for k in range(KB):
                if k >= 4:
                    sp.wait_ge(S["mx_o_lo"], k - 3)
                sp.dma_start(OF[:, k % 4, :], o_d[k]).then_inc(S[f"mx_o_loaded{k % 4}"], 16)

            def block_pair(i, last):
                for u in range(N):
                    sp.wait_ge(S["mx_sum"], N * i + u + 1)
                    for g in range(2):
                        sp.dma_start(G[:, u, g, :], row(gates_d, N * i + u + KB * g)).then_inc(S[f"mx_gates{u}"], 16)
                    W.load(sp, ahead[u] if last else row(A["w_br"], N * i + u + 2), u + 2, N, i)
            with sp.Fori(0, KB // N - 1) as i:
                block_pair(i, False)
            block_pair(KB // N - 1, True)

        @block.gpsimd
        def _(pool):
            with pool.Fori(0, KB // N) as i:
                for u in range(N):
                    W.split_lo(pool, u + 2, N, i)

        @block.tensor
        def _(pe):
            with pe.Fori(0, KB // N) as i:
                for u in range(N):
                    W.ready(pe, u, N, i)
                    pe.wait_ge(S["mx_mixed"], 2 * (N * i + u) + 2)
                    for g in range(2):
                        pe.wait_ge(S["mx_o_lo"], 8 * g + 8)
                        for mm in product(pe, ps[u][g], lambda k: W.hi[:, u, (8 * g + k) * P:(8 * g + k + 1) * P],
                                          lambda k: W.lo[:, u, (8 * g + k) * P:(8 * g + k + 1) * P],
                                          lambda k, h: oh[:, 8 * g + k, h * H2:(h + 1) * H2],
                                          lambda k, h: ol[:, 8 * g + k, h * H2:(h + 1) * H2], 8):
                            pass
                    mm.then_inc(W.used, 1)

        @block.scalar
        def _(act):
            for k in range(KB):
                act.wait_ge(S[f"mx_o_loaded{k % 4}"], 16 * (k // 4 + 1))
                act.activation(oh[:, k, :], OF[:, k % 4, :], ACT.Copy).then_inc(S["mx_o_hi"], 1)

            with act.Fori(0, KB // N) as i:
                for u in range(N):
                    act.wait_ge(S["mx_sum"], N * i + u + 3)
                    act.activation(mh[:, bass.ds(N * i + u, 1), :].rearrange("p a t -> p (a t)"),
                                   MX[:, u, :], ACT.Copy).then_inc(S["mx_hi_part"], 1)
                    W.split_hi(act, u + 2, N, i)

        @block.vector
        def _(dve):
            dve.sem_inc(S["mx_mixed"], 4)
            dve.sem_inc(S["mx_sum"], 2)
            for k in range(KB):
                dve.wait_ge(S["mx_o_hi"], k + 1)
                dve.tensor_tensor(ol[:, k, :], OF[:, k % 4, :], oh[:, k, :].bitcast(F32), ALU.subtract).then_inc(S["mx_o_lo"], 1)
            with dve.Fori(0, KB // N) as i:
                for u in range(N):
                    dve.wait_ge(S[f"mx_gates{u}"], 32 * i + 32)
                    W.wait_used(dve, u, N, i)
                    g = G[:, u, :, :]
                    for b in range(2):
                        dve.tensor_tensor(halves(g[:, b, :]), ps[u][b][:, :, 0:H2], halves(g[:, b, :]), ALU.mult).then_inc(S["mx_mixed"], 1)
                    dve.wait_ge(S["mx_mixed"], 2 * (N * i + u) + 6)
                    dve.tensor_tensor(MX[:, u, :], g[:, 0, :], g[:, 1, :], ALU.add).then_inc(S["mx_sum"], 1)
                    dve.wait_ge(S["mx_hi_part"], N * i + u + 1)
                    k = bass.ds(N * i + u, 1)
                    flat = lambda t: t[:, k, :].rearrange("p a t -> p (a t)")
                    dve.tensor_tensor(flat(ml), MX[:, u, :], flat(mh).bitcast(F32), ALU.subtract).then_inc(S["mx_lo_part"], 1)
                    dve.wait_ge(S["mx_lo_part"], N * i + u + 1)


def out_projection(nc, S, A, W, ahead, acc, psS, mh, ml, X):
    with ExitStack() as ctx:
        sb = lambda n, s, d=F32: ctx.enter_context(nc.sbuf_tensor(n, s, d))
        SQ, ones = sb("wo_SQ", [P, 2, T]), sb("wo_ones", [P, P])
        N = 2
        halves = lambda t: t.rearrange("p (h t) -> p h t", h=2)
        flat = lambda k: X[:, bass.ds(k, 1), :].rearrange("p a t -> p (a t)")
        block = ctx.enter_context(nc.Block())

        @block.sync
        def _(sp):
            for q in range(4):
                sp.dma_start(X[:, 4 * q:4 * q + 4, :], A["xT"][:, 4 * q:4 * q + 4, :]).then_inc(S["wo_x"], 16)

            def block_pair(i, last):
                for u in range(N):
                    W.load(sp, ahead[u] if last else row(A["w_out"], N * i + u + 2), u + 2, N, i)
            with sp.Fori(0, KB // N - 1) as i:
                block_pair(i, False)
            block_pair(KB // N - 1, True)

        @block.gpsimd
        def _(pool):
            with pool.Fori(0, KB // N) as i:
                for u in range(N):
                    W.split_lo(pool, u + 2, N, i)

        @block.tensor
        def _(pe):
            def add_squares(u, start=False):
                for half in range(2):
                    mm = pe.matmul(psS[:, half, 0:H2], ones[:, :], SQ[:, u, half * H2:(half + 1) * H2], start=start, stop=True,
                                   skip_group_check=True)
                mm.then_inc(S["wo_summed"], 1)
            pe.wait_ge(S["wo_set"], 2)
            add_squares(1, True)
            with pe.Fori(0, KB // N) as i:
                for u in range(N):
                    pe.wait_ge(S["wo_sum"], N * i + u + 1)
                    for mm in unit_product(pe, W, u, acc[u], mh, ml, N, i):
                        pass
                    mm.then_inc(W.used, 1)
                    pe.wait_ge(S["wo_square"], N * i + u + 1)
                    add_squares(1 - u)
            pe.wait_ge(S["wo_square"], KB + 1)
            add_squares(1)

        @block.scalar
        def _(act):
            act.sem_inc(S["wo_square"], 1)
            with act.Fori(0, KB // N) as i:
                for u in range(N):
                    act.wait_ge(S["wo_sum"], N * i + u + 3)
                    act.wait_ge(S["wo_summed"], N * i + u + 1)
                    act.activation(SQ[:, u, :], flat(N * i + u), ACT.Square).then_inc(S["wo_square"], 1)
                    W.split_hi(act, u + 2, N, i)

        @block.vector
        def _(dve):
            dve.memset(ones[:, :], 1.0).then_inc(S["wo_set"], 1)
            dve.memset(SQ[:, 1, :], 0.0).then_inc(S["wo_set"], 1)
            dve.sem_inc(S["wo_sum"], 2)
            dve.wait_ge(S["wo_x"], 64)
            with dve.Fori(0, KB // N) as i:
                for u in range(N):
                    W.wait_used(dve, u, N, i)
                    h = halves(flat(N * i + u))
                    dve.tensor_tensor(h, acc[u][:, :, 0:H2], h, ALU.add).then_inc(S["wo_sum"], 1)


def retrieval(nc, S, A, W, ahead, acc, psS, psR, hh, hl, IT, pre_d):
    with ExitStack() as ctx:
        sb = lambda n, s, d=F32: ctx.enter_context(nc.sbuf_tensor(n, s, d))
        ident, iota = sb("tk_ident", [P, P]), sb("tk_iota", [P, P])
        QT, KEYS = sb("tk_QT", [P, 2, T]), sb("KEYS", [P, 2, NK])
        SC, SC2 = sb("SC", [P, 1, 5, 2, NK]), sb("SC2", [P, 5, 2, NK])
        V, I = sb("V", [P, 5, 2, TOPK]), sb("I", [P, 5, 2, TOPK], U32)
        IF = sb("IF", [P, 5, 2, TOPK])
        CA, CA2 = sb("CA", [P, 5, TOPK * TOPK]), sb("CA2", [P, 5, TOPK * TOPK])
        TOP = sb("TOP", [P, 5, TOPK])
        POS, PH2, PHF = sb("POS", [P, 5, TOPK], U32), sb("PH2", [P, 5, 2, TOPK], U32), sb("PHF", [P, 5, 2, TOPK])
        OUT = sb("OUT", [P, 3, 5, PH, TOPK])
        SUM = sb("SUM", [P, 5, PH])
        GEL = sb("tk_GEL", [P, 2, T])
        N = 2
        U0 = N * PH
        NCH = 8
        halves = lambda t: t.rearrange("p (h t) -> p h t", h=2)
        rows = lambda t: P if t < 4 else DEC
        LOW = -3.0e38
        block = ctx.enter_context(nc.Block())

        @block.sync
        def _(sp):
            sp.dma_start(KEYS[:, :, :], A["keys"]).then_inc(S["tk_cst"], 16)
            for t, n in ((ident, "ident"), (iota, "iota")):
                sp.dma_start(t[:, :], A["cst"][:, CST_AT[n][0]:CST_AT[n][0] + P]).then_inc(S["tk_cst"], 16)
            with sp.Fori(0, PH - 1) as i:
                for u in range(N):
                    W.load(sp, A["w_q"][bass.ds(N * i + u + 2, 1)].rearrange("a p n -> (a p) n"), u + 2, N, i)
            for u in range(2):
                W.load(sp, A["u"][u], U0 + u)

            def blocks(i, last):
                for u in range(2):
                    W.load(sp, ahead[u] if last else row(A["u"], N * i + u + 2), U0 + u + 2, N, i)
                for u in range(2):
                    sp.wait_ge(S["tk_q"], N * i + U0 + u + 3)
                    sp.dma_start(row(pre_d, N * i + u), GEL[:, u, :]).then_inc(S[f"tk_kept{u}"], 16)
            with sp.Fori(0, TAIL // 2 - 1) as i:
                blocks(i, False)
            blocks(TAIL // 2 - 1, True)
            for u in range(2):
                sp.wait_ge(S[f"tk_kept{u}"], 16 * (TAIL // 2) + 16)

        @block.gpsimd
        def _(pool):
            with pool.Fori(0, PH) as i:
                for u in range(N):
                    W.split_lo(pool, u + 2, N, i)
            with pool.Fori(0, TAIL // 2) as i:
                for u in range(N):
                    W.split_lo(pool, U0 + u + 2, N, i)

        @block.tensor
        def _(pe):
            pe.wait_ge(S["tk_cst"], 48)
            with pe.Fori(0, PH) as i:
                for u in range(N):
                    pe.wait_ge(S["tk_q"], N * i + u + 1)
                    for mm in unit_product(pe, W, u, acc[u], hh, hl, N, i):
                        pass
                    mm.then_inc(W.used, 1)
                for u, ps in enumerate((psS, psR)):
                    pe.wait_ge(S["tk_q"], N * i + u + 3)
                    pe.wait_ge(S["tk_scores"], N * i + u + 1)
                    for t in range(5):
                        n = rows(t)
                        mm = pe.matmul(ps[0:n, t // 4, (t % 4) * P:(t % 4 + 1) * P], QT[:, u, t * P:t * P + n],
                                       KEYS[:, u, :], start=t % 4 == 0, stop=True, skip_group_check=True)
                    mm.then_inc(S["tk_scored"], 1)
            with pe.Fori(0, TAIL // 2) as i:
                for u in range(N):
                    pe.wait_ge(S["tk_q"], N * i + U0 + u + 1)
                    for mm in unit_product(pe, W, U0 + u, acc[u], hh, hl, N, i):
                        pass
                    mm.then_inc(W.used, 1)
            pe.wait_ge(S["tk_gate"], 4)
            for t in range(5):
                n = rows(t)
                if t >= 2:
                    pe.wait_ge(S["tk_out"], t - 1)
                for a in range(3):
                    mm = pe.transpose((psS, psR)[t % 2][:, 0, a * P:a * P + n], OUT[0:n, a, t].rearrange("p h k -> p (h k)"), ident[0:n, 0:n])
                mm.then_inc(S["tk_turned"], 1)

        @block.scalar
        def _(act):
            act.sem_inc(S["tk_q"], 2)
            for u in range(2):
                act.sem_inc(S[f"tk_kept{u}"], 16)
            act.sem_inc(S["tk_scores"], 2)
            act.wait_ge(S["tk_set"], 3)

            with act.Fori(0, PH) as i:
                for u in range(N):
                    W.wait_used(act, u, N, i)
                    act.activation(halves(QT[:, u, :]), acc[u][:, :, 0:H2], ACT.Copy).then_inc(S["tk_q"], 1)
                    W.split_hi(act, u + 2, N, i)
                for u, ps in enumerate((psS, psR)):
                    act.wait_ge(S["tk_scored"], N * i + u + 1)
                    act.wait_ge(S["tk_head"], i + 1)
                    act.activation(SC[:, 0, 0:4, u, :], ps[:, 0, :].rearrange("p (t n) -> p t n", t=4), ACT.Copy)
                    act.activation(SC[0:DEC, 0, 4, u, :], ps[0:DEC, 1, 0:P], ACT.Copy).then_inc(S["tk_scores"], 1)

            def blocks(i):
                for u in range(2):
                    W.wait_used(act, U0 + u, N, i)
                    act.wait_ge(S[f"tk_kept{u}"], 16 * i + 16)
                    act.activation(halves(GEL[:, u, :]), acc[u][:, :, 0:H2], ACT.Gelu).then_inc(S["tk_q"], 1)
                    W.split_hi(act, U0 + u + 2, N, i)
            with act.Fori(0, TAIL // 2 - 1) as i:
                blocks(i)
            act.wait_ge(S["tk_gate"], 1)
            best = OUT[:, 2].rearrange("p t h k -> p (t h k)")
            act.activation(best, best, ACT.Exp).then_inc(S["tk_exp"], 1)
            blocks(TAIL // 2 - 1)
            for t in range(5):
                n = rows(t)
                act.wait_ge(S["tk_turned"], t + 1)
                act.activation(IT[:, :, t * P:t * P + n], (psS, psR)[t % 2][:, 0, 0:3 * P].rearrange("p (a n) -> p a n", a=3)[:, :, 0:n],
                               ACT.Copy).then_inc(S["tk_out"], 1)

        @block.vector
        def _(dve):
            dve.memset(SC[:, 0, 4], 0.0).then_inc(S["tk_set"], 1)
            dve.memset(V[:, 4], 0.0).then_inc(S["tk_set"], 1)
            dve.memset(I[:, 4], 0).then_inc(S["tk_set"], 1)
            dve.memset(POS[:, 4], 0).then_inc(S["tk_set"], 1)
            dve.memset(TOP[:, 4], 0.0).then_inc(S["tk_set"], 1)
            dve.sem_inc(S["tk_head"], 1)
            dve.wait_ge(S["tk_set"], 5)
            dve.wait_ge(S["tk_cst"], 48)

            with dve.Fori(0, PH) as i:
                dve.wait_ge(S["tk_scores"], N * i + 4)
                ch = Chain(dve, S["tk_chain"], 13, i)

                def best16(values, rest, top, index, where):
                    stage = [lambda w: dve.max(top(w, 0), values(w)),
                             lambda w: dve.match_replace(rest(w), top(w, 0), values(w), LOW),
                             lambda w: dve.max(top(w, 1), rest(w)),
                             lambda w: dve.max_index(index(w, 0), top(w, 0), values(w)),
                             lambda w: dve.max_index(index(w, 1), top(w, 1), rest(w))]
                    for n, f in enumerate(stage):
                        dve.sem_inc(S["waits_passed"], 1)
                        for w in where[:-1]:
                            f(w)
                        ch(f(where[-1]), wait=n != 3)
                where = [(t, u) for t in range(5) for u in range(2)]
                eight = lambda n: slice(8 * n, 8 * n + 8)
                best16(lambda w: SC[0:rows(w[0]), 0, w[0], w[1], :], lambda w: SC2[0:rows(w[0]), w[0], w[1], :],
                       lambda w, n: V[0:rows(w[0]), w[0], w[1], eight(n)], lambda w, n: I[0:rows(w[0]), w[0], w[1], eight(n)], where)
                dve.sem_inc(S["tk_head"], 1)
                ca = CA.rearrange("p t (a b) -> p t a b", a=TOPK)
                four = [P, 5, TOPK, TOPK]
                for t in range(5):
                    n = rows(t)
                    add = dve.tensor_tensor(ca[0:n, t], V[0:n, t, 0, :].unsqueeze(2).to_broadcast([n, TOPK, TOPK]),
                                            V[0:n, t, 1, :].unsqueeze(1).to_broadcast([n, TOPK, TOPK]), ALU.add)
                ch(add)
                best = lambda t, n: TOP[0:rows(t), t, eight(n)]
                best16(lambda t: CA[0:rows(t), t, :], lambda t: CA2[0:rows(t), t, :], best,
                       lambda t, n: POS[0:rows(t), t, eight(n)], list(range(5)))
                dve.tensor_scalar(PH2[:, :, 0, :], POS[:, :, :], 4, None, ALU.logical_shift_right)
                dve.tensor_scalar(PH2[:, :, 1, :], POS[:, :, :], 15, None, ALU.bitwise_and)
                dve.tensor_copy(OUT[:, 2, :, bass.ds(i, 1), :].rearrange("p t a k -> p t (a k)"), TOP[:, :, :])
                ch(dve.tensor_copy(IF[:, :, :, :], I[:, :, :, :]))
                ch(dve.tensor_copy(PHF[:, :, :, :], PH2[:, :, :, :]))
                row = iota[:, 0:TOPK].unsqueeze(1).to_broadcast([P, TOPK, TOPK])
                for u, o in ((0, CA), (1, CA2)):
                    for t in range(5):
                        o3 = o[:, t, :].rearrange("p (k a) -> p k a", a=TOPK)
                        eq = dve.tensor_tensor(o3, PHF[:, t, u, :].unsqueeze(2).to_broadcast([P, TOPK, TOPK]), row, ALU.is_equal)
                eq.then_inc(S["tk_eq"], 1)
                dve.wait_ge(S["tk_eq"], 3 * i + 1)
                for u, o in ((0, CA), (1, CA2)):
                    for t in range(5):
                        o3 = o[:, t, :].rearrange("p (k a) -> p k a", a=TOPK)
                        pick = dve.tensor_tensor(o3, o3, IF[:, t, u, :].unsqueeze(1).to_broadcast([P, TOPK, TOPK]), ALU.mult)
                pick.then_inc(S["tk_eq"], 1)
                dve.wait_ge(S["tk_eq"], 3 * i + 2)
                for u, o in ((0, CA), (1, CA2)):
                    got = dve.tensor_reduce(OUT[:, u, :, bass.ds(i, 1), :].rearrange("p t a k -> p t (a k)"),
                                            o.rearrange("p t (k a) -> p t k a", a=TOPK), AX_X, ALU.add)
                got.then_inc(S["tk_eq"], 1)
                dve.wait_ge(S["tk_eq"], 3 * i + 3)
                ch.end()
            g = OUT[:, 2].rearrange("p t h k -> p (t h) k")
            flat = [P, 5 * PH, TOPK]
            total = SUM.rearrange("p t h -> p (t h)")
            dve.tensor_copy(total, g[:, :, 0]).then_inc(S["tk_top"], 1)
            dve.wait_ge(S["tk_top"], 1)
            dve.tensor_tensor(g, g, total.unsqueeze(2).to_broadcast(flat), ALU.subtract).then_inc(S["tk_gate"], 1)
            dve.wait_ge(S["tk_exp"], 1)
            dve.tensor_reduce(total, g, AX_X, ALU.add).then_inc(S["tk_gate"], 1)
            dve.wait_ge(S["tk_gate"], 2)
            dve.reciprocal(total, total).then_inc(S["tk_gate"], 1)
            dve.wait_ge(S["tk_gate"], 3)
            dve.tensor_tensor(g, g, total.unsqueeze(2).to_broadcast(flat), ALU.mult).then_inc(S["tk_gate"], 1)


GB_T = 68
GB_N = T // GB_T
TAIL = 8
PRE = TAIL + 2 * GB_N


def gate_matrix(nc, S, A, W, ahead, acc, psS, psR, hh, hl, IT, g_d, pre_d):
    with ExitStack() as ctx:
        sb = lambda n, s, d=F32: ctx.enter_context(nc.sbuf_tensor(n, s, d))
        iota = sb("gm_iota", [P, P])
        ONE = sb("ONE", [P, 3, 4, 2, P])
        STG = sb("STG", [P, 2, NK, GB_T])
        GEL = sb("GEL", [P, 2, T])
        QUADS, N = GB_T // 4, 4
        ITER = GB_N // 2
        MIDDLE = QUADS // 2
        bank = lambda q: (psS, psR)[q % 4 // 2][:, q % 2, :]

        def turn(q, n):
            return q + 1 if q >= n else max(x for x in range(QUADS) if x % n == q) + 1 - QUADS + n

        block = ctx.enter_context(nc.Block())

        @block.sync
        def _(sp):
            sp.dma_start(iota[:, :], A["cst"][:, CST_AT["iota"][0]:CST_AT["iota"][0] + P]).then_inc(S["gm_cst"], 16)

            def token_block(i, par, last):
                for u in range(2):
                    c = 2 * par + u
                    W.load(sp, ahead[u] if last else row(A["u"], N * i + c + 2 + TAIL), c + 2, N, i)
                for u in range(2):
                    c = 2 * par + u
                    sp.wait_ge(S["gm_gelu"], N * i + c + 3)
                    sp.dma_start(row(pre_d, N * i + c + TAIL), GEL[:, u, :]).then_inc(S[f"gm_kept{u}"], 16)
                sp.wait_ge(S["gm_evac"], QUADS * (2 * i + par + 1) + 4)
                sp.dma_start(g_d[bass.ds(2 * i + par, 1)].rearrange("a p n t -> (a p) (n t)"),
                             STG[:, par].rearrange("p n t -> p (n t)")).then_inc(S[f"gm_stored{par}"], 16)
            with sp.Fori(0, ITER - 1) as i:
                token_block(i, 0, False)
                token_block(i, 1, False)
            token_block(ITER - 1, 0, False)
            token_block(ITER - 1, 1, True)
            for n in range(2):
                sp.wait_ge(S[f"gm_stored{n}"], 16 * ITER + 16)
                sp.wait_ge(S[f"gm_kept{n}"], 16 * GB_N + 16)

        @block.gpsimd
        def _(pool):
            with pool.Fori(0, ITER) as i:
                for c in range(N):
                    W.split_lo(pool, c + 2, N, i)

        @block.vector
        def _(dve):
            dve.wait_ge(S["gm_cst"], 16)
            with dve.Fori(0, GB_N) as i:
                for q in range(QUADS):
                    dve.wait_ge(S["gm_summed"], QUADS * i + turn(q, 3))
                    for j in range(4):
                        tok = bass.ds(GB_T * i + 4 * q + j, 1)
                        dve.tensor_scalar(ONE[:, q % 3, j, 0, :], iota[:, :], IT[:, 0, tok], IT[:, 2, tok], ALU.is_equal, ALU.mult)
                        one = dve.tensor_scalar(ONE[:, q % 3, j, 1, :], iota[:, :], IT[:, 1, tok], None, ALU.is_equal)
                    one.then_inc(S["gm_onehot"], 1)

        @block.tensor
        def _(pe):
            pe.sem_inc(S["gm_summed"], 3)
            with pe.Fori(0, ITER) as i:
                def units():
                    for c in range(N):
                        pe.wait_ge(S["gm_gelu"], N * i + c + 1)
                        for n, mm in enumerate(unit_product(pe, W, c, acc[c % 2], hh, hl, N, i)):
                            if n == KB - 1:
                                mm.then_inc(W.used, 1)
                            yield
                background = units()
                for par in range(2):
                    for q in range(QUADS):
                        pe.wait_ge(S["gm_onehot"], QUADS * (2 * i + par) + q + 1)
                        pe.wait_ge(S["gm_evac"], QUADS * (2 * i + par) + turn(q, 4))
                        for j in range(4):
                            mm = pe.matmul(bank(q)[:, j * P:(j + 1) * P], ONE[:, q % 3, j, 1, :], ONE[:, q % 3, j, 0, :], start=True, stop=True)
                        mm.then_inc(S["gm_summed"], 1)
                        if q > 0:
                            next(background)
                            next(background)
                next(background, None)

        @block.scalar
        def _(act):
            for n in range(2):
                act.sem_inc(S[f"gm_stored{n}"], 16)
                act.sem_inc(S[f"gm_kept{n}"], 16)
            act.sem_inc(S["gm_evac"], 4)
            act.sem_inc(S["gm_gelu"], 2)

            def token_block(i, par):
                def unit_done(u):
                    c = 2 * par + u
                    W.wait_used(act, c, N, i)
                    act.wait_ge(S[f"gm_kept{u}"], 16 * (2 * i + par) + 16)
                    act.activation(GEL[:, u, :].rearrange("p (h t) -> p h t", h=2), acc[c % 2][:, :, 0:H2],
                                   ACT.Gelu).then_inc(S["gm_gelu"], 1)
                    W.split_hi(act, c + 2, N, i)
                act.wait_ge(S[f"gm_stored{par}"], 16 * i + 16)
                for q in range(QUADS):
                    act.wait_ge(S["gm_summed"], QUADS * (2 * i + par) + q + 4)
                    act.activation(STG[:, par, :, 4 * q:4 * q + 4], bank(q).rearrange("p (t n) -> p n t", t=4),
                                   ACT.Copy).then_inc(S["gm_evac"], 1)
                    if q == MIDDLE:
                        unit_done(0)
                unit_done(1)
            with act.Fori(0, ITER) as i:
                token_block(i, 0)
                token_block(i, 1)


def experts(nc, S, A, W, acc, psS, psR, H, load_h, hh, hl, g_d, pre_d):
    with ExitStack() as ctx:
        sb = lambda n, s, d=F32: ctx.enter_context(nc.sbuf_tensor(n, s, d))
        G = sb("Ge", [P, 2, GB_N, 2, GB_T])
        GE, CX = sb("GE", [P, 2, T]), sb("CX", [P, 2, T])
        chi, clo = sb("chi", [P, 2, 2, T], F32R), sb("clo", [P, 2, 2, T], F32R)
        GROUPS = NK // 2
        N = 8
        U = lambda k: A["u"][k]
        v_units = v_rows(A)
        halves = lambda t: t.rearrange("p (h t) -> p h t", h=2)
        vps = [psS, psR, *acc]
        block = ctx.enter_context(nc.Block())
        FIRST = PRE // 2
        ITER = (GROUPS - FIRST) // 2 - 1
        C0 = 2 * FIRST

        @block.sync
        def _(sp):
            def u_unit(c, i, k):
                src = A["u"][bass.ds(k, 1)].rearrange("a p n -> (a p) n") if not isinstance(k, int) else A["u"][k]
                W.load(sp, src, c, N, i)

            def v_unit(c, i, group, half, per=N):
                src = v_units[group, half] if isinstance(group, int) else v_units[bass.ds(group, 1), half].rearrange("g p k n -> (g p) k n")
                W.load(sp, src, c, per, i)

            def gates(group, slot, count):
                sp.wait_ge(S["ex_coef"], count)
                src = g_d.rearrange("b p n t -> p b n t")
                if isinstance(group, int):
                    a = src[:, :, 2 * group:2 * group + 2, :]
                else:
                    a = src[:, :, bass.ds(2 * group, 2), :]
                sp.dma_start(G[:, slot].rearrange("p b n t -> p b (n t)"), a.rearrange("p b n t -> p b (n t)")).then_inc(S[f"ex_gates{slot}"], 16)

            def kept(group):
                for k in range(2):
                    sp.wait_ge(S["ex_coef"], 2 * group + k + 1)
                    src = pre_d[2 * group + k] if isinstance(group, int) else pre_d[bass.ds(2 * group + k, 1)].rearrange("a p t -> (a p) t")
                    sp.dma_start(GE[:, k, :], src).then_inc(S[f"ex_kept{k}"], 16)

            kept(0)
            gates(0, 0, 1)
            def first_groups(i, last=False):
                kept(2 * i + 1)
                gates(2 * i + 1, 1, 4 * i + 2)
                v_unit(2, i, 2 * i + 1, 0, 4)
                v_unit(3, i, 2 * i + 1, 1, 4)
                if not last:
                    kept(2 * i + 2)
                    gates(2 * i + 2, 0, 4 * i + 4)
                    v_unit(4, i, 2 * i + 2, 0, 4)
                    v_unit(5, i, 2 * i + 2, 1, 4)
            with sp.Fori(0, FIRST // 2 - 1) as i:
                first_groups(i)
            first_groups(FIRST // 2 - 1, True)
            gates(FIRST, 0, 2 * FIRST)
            W.load(sp, A["u"][PRE], C0)
            W.load(sp, A["u"][PRE + 1], C0 + 1)

            def groups(i, part=2):
                g = FIRST + 2 * i
                gates(g + 1, 1, 2 * g + 2)
                u_unit(C0 + 2, i, 2 * g + 2)
                u_unit(C0 + 3, i, 2 * g + 3)
                v_unit(C0 + 4, i, g, 0)
                v_unit(C0 + 5, i, g, 1)
                if part == 2:
                    gates(g + 2, 0, 2 * g + 4)
                    u_unit(C0 + 6, i, 2 * g + 4)
                    u_unit(C0 + 7, i, 2 * g + 5)
                c = C0 + (8 if part == 2 else 6)
                v_unit(c, i, g + 1, 0)
                v_unit(c + 1, i, g + 1, 1)
            with sp.Fori(0, ITER) as i:
                groups(i)
            groups(ITER, 1)

        @block.gpsimd
        def _(pool):
            with pool.Fori(0, FIRST // 2) as i:
                for c in range(2, 6):
                    W.split_lo(pool, c, 4, i)
            with pool.Fori(0, ITER) as i:
                for c in range(2, 2 + N):
                    W.split_lo(pool, C0 + c, N, i)
            for c in range(2, 8):
                W.split_lo(pool, C0 + c, N, ITER)

        @block.tensor
        def _(pe):

            def u_products(c, i, count):
                pe.wait_ge(S["ex_gelu"], count + 1)
                for mm in unit_product(pe, W, c, acc[c % 2], hh, hl, N, i):
                    pass
                mm.then_inc(W.used, 1)

            def v_products(c, i, par, half, group, per=N):
                W.ready(pe, c, per, i)
                if half == 0:
                    pe.wait_ge(S["ex_coef"], 2 * group + 4)
                for d in range(8):
                    n = 16 * group + 8 * half + d
                    pe.wait_ge(S["ex_added"], n + (3 if per == N else 1))
                    w = lambda t: lambda k: t[:, c % 2, k * 1024 + d * P:k * 1024 + (d + 1) * P]
                    x = lambda t: lambda k, h: t[:, par, k, h * H2:(h + 1) * H2]
                    for mm in product(pe, vps[d % (2 if per == N else 4)], w(W.hi), w(W.lo), x(chi), x(clo), 2):
                        pass
                    if d < 7:
                        mm.then_inc(S["ex_v"], 1)
                mm.then_inc(W.used, 1)

            with pe.Fori(0, FIRST // 2) as i:
                for c in range(4):
                    v_products(c, i, c // 2, c % 2, 2 * i + c // 2, 4)
            pe.wait_ge(S["ex_added"], 16 * FIRST + 4)
            u_products(C0, 0, PRE)
            u_products(C0 + 1, 0, PRE + 1)

            def groups(i, part=2):
                g = FIRST + 2 * i
                u_products(C0 + 2, i, 2 * g + 2)
                u_products(C0 + 3, i, 2 * g + 3)
                v_products(C0 + 4, i, 0, 0, g)
                v_products(C0 + 5, i, 0, 1, g)
                if part == 2:
                    u_products(C0 + 6, i, 2 * g + 4)
                    u_products(C0 + 7, i, 2 * g + 5)
                c = C0 + (8 if part == 2 else 6)
                v_products(c, i, 1, 0, g + 1)
                v_products(c + 1, i, 1, 1, g + 1)
            with pe.Fori(0, ITER) as i:
                groups(i)
            groups(ITER, 1)

        @block.scalar
        def _(act):
            act.wait_ge(S["ex_gates0"], 16)
            for q in range(4):
                act.dma_start(H[:, 4 * q:4 * q + 4, :], load_h(4 * q, 4 * q + 4)).then_inc(S[f"ex_h{q}"], 16)
            act.sem_inc(S["ex_gelu"], PRE + 2)

            def gelu(c, i, count):
                W.wait_used(act, c, N, i)
                act.wait_ge(S["ex_coef"], count + 1)
                act.activation(halves(GE[:, c % 2, :]), acc[c % 2][:, :, 0:H2], ACT.Gelu).then_inc(S["ex_gelu"], 1)

            with act.Fori(0, FIRST // 2) as i:
                for c in range(2, 6):
                    W.split_hi(act, c, 4, i)
            gelu(C0, 0, PRE)
            W.split_hi(act, C0 + 2)
            gelu(C0 + 1, 0, PRE + 1)

            def groups(i, part=2):
                g = FIRST + 2 * i
                W.split_hi(act, C0 + 3, N, i)
                gelu(C0 + 2, i, 2 * g + 2)
                W.split_hi(act, C0 + 4, N, i)
                gelu(C0 + 3, i, 2 * g + 3)
                W.split_hi(act, C0 + 5, N, i)
                W.split_hi(act, C0 + 6, N, i)
                W.split_hi(act, C0 + 7, N, i)
                if part == 2:
                    gelu(C0 + 6, i, 2 * g + 4)
                    W.split_hi(act, C0 + 8, N, i)
                    gelu(C0 + 7, i, 2 * g + 5)
                    W.split_hi(act, C0 + 9, N, i)
                    W.split_hi(act, C0 + 10, N, i)
            with act.Fori(0, ITER) as i:
                groups(i)
            groups(ITER, 1)

        @block.vector
        def _(dve):
            dve.sem_inc(S["ex_coef"], 2)
            dve.sem_inc(S["ex_added"], 4)

            def coefficients(par, k, slot, count):
                dve.wait_ge(S["ex_gelu"], count + 3)
                tok = lambda t: t.rearrange("p (b t) -> p b t", b=GB_N)
                dve.tensor_tensor(tok(CX[:, k, :]), tok(GE[:, k, :]), G[:, slot, :, k, :], ALU.mult).then_inc(S["ex_prod"], 1)
                dve.wait_ge(S["ex_prod"], 2 * count + 1)
                dve.tensor_copy(chi[:, par, k, :], CX[:, k, :]).then_inc(S["ex_prod"], 1)
                dve.wait_ge(S["ex_prod"], 2 * count + 2)
                dve.tensor_tensor(clo[:, par, k, :], CX[:, k, :], chi[:, par, k, :].bitcast(F32), ALU.subtract).then_inc(S["ex_coef"], 1)

            def add(half, c, i, group, per=N):
                for d in range(8):
                    if per != N and d % 4 == 0:
                        dve.wait_ge(S[f"ex_h{2 * half + d // 4}"], 16)
                    n = 14 * group + 7 * half + d + 1
                    if d < 7:
                        dve.wait_ge(S["ex_v"], n)
                    else:
                        W.wait_used(dve, c, per, i)
                    h = halves(H[:, 8 * half + d, :])
                    dve.tensor_tensor(h, vps[d % (2 if per == N else 4)][:, :, 0:H2], h, ALU.add).then_inc(S["ex_added"], 1)

            def first(group, par, turn):
                dve.wait_ge(S[f"ex_gates{par}"], 16 * turn + 16)
                for k in range(2):
                    dve.wait_ge(S[f"ex_kept{k}"], 16 * group + 16)
                    coefficients(par, k, par, 2 * group + k)

            first(0, 0, 0)

            def first_groups(i, last=False):
                first(2 * i + 1, 1, i)
                add(0, 0, i, 2 * i, 4)
                add(1, 1, i, 2 * i, 4)
                if not last:
                    first(2 * i + 2, 0, i + 1)
                add(0, 2, i, 2 * i + 1, 4)
                add(1, 3, i, 2 * i + 1, 4)
            with dve.Fori(0, FIRST // 2 - 1) as i:
                first_groups(i)
            first_groups(FIRST // 2 - 1, True)
            dve.wait_ge(S["ex_gates0"], 8 * FIRST + 16)
            coefficients(0, 0, 0, PRE)
            coefficients(0, 1, 0, PRE + 1)

            def groups(i, part=2):
                g = FIRST + 2 * i
                dve.wait_ge(S["ex_gates1"], 8 * g + 16)
                coefficients(1, 0, 1, 2 * g + 2)
                coefficients(1, 1, 1, 2 * g + 3)
                add(0, C0 + 4, i, g)
                add(1, C0 + 5, i, g)
                if part == 2:
                    dve.wait_ge(S["ex_gates0"], 8 * g + 32)
                    coefficients(0, 0, 0, 2 * g + 4)
                    coefficients(0, 1, 0, 2 * g + 5)
                c = C0 + (8 if part == 2 else 6)
                add(0, c, i, g + 1)
                add(1, c + 1, i, g + 1)
            with dve.Fori(0, ITER) as i:
                groups(i)
            groups(ITER, 1)


def layout(x):
    c = np.ascontiguousarray
    f = lambda a: np.asarray(a)
    def blocks(w):
        k, n = w.shape
        return c(w.reshape(k // P, P, n // P, P).transpose(2, 1, 0, 3).reshape(n // P, P, k))
    def cols(v):
        return v.reshape(-1, P).T
    A = {}
    xall = np.concatenate([f(x["x_prompt"])[0], f(x["x_sample"])[0]], axis=0)
    A["xT"] = c(xall.T.reshape(KB, P, T).transpose(1, 0, 2))
    A["w_in"] = blocks(f(x["w_in"])[0])
    A["ckT"] = c(f(x["cache_sb_k"])[0, 0].transpose(1, 2, 0))
    A["cv"] = c(f(x["cache_sb_v"])[0, 0].reshape(4, P, HEADS, P).transpose(2, 1, 0, 3))
    w2a2 = np.concatenate([f(x["rw_w2"])[0], f(x["rw_a2"])[0]], axis=0)
    A["lora"] = c(np.stack([w2a2, f(x["rw_g2"])[0]], axis=1).reshape(P, 2, PAIRS, P).transpose(2, 0, 1, 3))
    A["s0T"] = c(f(x["state_rwkv_wkv"])[0, 0].transpose(0, 2, 1).reshape(PAIRS, P, CH))
    mu = f(x["rw_mu"])[0]
    per = {"mu_r": mu[0:RW], "mu_k": mu[RW:2 * RW], "mu_v": mu[2 * RW:3 * RW], "w0": x["rw_w0"][0],
           "a0": x["rw_a0"][0], "k_k": x["rw_k_k"][0], "k_a": x["rw_k_a"][0],
           "r_k": f(x["rw_r_k"])[0].reshape(-1), "ln_g": x["rw_ln_g"][0], "ln_b": x["rw_ln_b"][0]}
    pairs = np.stack([cols(f(per[n])) for n in PAR], axis=2).reshape(P, PAIRS * NPAR)
    A["par"] = c(np.concatenate([pairs, cols(mu[3 * RW:]), cols(f(x["norm1_g"])[0]), cols(f(x["norm2_g"])[0]),
                                 cols(f(x["final_norm_g"])), cols(f(x["state_rwkv_shift"])[0, 0, 0])], axis=1))
    sbw, rww = blocks(f(x["w_branch_sb"])[0]), blocks(f(x["w_branch_rw"])[0])
    A["w_br"] = c(np.concatenate([sbw, rww], axis=2))
    A["w_out"] = blocks(f(x["w_out"])[0])
    A["w_q"] = blocks(f(x["peer_wq"])[0])
    A["keys"] = c(np.stack([f(x["peer_k1"])[0].T, f(x["peer_k2"])[0].T], axis=1))
    A["u"] = blocks(f(x["peer_u"])[0].T)
    A["v"] = c(f(x["peer_v"])[0])
    A["cst"] = c(np.concatenate([*constants().values()], axis=1))
    return A


OUTS = {"kT": (HEADS, P, T), "vT": (HEADS, P, T), "wkvp": (PAIRS, P, CH), "wkvs": (PAIRS, P, CH), "shift": (P, 26, 2), "yT": (P, KB, T)}


def kernel(**inputs):
    import concourse.bacc as _bacc
    from concourse.bass_utils import run_bass_kernel_spmd as _run

    arrays = layout({k: np.asarray(v) for k, v in inputs.items()})
    nc = _bacc.Bacc("TRN2", target_bir_lowering=False, num_devices=1)
    A = {n: nc.dram_tensor("in_" + n, a.shape, F32, kind="ExternalInput").ap() for n, a in arrays.items()}
    O = {n: nc.dram_tensor("out_" + n, s, F32, kind="ExternalOutput").ap() for n, s in OUTS.items()}
    build(nc, A, O)
    r = _run(nc, [{"in_" + n: a for n, a in arrays.items()}], core_ids=[0]).results[0]
    y = r["out_yT"].transpose(2, 1, 0).reshape(T, D)
    k, v = (r[n].transpose(2, 0, 1) for n in ("out_kT", "out_vT"))
    wkv = [r[n].reshape(PAIRS * 2, CH, CH).transpose(0, 2, 1)[None, None] for n in ("out_wkvp", "out_wkvs")]
    shift = [r["out_shift"][:, :, n].T.reshape(1, 1, 1, -1) for n in range(2)]
    c = np.ascontiguousarray
    return (c(y[None, :SEQ]), c(y[None, SEQ:]), c(k[None, None, :SEQ]), c(v[None, None, :SEQ]), c(wkv[0]), c(shift[0]),
            c(k[None, None, SEQ:]), c(v[None, None, SEQ:]), c(wkv[1]), c(shift[1]))
```
